# Optimizing a Trainium2 kernel written in Bass

```python
import math
import jax, jax.numpy as jnp
from jax import lax
import numpy as np

D_MODEL = 1024
BATCH = 1
SEQ = 512
DEPTH = 2

GRID_W = 64
CTX_LEN = 256
N_MIXERS = 2
N_MOD = 6
NORM_EPS = 1e-6
MLA_HEADS = 8
Q_LORA = 384
KV_LORA = 256
NOPE_DIM = 128
ROPE_DIM = 64
V_DIM = 128
ROPE_BASE = 10000.0
Q_BLOCK = 128
S5_GROUP = 16
S5_GROUPS = D_MODEL // S5_GROUP
S5_STATE = 64
S5_DT_MIN = 1e-3
S5_DT_MAX = 1e-1
N_EXPERTS = 64
TOP_K = 8
N_EXPERT_GROUPS = 8
TOPK_GROUPS = 4
D_EXPERT = 256
D_SHARED = 256
ROUTED_SCALE = 2.5
MOE_BLOCK = 128

kernel_name = "hybrid_mla_s5_moe_diffusion_trunk"

def rms_norm(x, g):
    xf = x.astype(jnp.float32)
    y = xf * lax.rsqrt(jnp.mean(xf * xf, axis=-1, keepdims=True) + NORM_EPS)
    return (y * g.astype(jnp.float32)).astype(x.dtype)

def modulate(h, shift, scale):
    return h * (1 + scale) + shift

def axial_rope_tables(n_tokens):
    rows = n_tokens // GRID_W
    row = jnp.repeat(jnp.arange(rows), GRID_W).astype(jnp.float32)
    col = jnp.tile(jnp.arange(GRID_W), rows).astype(jnp.float32)
    n_freq = ROPE_DIM // 4
    inv_freq = ROPE_BASE ** (-jnp.arange(n_freq, dtype=jnp.float32) / n_freq)
    ang = jnp.concatenate([row[:, None] * inv_freq, col[:, None] * inv_freq], axis=-1)
    return jnp.cos(ang), jnp.sin(ang)

def apply_rope(x, cos, sin):
    xf = x.astype(jnp.float32).reshape(*x.shape[:-1], ROPE_DIM // 2, 2)
    x0, x1 = xf[..., 0], xf[..., 1]
    out = jnp.stack([x0 * cos - x1 * sin, x0 * sin + x1 * cos], axis=-1)
    return out.reshape(x.shape).astype(x.dtype)

def mla_attend(q_nope, q_pe, k_nope, k_pe, v):
    scale = (NOPE_DIM + ROPE_DIM) ** -0.5
    s = (jnp.einsum('bqhd,bkhd->bhqk', q_nope, k_nope, preferred_element_type=jnp.float32)
         + jnp.einsum('bqhr,bkr->bhqk', q_pe, k_pe, preferred_element_type=jnp.float32)) * scale
    p = jax.nn.softmax(s, axis=-1).astype(v.dtype)
    return jnp.einsum('bhqk,bkhv->bqhv', p, v)

def blocked_attend(q_nope, q_pe, k_nope, k_pe, v):
    B, L, H, _ = q_nope.shape
    nb = L // Q_BLOCK

    def to_blocks(t):
        return jnp.moveaxis(t.reshape(B, nb, Q_BLOCK, *t.shape[2:]), 1, 0)

    out = lax.map(lambda qs: mla_attend(qs[0], qs[1], k_nope, k_pe, v),
                  (to_blocks(q_nope), to_blocks(q_pe)))
    return jnp.moveaxis(out, 0, 1).reshape(B, L, H, V_DIM)

def mla_mixer(h_ctx, h_lat, cos, sin, w_dqkv, g_q, g_kv, w_uq, w_ukv, w_o, need_ctx):
    B, L, _ = h_lat.shape
    n_ctx = h_ctx.shape[1]
    n_all = n_ctx + L
    h = jnp.concatenate([h_ctx, h_lat], axis=1)
    a = h @ w_dqkv
    c_q, c_kv, k_pe = jnp.split(a, [Q_LORA, Q_LORA + KV_LORA], axis=-1)
    q = (rms_norm(c_q, g_q) @ w_uq).reshape(B, n_all, MLA_HEADS, NOPE_DIM + ROPE_DIM)
    kv = (rms_norm(c_kv, g_kv) @ w_ukv).reshape(B, n_all, MLA_HEADS, NOPE_DIM + V_DIM)
    q_nope, q_pe = jnp.split(q, [NOPE_DIM], axis=-1)
    k_nope, v = jnp.split(kv, [NOPE_DIM], axis=-1)
    q_pe = apply_rope(q_pe, cos[:, None, :], sin[:, None, :])
    k_pe = apply_rope(k_pe, cos, sin)
    o_lat = blocked_attend(q_nope[:, n_ctx:], q_pe[:, n_ctx:], k_nope, k_pe, v)
    o_lat = o_lat.reshape(B, L, MLA_HEADS * V_DIM) @ w_o
    if not need_ctx:
        return o_lat, None
    o_ctx = mla_attend(q_nope[:, :n_ctx], q_pe[:, :n_ctx], k_nope[:, :n_ctx], k_pe[:, :n_ctx], v[:, :n_ctx])
    o_ctx = o_ctx.reshape(B, n_ctx, MLA_HEADS * V_DIM) @ w_o
    return o_lat, o_ctx

def _ssm_combine(e1, e2):
    a1, b1 = e1
    a2, b2 = e2
    return a1 * a2, a2 * b1 + b2

def diag_scan(bu, lam_bar, reverse):
    a = jnp.broadcast_to(lam_bar, (1, bu.shape[1]) + lam_bar.shape)
    return lax.associative_scan(_ssm_combine, (a, bu), axis=1, reverse=reverse)[1]

def s5_glu(y, w_glu, b_glu):
    z = jax.nn.gelu(y).astype(w_glu.dtype) @ w_glu + b_glu
    z1, z2 = jnp.split(z, 2, axis=-1)
    return z1 * jax.nn.sigmoid(z2)

def s5_mixer(h_ctx, h_lat, lam_re, lam_im, log_step, b_re, b_im, c_re, c_im, d_skip, w_glu, b_glu, need_ctx):
    B, L, D = h_lat.shape
    n_ctx = h_ctx.shape[1]
    f32 = jnp.float32
    u_ctx = h_ctx.astype(f32).reshape(B, n_ctx, S5_GROUPS, S5_GROUP).astype(jnp.complex64)
    u_lat = h_lat.astype(f32).reshape(B, L, S5_GROUPS, S5_GROUP).astype(jnp.complex64)
    dsk = d_skip.astype(f32)
    y_lat = h_lat.astype(f32) * dsk
    y_ctx = h_ctx.astype(f32) * dsk if need_ctx else None
    for direction in range(2):
        reverse = direction == 1
        lam = lax.complex(lam_re[direction].astype(f32), lam_im[direction].astype(f32))
        step = jnp.exp(log_step[direction].astype(f32))[:, None]
        lam_bar = jnp.exp(lam * step)
        b_bar = ((lam_bar - 1.0) / lam)[:, :, None] * lax.complex(
            b_re[direction].astype(f32), b_im[direction].astype(f32))
        c_mat = lax.complex(c_re[direction].astype(f32), c_im[direction].astype(f32))
        s_ctx = diag_scan(jnp.einsum('blgi,gpi->blgp', u_ctx, b_bar), lam_bar, reverse)
        h0 = s_ctx[:, 0] if reverse else s_ctx[:, -1]
        bu_lat = jnp.einsum('blgi,gpi->blgp', u_lat, b_bar)
        bu_lat = bu_lat.at[:, -1 if reverse else 0].add(lam_bar * h0)
        s_lat = diag_scan(bu_lat, lam_bar, reverse)
        y_lat = y_lat + jnp.einsum('blgp,gip->blgi', s_lat, c_mat).real.reshape(B, L, D)
        if need_ctx:
            y_ctx = y_ctx + jnp.einsum('blgp,gip->blgi', s_ctx, c_mat).real.reshape(B, n_ctx, D)
    o_lat = s5_glu(y_lat, w_glu, b_glu).astype(h_lat.dtype)
    o_ctx = s5_glu(y_ctx, w_glu, b_glu).astype(h_ctx.dtype) if need_ctx else None
    return o_lat, o_ctx

def swiglu(x, w_gate, w_up, w_down):
    return (jax.nn.silu(x @ w_gate) * (x @ w_up)) @ w_down

def moe_ffn(tok, w_router, router_bias, w_gate, w_up, w_down, sh_gate, sh_up, sh_down):
    T, D = tok.shape
    scores = jax.nn.sigmoid(tok.astype(jnp.float32) @ w_router.astype(jnp.float32))
    biased = scores + router_bias.astype(jnp.float32)
    grp = biased.reshape(T, N_EXPERT_GROUPS, N_EXPERTS // N_EXPERT_GROUPS)
    grp_score = lax.top_k(grp, 2)[0].sum(-1)
    _, gidx = lax.top_k(grp_score, TOPK_GROUPS)
    gmask = jax.nn.one_hot(gidx, N_EXPERT_GROUPS, dtype=jnp.bool_).any(axis=1)
    emask = jnp.repeat(gmask, N_EXPERTS // N_EXPERT_GROUPS, axis=1)
    _, eidx = lax.top_k(jnp.where(emask, biased, -jnp.inf), TOP_K)
    gates = jnp.take_along_axis(scores, eidx, axis=1)
    gates = gates / jnp.sum(gates, axis=-1, keepdims=True) * ROUTED_SCALE

    A = T * TOP_K
    flat_e = eidx.reshape(-1)
    flat_tok = jnp.repeat(jnp.arange(T), TOP_K)
    flat_w = gates.reshape(-1)
    order = jnp.argsort(flat_e)
    se, stok, sw = flat_e[order], flat_tok[order], flat_w[order]
    counts = jnp.bincount(flat_e, length=N_EXPERTS)
    padded = (counts + MOE_BLOCK - 1) // MOE_BLOCK * MOE_BLOCK
    pad_end = jnp.cumsum(padded)
    pad_start = pad_end - padded
    start = jnp.cumsum(counts) - counts
    dest = pad_start[se] + (jnp.arange(A) - start[se])
    n_blocks = -(-A // MOE_BLOCK) + N_EXPERTS
    buf = jnp.zeros((n_blocks * MOE_BLOCK, D), tok.dtype).at[dest].set(tok[stok])
    blk_e = jnp.minimum(jnp.searchsorted(pad_end, jnp.arange(n_blocks) * MOE_BLOCK, side='right'),
                        N_EXPERTS - 1)

    def expert_block(args):
        xb, e = args
        return swiglu(xb, w_gate[e], w_up[e], w_down[e])

    out = lax.map(expert_block, (buf.reshape(n_blocks, MOE_BLOCK, D), blk_e)).reshape(-1, D)
    y = out[dest] * sw[:, None].astype(out.dtype)
    routed = jax.ops.segment_sum(y, stok, num_segments=T)
    return routed + swiglu(tok, sh_gate, sh_up, sh_down)

def setup_inputs(seed: int = 0) -> dict:
    key = jax.random.key(seed)
    ks = iter(jax.random.split(key, 48))
    f32 = jnp.float32

    def nrm(shape, scale):
        return jax.random.normal(next(ks), shape, f32) * scale

    n_a = (DEPTH + N_MIXERS - 1) // N_MIXERS
    n_b = DEPTH // N_MIXERS
    D = D_MODEL
    G, P, I = S5_GROUPS, S5_STATE, S5_GROUP
    lam_im0 = jnp.broadcast_to(jnp.pi * jnp.arange(P, dtype=f32), (n_b, 2, G, P))
    return {
        "x": nrm((BATCH, SEQ, D), 1.0),
        "c": nrm((BATCH, D), 1.0),
        "ctx": nrm((BATCH, CTX_LEN, D), 1.0),
        "c_ctx": nrm((D,), 1.0),
        "ada_w": nrm((DEPTH, D, N_MOD * D), 0.5 * D ** -0.5),
        "ada_b": nrm((DEPTH, N_MOD * D), 0.02),
        "norm_g": 1.0 + nrm((DEPTH, 4, D), 0.02),
        "mla_w_dqkv": nrm((n_a, D, Q_LORA + KV_LORA + ROPE_DIM), D ** -0.5),
        "mla_g_q": 1.0 + nrm((n_a, Q_LORA), 0.02),
        "mla_g_kv": 1.0 + nrm((n_a, KV_LORA), 0.02),
        "mla_w_uq": nrm((n_a, Q_LORA, MLA_HEADS * (NOPE_DIM + ROPE_DIM)), Q_LORA ** -0.5),
        "mla_w_ukv": nrm((n_a, KV_LORA, MLA_HEADS * (NOPE_DIM + V_DIM)), KV_LORA ** -0.5),
        "mla_w_o": nrm((n_a, MLA_HEADS * V_DIM, D), (MLA_HEADS * V_DIM) ** -0.5),
        "s5_lam_re": -0.5 + nrm((n_b, 2, G, P), 0.01),
        "s5_lam_im": lam_im0 + nrm((n_b, 2, G, P), 0.01),
        "s5_log_step": jax.random.uniform(next(ks), (n_b, 2, G), f32,
                                          minval=math.log(S5_DT_MIN), maxval=math.log(S5_DT_MAX)),
        "s5_b_re": nrm((n_b, 2, G, P, I), (2 * I) ** -0.5),
        "s5_b_im": nrm((n_b, 2, G, P, I), (2 * I) ** -0.5),
        "s5_c_re": nrm((n_b, 2, G, I, P), (2 * P) ** -0.5),
        "s5_c_im": nrm((n_b, 2, G, I, P), (2 * P) ** -0.5),
        "s5_d": nrm((n_b, D), 1.0),
        "s5_w_glu": nrm((n_b, D, 2 * D), D ** -0.5),
        "s5_b_glu": nrm((n_b, 2 * D), 0.02),
        "moe_w_router": nrm((DEPTH, D, N_EXPERTS), D ** -0.5),
        "moe_bias": nrm((DEPTH, N_EXPERTS), 0.01),
        "moe_w_gate": nrm((DEPTH, N_EXPERTS, D, D_EXPERT), D ** -0.5),
        "moe_w_up": nrm((DEPTH, N_EXPERTS, D, D_EXPERT), D ** -0.5),
        "moe_w_down": nrm((DEPTH, N_EXPERTS, D_EXPERT, D), D_EXPERT ** -0.5),
        "sh_w_gate": nrm((DEPTH, D, D_SHARED), D ** -0.5),
        "sh_w_up": nrm((DEPTH, D, D_SHARED), D ** -0.5),
        "sh_w_down": nrm((DEPTH, D_SHARED, D), D_SHARED ** -0.5),
    }

def reference(x, c, ctx, c_ctx, ada_w, ada_b, norm_g,
              mla_w_dqkv, mla_g_q, mla_g_kv, mla_w_uq, mla_w_ukv, mla_w_o,
              s5_lam_re, s5_lam_im, s5_log_step, s5_b_re, s5_b_im, s5_c_re, s5_c_im,
              s5_d, s5_w_glu, s5_b_glu,
              moe_w_router, moe_bias, moe_w_gate, moe_w_up, moe_w_down,
              sh_w_gate, sh_w_up, sh_w_down):
    B, L, D = x.shape
    n_ctx = ctx.shape[1]
    cos_l, sin_l = axial_rope_tables(L)
    cos = jnp.concatenate([jnp.ones((n_ctx, ROPE_DIM // 2), jnp.float32), cos_l], axis=0)
    sin = jnp.concatenate([jnp.zeros((n_ctx, ROPE_DIM // 2), jnp.float32), sin_l], axis=0)
    silu_c = jax.nn.silu(c)
    silu_cc = jax.nn.silu(c_ctx)
    x_lat, x_ctx = x, ctx
    for i in range(DEPTH):
        need_ctx = i < DEPTH - 1
        j = i // N_MIXERS
        mod_lat = jnp.split((silu_c @ ada_w[i] + ada_b[i])[:, None, :], N_MOD, axis=-1)
        mod_ctx = jnp.split((silu_cc @ ada_w[i] + ada_b[i])[None, None, :], N_MOD, axis=-1)
        h_lat = modulate(rms_norm(x_lat, norm_g[i, 0]), mod_lat[0], mod_lat[1])
        h_ctx = modulate(rms_norm(x_ctx, norm_g[i, 0]), mod_ctx[0], mod_ctx[1])
        if i % N_MIXERS == 0:
            o_lat, o_ctx = mla_mixer(h_ctx, h_lat, cos, sin, mla_w_dqkv[j], mla_g_q[j], mla_g_kv[j],
                                     mla_w_uq[j], mla_w_ukv[j], mla_w_o[j], need_ctx)
        else:
            o_lat, o_ctx = s5_mixer(h_ctx, h_lat, s5_lam_re[j], s5_lam_im[j], s5_log_step[j],
                                    s5_b_re[j], s5_b_im[j], s5_c_re[j], s5_c_im[j], s5_d[j],
                                    s5_w_glu[j], s5_b_glu[j], need_ctx)
        x_lat = x_lat + mod_lat[2] * rms_norm(o_lat, norm_g[i, 1])
        f_lat_in = modulate(rms_norm(x_lat, norm_g[i, 2]), mod_lat[3], mod_lat[4])
        moe_args = (moe_w_router[i], moe_bias[i], moe_w_gate[i], moe_w_up[i], moe_w_down[i],
                    sh_w_gate[i], sh_w_up[i], sh_w_down[i])
        if need_ctx:
            x_ctx = x_ctx + mod_ctx[2] * rms_norm(o_ctx, norm_g[i, 1])
            f_ctx_in = modulate(rms_norm(x_ctx, norm_g[i, 2]), mod_ctx[3], mod_ctx[4])
            tok = jnp.concatenate([f_ctx_in.reshape(-1, D), f_lat_in.reshape(-1, D)], axis=0)
            f = moe_ffn(tok, *moe_args)
            f_ctx = f[:B * n_ctx].reshape(B, n_ctx, D)
            f_lat = f[B * n_ctx:].reshape(B, L, D)
            x_ctx = x_ctx + mod_ctx[5] * rms_norm(f_ctx, norm_g[i, 3])
        else:
            f_lat = moe_ffn(f_lat_in.reshape(-1, D), *moe_args).reshape(B, L, D)
        x_lat = x_lat + mod_lat[5] * rms_norm(f_lat, norm_g[i, 3])
    return x_lat


_drawn_inputs = setup_inputs


def setup_inputs(seed=0):
    import zlib

    import numpy as np

    out = dict(_drawn_inputs(seed))
    spreads = {}
    factors = {}
    for name, (base, spread) in spreads.items():
        noise = np.random.default_rng([zlib.crc32(name.encode()), seed]).standard_normal(out[name].shape)
        drawn = base * np.exp(spread * noise) if base else spread * noise
        out[name] = __import__('jax').numpy.asarray(drawn.astype(out[name].dtype))
    for name, factor in factors.items():
        out[name] = (out[name] * factor).astype(out[name].dtype)
    return out
```

```python
from contextlib import ExitStack

import numpy as np

import concourse.bass as bass
from concourse import mybir

F32 = mybir.dt.float32
BF16 = mybir.dt.bfloat16
U32 = mybir.dt.uint32
I32 = mybir.dt.int32
ALU = mybir.AluOpType
ACT = mybir.ActivationFunctionType
AX_X = mybir.AxisListType.X

P = 128
D = 1024
DC = D // P
N_LAT, N_CTX = 512, 256
N_ALL = N_LAT + N_CTX
CT, LT = N_CTX // P, N_LAT // P
AT = CT + LT
EPS = 1e-6
HEADS, NOPE, ROPE, VD = 8, 128, 64, 128
QL, KVL = 384, 256
QC, KC = QL // P, KVL // P
AW = QL + KVL + ROPE
QW, KVW = HEADS * (NOPE + ROPE), HEADS * (NOPE + VD)
SCALE = float(NOPE + ROPE) ** -0.5
N_EXP, FE = 64, 256
EPAD = N_EXP + 2
FC = FE // P
ROUTED = 2.5
BIG = 1.0e30
SLOT = 2 * DC * FE + FC * D
NSLOT = 4
GROUPS, GI, ST = 64, 16, 64
L = 8
LC, CC_ = N_LAT // L, N_CTX // L
NCH = LC + CC_
Q = 2 * GROUPS
QB = 8
TWO_PI = float(2.0 * np.pi)
ROUND = 12582912.0
PI_A, PI_B = 6.28125, 0.0019350051879882812
PI_C = TWO_PI - PI_A - PI_B
ADA_T = 6 * D // 512


class Steps:

    def __init__(self, eng, sem):
        self.eng, self.sem, self.n, self.off = eng, sem, 0, None

    def __call__(self, ins):
        self.n += 1
        ins.then_inc(self.sem, 1)
        self.eng.wait_ge(self.sem, self.n if self.off is None else self.off + self.n)

    def enter(self, i, per):
        self.start, self.per, self.off = self.n, per, i * per

    def leave(self, turns):
        assert self.n - self.start == self.per, self.n - self.start
        self.n, self.off = self.start + self.per * turns, None


def build(nc, I, O):
    ctx = ExitStack()
    with ctx:
        def sb(name, shape, dt=F32):
            return ctx.enter_context(nc.sbuf_tensor("sb_" + name, shape, dt))

        def dram(name, shape):
            return nc.dram_tensor("scratch_" + name, shape, F32).ap()

        sems = {}

        def S(name):
            if name not in sems:
                sems[name] = ctx.enter_context(nc.semaphore(name))
            return sems[name]

        RING = sb("ring", [P, NSLOT * SLOT])
        X = sb("x", [P, AT, D])
        ROWS = sb("rows", [P, 4, D])
        WORK = sb("work", [P, 16384])
        ident = sb("ident", [P, P])
        rot = sb("rot", [ROPE, ROPE])
        cst = sb("cst", [P, 80])
        tri = sb("tri", [P, P], BF16)
        ones_b = sb("ones_b", [P, P], BF16)
        iota_b = sb("iota_b", [P, P], BF16)
        cs = sb("cs", [P, DC, 2])
        csl = sb("csl", [P, DC, 2])
        gcol = sb("gcol", [P, QC + KC])
        eps = sb("eps", [P, 1])
        junk = sb("junk", [P, D], BF16)
        ss = sb("ss", [P, 16])
        sd = sb("sd", [P, 16])
        rs = sb("rs", [P, 16])
        sm = sb("sm", [P, 8])
        mx = sb("mx", [P, 2])
        words = sb("words", [1, 16], I32)
        befores = sb("befores", [1, N_EXP], I32)
        idxu = sb("idxu", [P, 5], U32)
        gate = sb("gate", [P, 5])
        it = sb("it", [P, 8])
        sc = sb("sc", [P, 4, GROUPS])
        PS = ctx.enter_context(nc.psum_tensor("ps", [P, 8, 512], F32))

        mod_d = dram("mod", (2, 2, 6 * D))
        f_d = [dram("f0", (N_ALL + P, D)), dram("f1", (N_LAT + P, D))]
        acc_d = [dram("acc0", (N_ALL + P, D)), dram("acc1", (N_LAT + P, D))]

        def work(a, n):
            return WORK[:, a:a + n]

        def bank2(b, n=1024):
            return PS[:, b:b + 2, :].rearrange("p b n -> p (b n)")[:, 0:n]

        ring = RING[:, :]
        w_dqkv = ring[:, 0:DC * AW].rearrange("p (j n) -> p j n", j=DC)
        OT = ring[:, 0:HEADS * N_ALL].rearrange("p (h n) -> p h n", h=HEADS)
        w_uq = ring[:, 7680:7680 + QC * QW].rearrange("p (j n) -> p j n", j=QC)
        w_ukv = ring[:, 12288:12288 + KC * KVW].rearrange("p (j n) -> p j n", j=KC)
        w_o = ring[:, 16384:24576].rearrange("p (h n) -> p h n", h=HEADS)
        HT = work(0, DC * N_ALL).rearrange("p (j n) -> p j n", j=DC)
        V = work(0, AT * D).rearrange("p (t n) -> p t n", t=AT)
        CQT = work(6144, QC * N_ALL).rearrange("p (j n) -> p j n", j=QC)
        CKT = work(8448, KC * N_ALL).rearrange("p (j n) -> p j n", j=KC)
        KPT = work(9984, N_ALL)[0:ROPE, :]
        KPR = work(10752, N_ALL)[0:ROPE, :]
        H = [work(11520, D), work(12544, D)]
        CA = work(13568, AW)
        qnT = work(11520, N_ALL)
        knT = work(12288, N_ALL)
        qpT = work(13056, N_ALL)[0:ROPE, :]
        qpR = work(13824, N_ALL)[0:ROPE, :]
        cosT = work(14592, N_ALL)[0:ROPE, :]
        sinT = work(15360, N_ALL)[0:ROPE, :]
        rows1 = ROWS[:, :, :].rearrange("p a b -> p (a b)")
        PR = [rows1[:, 0:N_ALL], work(9984, N_ALL)]
        PT = rows1[:, N_ALL:N_ALL + AT * N_LAT].rearrange("p (k q) -> p k q", k=AT)
        MOD = work(0, 6 * D)[0:2, :]
        MODB = work(6144, 6 * D)[0:2, :]
        NG = work(12288, 4 * D)[0:2, :]

        def ada_slot(n):
            return ring[:, (n % 4) * SLOT:(n % 4) * SLOT + DC * 512].rearrange("p (j n) -> p j n", j=DC)

        def slot(u):
            return ring[:, u * SLOT:(u + 1) * SLOT]

        def gu_rhs(u, j):
            return slot(u)[:, 0:2 * DC * FE].rearrange("p (w j n) -> p w j n", w=2, j=DC)[:, :, j, :]

        def dn_rhs(u, j, h):
            return slot(u)[:, 2 * DC * FE + j * D + h * 512:2 * DC * FE + j * D + h * 512 + 512]

        XG = [work(0, D), work(1024, D)]
        XT = [work(2048, D).rearrange("p (j n) -> p j n", j=DC), work(3072, D).rearrange("p (j n) -> p j n", j=DC)]
        OS = [work(4096, D), work(5120, D)]
        XGo = work(6144, D)
        SG = [work(7168, FE), work(7424, FE)]
        HH = [work(7680, FE), work(7936, FE)]
        HHT = [work(8192, FE).rearrange("p (j n) -> p j n", j=FC), work(8448, FE).rearrange("p (j n) -> p j n", j=FC)]
        OH = [work(8704 + 384 * k, 384).bitcast(BF16).rearrange("p (t n) -> p t n", t=AT) for k in range(2)]
        POSM = work(9472, AT * EPAD).rearrange("p (t e) -> p t e", t=AT)
        RH = work(9872, AT * EPAD * 3).bitcast(BF16).rearrange("p (t e c) -> p t e c", t=AT, c=6)
        MB16 = work(11064, 192).bitcast(BF16).rearrange("p (t e) -> p t e", t=AT)
        at = [13568]

        def temp(n):
            at[0] += n
            assert at[0] <= 16384
            return work(at[0] - n, n)

        def t_e(n):
            return temp(AT * n).rearrange("p (t e) -> p t e", t=AT)

        SC, BI, MR = t_e(64), t_e(64), t_e(64)
        GTE = t_e(64)
        M8 = work(6656, AT * 64).rearrange("p (t g k) -> p t g k", t=AT, g=8)
        GS, GR, G8, TR, GM, TB, E8 = t_e(16), t_e(16), t_e(8), t_e(8), t_e(8), t_e(8), t_e(8)
        WR = work(6144, DC * N_EXP).rearrange("p (j e) -> p j e", j=DC)
        BROW = temp(N_EXP)
        POSJ = temp(8)
        CNT, NB = temp(64), temp(64)


        x_rows = [I["ctx"][k * P:(k + 1) * P, :] for k in range(CT)] + [I["x"][k * P:(k + 1) * P, :] for k in range(LT)]
        stream = [1] * CT + [0] * LT
        TILES = [list(range(AT)), list(range(LT))]

        def row(k):
            return ROWS[:, k, :]

        def pe_transposes(src, dst, n, done):
            for j in range(n):
                ins = nc.tensor.transpose(dst[:, j * P:j * P + src.shape[0]], src[:, j::n], ident[0:src.shape[0], 0:src.shape[0]])
            ins.then_inc(done, 1)

        h1_d, x2_d = dram("h1", (N_ALL, D)), dram("x2", (N_LAT, D))
        left = {}

        def again(name, old, count):
            sems[name], left[name] = S(old), count

        for name, old, count in (
                ("s_rows", "rows_a", 64), ("s_h_out0", "ada_in0", 96), ("s_h_out1", "ada_in1", 96), ("s_x_out", "x_in", 16 * AT),
                ("s_hc_in", "w_dqkv_in", 16), ("s_par_in", "w_ukv_in", 16), ("s_b_in0", "w_uq_in", 16), ("s_b_in1", "w_o_in", 16),
                ("s_c_in", "ada_in2", 96), ("s_t_in", "ada_in3", 96), ("s_d_in", "rope_in", 32), ("s_wg_in0", "rows_m", 64),
                ("s_wg_in1", "const_in", 80), ("s_bg_in", "modb_in", 64), ("s_rowg", "rows_g", 32), ("s_xr_in", "mod_out", 32),
                ("s_rown", "tri_in", 32),
                ("s_hg_ready", "a_mm", AT), ("s_sd", "a_sd", 1), ("s_h_ready", "a_h_ready", AT), ("s_u_tp", "a_tp", AT), ("s_u_ready", "a_ht", 2 * AT),
                ("s_tab_v", "ca_ready", AT), ("s_tab_a", "c_sd", AT), ("s_tab_ready", "k_rope", 1), ("s_w_ready", "qn_ready", HEADS),
                ("s_w_tp", "qn_mm", HEADS), ("s_wt_ready", "qp_ready", HEADS), ("s_v_mm", "kn_mm", HEADS),
                ("s_v_ready", "ot_lat", HEADS), ("s_fwd_done", "kn_ready", HEADS), ("s_bwd_done", "mod_free", 1),
                ("s_cc_ready", "q_rope", HEADS), ("s_kk_mm", "qp_mm", HEADS), ("s_kk_ready", "ot_ctx", HEADS),
                ("s_y_mm", "q_rot", HEADS), ("s_y_ready", "p_ready", HEADS * AT), ("s_hd", "mod_ready", 2),
                ("s_gelu", "p_exp", HEADS * AT), ("s_yt_tp", "p_tp", HEADS * AT), ("s_yt", "nmax", HEADS * AT),
                ("s_glu_mm", "s_mm", HEADS * AT), ("s_z", "ct_ready", AT), ("s_sig", "pt_ready", HEADS * AT),
                ("s_oo", "o_used", AT), ("s_osd", "v_ready_a", AT), ("x3_ready", "v_ready_v", AT)):
            again(name, old, count)

        def B(name):
            return left[name]

        VST = ring[:, 0:(NCH + 1) * Q].rearrange("p (s q) -> p s q", q=Q)
        HC = ring[:, 12416:12416 + L * D].rearrange("p (t n) -> p t n", t=L)
        TEMP = ring[:, 20608:24576]
        U = work(0, GROUPS * NCH).rearrange("p (g c) -> p g c", g=GROUPS)
        TZ = work(6144, GROUPS * P).rearrange("p (g n) -> p g n", g=GROUPS)
        KKS = work(14336, 8 * 240)[0:GI, :].rearrange("p (g n) -> p g n", g=8)
        DROW = work(14336, D)
        tx = X[:, :, :].rearrange("p a b -> p (a b)")
        X1, X2 = (tx[:, a:a + 1152].rearrange("p (j q) -> p j q", q=Q) for a in (0, 1152))
        Y1, Y2 = (tx[:, a:a + 1024].rearrange("p (j q) -> p j q", q=Q) for a in (2304, 3328))
        LRE, LIM, LST = (tx[:, 4352 + k * Q:4352 + (k + 1) * Q] for k in range(3))
        tA, tTH, tEA, tK, tR, tR2, tFR, tFI, tSMI, tM, tN = (tx[:, 4736 + k * Q:4736 + (k + 1) * Q] for k in range(11))
        F1, F2 = tA, tTH
        NR, NI = (rows1[:, a:a + 1152].rearrange("p (j q) -> p j q", q=Q) for a in (0, 1152))
        TMP = rows1[:, 2304:3456]
        GR_, GI_ = (TEMP[:, a:a + 1024].rearrange("p (j q) -> p j q", q=Q) for a in (0, 1024))
        WW = TEMP[:, 0:1024]
        WT = TEMP[:, 1024:2048].rearrange("p (k n) -> p k n", k=8)
        BB = [TEMP[:, 2048 + k * 256:2304 + k * 256].rearrange("p (c q i) -> p c q i", c=2, q=QB) for k in range(2)]
        HG = [TEMP[:, 2560 + k * 512:3072 + k * 512] for k in range(2)]
        CB = TEMP[:, 0:512].rearrange("p (d c q i) -> p d c q i", d=2, c=2, q=QB)
        BD = TEMP[:, 512:1024].rearrange("p (d c q i) -> p d c q i", d=2, c=2, q=QB)
        BB2 = TEMP[:, 1024:1280].rearrange("p (d q i) -> p d q i", d=2, q=QB)
        CC = TEMP[:, 1280:3584].rearrange("p (d q j i) -> p d q j i", d=2, q=QB, i=GI)
        YT = work(0, DC * N_LAT).rearrange("p (j n) -> p j n", j=DC)
        OO = work(6144, LT * D).rearrange("p (t n) -> p t n", t=LT)
        BG = work(10240, 2 * D)
        ZT = [work(12288, D), work(13312, D)]
        WG = [ring[:, k * 8192:(k + 1) * 8192].rearrange("p (j w n) -> p j w n", j=DC, w=2) for k in range(2)]

        def scan_turn(eng, W, d):
            q = slice(d * GROUPS, (d + 1) * GROUPS)
            t1, t2 = (sc[:, k, :] for k in (2 * d, 2 * d + 1))
            half = ST

            def turn(i, step):
                cur = VST[:, bass.ds(i, 1), q].rearrange("p a q -> p (a q)")
                last = VST[:, bass.ds(i + step, 1), q].rearrange("p a q -> p (a q)")
                W(eng.tensor_tensor(t1, last, NR[:, L, q], ALU.mult))
                eng.tensor_tensor(t2[0:half], last[half:P], tSMI[half:P, q], ALU.mult)
                W(eng.tensor_tensor(t2[half:P], last[0:half], tSMI[0:half, q], ALU.mult))
                W(eng.tensor_tensor(t2, t2, t1, ALU.add))
                W(eng.tensor_tensor(cur, cur, t2, ALU.add))

            return turn

        def before_moe(l):
            n0, blocks = AT, N_EXP * (AT - 1)
            left = dict(
                wr_in=32, sh_in=48, w_in0=768, w_in1=768, w_in2=768, w_in3=768, f_out0=n0 // 2 * 16, f_out1=n0 // 2 * 16,
                f_trash=16, acc_out0=n0 // 2 * 16, acc_out1=n0 // 2 * 16, acc_out2=16, rows_in=32,
                acc_in0=n0 // 2 * 16, acc_in1=n0 // 2 * 16, h_ready=n0, zero_ready=1, so_ready_a=n0, so_ready_v=n0,
                sh_down=n0, ht_tp=n0, ht_ready=2 * n0, logits=n0, sh_gu=n0, sh_h=n0, sh_tp=n0, sh_ht=n0, mask_ready=1,
                pos_mm=1, oh_ready=EPAD, idx_mm=EPAD, idx_ready=EPAD, xg_in0=EPAD * 8, xg_in1=EPAD * 8,
                xt_tp=N_EXP + 1, xt_ready=N_EXP + 1, h_ready2=N_EXP, gu_mm=N_EXP, h_tp=N_EXP, hht_ready=N_EXP,
                out_a=N_EXP, out_v=N_EXP, dn_mm=N_EXP, words_ready=1, silu=N_EXP, os_free=N_EXP,
                scat0=N_EXP * 8, scat1=N_EXP * 8, all_scattered=1, o_step=4 * blocks, o_sd=n0, x_ready=n0,
                scores=1, sd=1, sh_silu=n0)
            for name in ("o_dn", "o_idx_mm", "o_xt_tp", "o_gu", "o_htp", "o_xt", "o_silu", "o_out_a", "o_pos", "o_oh",
                         "o_idx", "o_h", "o_hht", "o_out_v", "o_os_free", "o_xg", "o_scat"):
                left[name] = blocks
            return lambda name: l * left[name]

        block = ctx.enter_context(nc.Block())

        def moe_sp(sp, l):
            tiles, NT = TILES[l], len(TILES[l])
            T = NT * P
            g, Z = "m_", before_moe(l)
            sp.dma_start(WR, I["w_router"][l].rearrange("(p j) e -> p j e", j=DC)).then_inc(S(g + "wr_in"), 16)
            sp.dma_start(BROW, I["moe_bias"][l:l + 1, :].to_broadcast((P, N_EXP))).then_inc(S(g + "wr_in"), 16)

            def load(u, gate_w, up_w, down_w, s):
                w = slot(u)
                sp.dma_start(w[:, 0:DC * FE], gate_w.rearrange("(p j) n -> p (j n)", j=DC)).then_inc(s, 16)
                sp.dma_start(w[:, DC * FE:2 * DC * FE], up_w.rearrange("(p j) n -> p (j n)", j=DC)).then_inc(s, 16)
                sp.dma_start(w[:, 2 * DC * FE:SLOT], down_w.rearrange("(p j) n -> p (j n)", j=FC)).then_inc(s, 16)

            if l == 0:
                sp.wait_ge(S("o_mm"), AT)
            load(3, I["sh_gate"][l], I["sh_up"][l], I["sh_down"][l], S(g + "sh_in"))
            for u in range(3):
                load(u, I["w_gate"][l, u], I["w_up"][l, u], I["w_down"][l, u], S(g + f"w_in{u}"))
            for n in range(len(tiles)):
                sp.wait_ge(S(g + "h_ready"), Z("h_ready") + n + 1)
                sp.dma_start(f_d[l][n * P:(n + 1) * P, :], H[n % 2]).then_inc(S(g + f"f_out{n % 2}"), 16)
            sp.wait_ge(S(g + "zero_ready"), Z("zero_ready") + 1)
            sp.dma_start(f_d[l][T:T + P, :], ROWS[:, 0, :]).then_inc(S(g + "f_trash"), 16)
            sp.dma_start(acc_d[l][T:T + P, :], ROWS[:, 0, :]).then_inc(S(g + "acc_out2"), 16)
            for n in range(len(tiles)):
                sp.wait_ge(S(g + "so_ready_a"), Z("so_ready_a") + n + 1)
                sp.wait_ge(S(g + "so_ready_v"), Z("so_ready_v") + n + 1)
                sp.dma_start(acc_d[l][n * P:(n + 1) * P, :], H[n % 2]).then_inc(S(g + f"acc_out{n % 2}"), 16)
            sp.wait_ge(S(g + "sh_down"), Z("sh_down") + len(tiles))
            load(3, I["w_gate"][l, 3], I["w_up"][l, 3], I["w_down"][l, 3], S(g + "w_in3"))
            wg = I["w_gate"][l].rearrange("e (p j) n -> p e (j n)", j=DC)
            wu = I["w_up"][l].rearrange("e (p j) n -> p e (j n)", j=DC)
            wd = I["w_down"][l].rearrange("e (p j) n -> p e (j n)", j=FC)
            with sp.Fori(1, N_EXP // NSLOT) as eb:
                for u in range(NSLOT):
                    e = sp.snap(eb * NSLOT + u, min_val=0, max_val=N_EXP - 1)
                    done = sp.snap(eb * NSLOT + (u - NSLOT + 1), min_val=1, max_val=N_EXP)
                    blocks = sp.snap(done * (NT - 1), min_val=1, max_val=N_EXP * NT)
                    sp.wait_ge(S(g + "dn_mm"), Z("dn_mm") + done)
                    sp.sem_inc(S("sp_starts"), 1)
                    sp.wait_ge(S(g + "o_dn"), Z("o_dn") + blocks)
                    sp.sem_inc(S("sp_starts"), 1)
                    w = slot(u)
                    sp.dma_start(w[:, 0:DC * FE], wg[:, bass.ds(e, 1), :].rearrange("p a n -> p (a n)")).then_inc(S(g + f"w_in{u}"), 16)
                    sp.dma_start(w[:, DC * FE:2 * DC * FE], wu[:, bass.ds(e, 1), :].rearrange("p a n -> p (a n)")).then_inc(S(g + f"w_in{u}"), 16)
                    sp.dma_start(w[:, 2 * DC * FE:SLOT], wd[:, bass.ds(e, 1), :].rearrange("p a n -> p (a n)")).then_inc(S(g + f"w_in{u}"), 16)
            sp.wait_ge(S(g + "f_trash"), Z("f_trash") + 16)
            sp.wait_ge(S(g + "acc_out2"), Z("acc_out2") + 16)
            for k in range(2 if l == 0 else 1):
                sp.dma_start(row(k), mod_d[l, k:k + 1, 5 * D:6 * D].to_broadcast((P, D))).then_inc(S(g + "rows_in"), 16)
            sp.wait_ge(S(g + "all_scattered"), Z("all_scattered") + 1)
            for n in range(len(tiles)):
                if n >= 2:
                    sp.wait_ge(S(g + "x_ready"), Z("x_ready") + n - 1)
                sp.dma_start(OS[n % 2], acc_d[l][n * P:(n + 1) * P, :]).then_inc(S(g + f"acc_in{n % 2}"), 16)


        def s5_sp(sp):
            sp.wait_ge(S("m_x_ready"), AT)
            for t in range(LT):
                sp.dma_start(x2_d[t * P:(t + 1) * P, :], X[:, CT + t, :]).then_inc(S("s_x_out"), 16)
            for k, (q, r) in enumerate([(1, 0), (0, 0), (1, 1), (0, 1)]):
                sp.dma_start(row(k), mod_d[1, r:r + 1, q * D:(q + 1) * D].to_broadcast((P, D))).then_inc(S("s_rows"), 16)
            for t in range(AT):
                sp.wait_ge(S("s_h_ready"), B("s_h_ready") + t + 1)
                sp.dma_start(h1_d[t * P:(t + 1) * P, :], H[t % 2]).then_inc(S(f"s_h_out{t % 2}"), 16)
            for k in range(2):
                sp.wait_ge(S(f"s_h_out{k}"), B(f"s_h_out{k}") + AT // 2 * 16)
            sp.dma_start(HC[0:LC, :, :], h1_d[N_CTX:N_ALL, :].rearrange("(c t) n -> c t n", t=L)).then_inc(S("s_hc_in"), 16)
            sp.dma_start(HC[LC:NCH, :, :], h1_d[0:N_CTX, :].rearrange("(c t) n -> c t n", t=L)).then_inc(S("s_hc_in"), 16)
            sp.wait_ge(S("s_x_out"), B("s_x_out") + 16 * LT)
            sp.dma_start(tx[:, 4352:4736], I["s5_par"]).then_inc(S("s_par_in"), 16)
            sp.wait_ge(S("s_tab_ready"), B("s_tab_ready") + 1)
            for n in range(Q // QB):
                if n >= 2:
                    sp.wait_ge(S("s_w_ready"), B("s_w_ready") + n - 1)
                sp.dma_start(BB[n % 2], I["s5_b"][:, :, n * QB:(n + 1) * QB, :]).then_inc(S(f"s_b_in{n % 2}"), 16)
            sp.dma_start(DROW, I["s5_d"].to_broadcast((P, D))).then_inc(S("s_d_in"), 16)
            sp.wait_ge(S("s_v_mm"), B("s_v_mm") + Q // 4)
            for n in range(GROUPS // QB):
                if n:
                    sp.wait_ge(S("s_cc_ready"), B("s_cc_ready") + n)
                for d in range(2):
                    c = slice(d * GROUPS + n * QB, d * GROUPS + (n + 1) * QB)
                    sp.dma_start(CB[:, d], I["s5_c"][:, :, c, :]).then_inc(S("s_c_in"), 16)
                    sp.dma_start(BD[:, d], I["s5_b"][:, :, c, :]).then_inc(S("s_c_in"), 16)
                sp.wait_ge(S("s_kk_ready"), B("s_kk_ready") + n + 1)
                for k in range(L):
                    sp.dma_start(TZ[k * GI:(k + 1) * GI, n * QB:(n + 1) * QB, :],
                                 KKS[:, :, (L - 1 - k) * GI:(L - 1 - k) * GI + P]).then_inc(S("s_t_in"), 16)
            sp.wait_ge(S("s_y_mm"), B("s_y_mm") + GROUPS // QB)
            wg = I["w_glu"].rearrange("(p j) (w h n) -> p j w h n", j=DC, w=2, h=2)
            sp.dma_start(BG, I["b_glu"].to_broadcast((P, 2 * D))).then_inc(S("s_bg_in"), 16)
            for w in range(2):
                sp.dma_start(WG[0][:, :, w, :], wg[:, :, w, 0, :]).then_inc(S("s_wg_in0"), 16)
            sp.dma_start(row(0), mod_d[1, 0:1, 2 * D:3 * D].to_broadcast((P, D))).then_inc(S("s_rowg"), 16)
            xr = x2_d.rearrange("(c t) n -> t c n", t=L)
            for t in range(L):
                sp.dma_start(X[(t % 2) * LC:(t % 2 + 1) * LC, t // 2, :], xr[t]).then_inc(S("s_xr_in"), 16)
            sp.wait_ge(S("s_yt_tp"), B("s_yt_tp") + L)
            for w in range(2):
                sp.dma_start(WG[1][:, :, w, :], wg[:, :, w, 1, :]).then_inc(S("s_wg_in1"), 16)
            sp.wait_ge(S("x3_ready"), B("x3_ready") + LT)
            for k, q in enumerate((4, 3)):
                sp.dma_start(row(k), mod_d[1, 0:1, q * D:(q + 1) * D].to_broadcast((P, D))).then_inc(S("s_rown"), 16)

        @block.sync
        def _(sp):
            for name, dst in (("ident", ident[:, :]), ("rot", rot[:, :]), ("cst", cst[:, :]), ("cs", cs[:, :, :]),
                              ("gcol", gcol[:, :])):
                sp.dma_start(dst, I[name]).then_inc(S("const_in"), 16)
            sp.dma_start(work(0, P), I["tri"]).then_inc(S("tri_in"), 16)
            sp.dma_start(work(P, P), I["iota"]).then_inc(S("tri_in"), 16)
            for l in range(2):
                w = I["ada_w"][l].rearrange("(p j) n -> p j n", j=DC)
                if l == 1:
                    sp.wait_ge(S("mod_ready"), 1)
                sp.dma_start(MODB, I["ada_b"][l:l + 1, :].to_broadcast((2, 6 * D))).then_inc(S("modb_in"), 16)
                sp.dma_start(NG, I["norm_g"][l:l + 1, :].to_broadcast((2, 4 * D))).then_inc(S("modb_in"), 16)
                for m in range(ADA_T):
                    n = l * ADA_T + m
                    if n >= 4:
                        sp.wait_ge(S("ada_mm"), n - 3)
                    sp.dma_start(ada_slot(n), w[:, :, m * 512:(m + 1) * 512]).then_inc(S(f"ada_in{n % 4}"), 16)
                if l == 0:
                    for t in range(AT):
                        sp.dma_start(X[:, t, :], x_rows[t]).then_inc(S("x_in"), 16)
                sp.wait_ge(S("mod_ready"), l + 1)
                sp.dma_start(mod_d[l], MOD).then_inc(S("mod_out"), 16)
                if l == 0:
                    sp.wait_ge(S("mod_out"), 16)
                    sp.sem_inc(S("mod_free"), 1)
            sp.wait_ge(S("mod_out"), 32)

            def load_rows(l, vectors, tag):
                for k, (v, r) in enumerate(vectors):
                    sp.dma_start(row(k), mod_d[l, r:r + 1, v * D:(v + 1) * D].to_broadcast((P, D))).then_inc(S(tag), 16)

            load_rows(0, [(1, 0), (0, 0), (1, 1), (0, 1)], "rows_a")
            sp.wait_ge(S("ada_mm"), 2 * ADA_T)
            sp.dma_start(w_dqkv, I["w_dqkv"].rearrange("(p j) n -> p j n", j=DC)).then_inc(S("w_dqkv_in"), 16)
            sp.dma_start(w_ukv, I["w_ukv"].rearrange("(p j) n -> p j n", j=KC)).then_inc(S("w_ukv_in"), 16)
            sp.dma_start(w_uq, I["w_uq"].rearrange("(p j) n -> p j n", j=QC)).then_inc(S("w_uq_in"), 16)
            sp.dma_start(w_o, I["w_o"].rearrange("(h p) n -> p h n", p=P)).then_inc(S("w_o_in"), 16)
            sp.dma_start(cosT, I["cosT"]).then_inc(S("rope_in"), 16)
            sp.dma_start(sinT, I["sinT"]).then_inc(S("rope_in"), 16)
            sp.wait_ge(S("pv_ctx"), HEADS)
            sp.wait_ge(S("pv_lat"), HEADS)
            load_rows(0, [(2, 0), (2, 1)], "rows_g")
            sp.wait_ge(S("x1_ready"), AT)
            load_rows(0, [(4, 0), (3, 0), (4, 1), (3, 1)], "rows_m")
            moe_sp(sp, 0)
            s5_sp(sp)
            moe_sp(sp, 1)
            out = O["out"].rearrange("(c t) n -> t c n", t=L)
            for m in range(LT):
                sp.wait_ge(S("m_x_ready"), AT + m + 1)
                for k in range(2):
                    sp.dma_start(out[2 * m + k], X[k * LC:(k + 1) * LC, m, :]).then_inc(S("out_done"), 16)
            sp.wait_ge(S("out_done"), 16 * L)

        def moe_pe(pe, l):
            tiles, NT = TILES[l], len(TILES[l])
            g, Z = "m_", before_moe(l)
            pe.wait_ge(S(g + "wr_in"), Z("wr_in") + 32)
            for n in range(NT + 1):
                if n < NT:
                    pe.wait_ge(S(g + "h_ready"), Z("h_ready") + n + 1)
                    if n >= 2:
                        pe.wait_ge(S(g + "ht_ready"), Z("ht_ready") + 2 * (n - 1))
                    pe_transposes(H[n % 2], bank2(2 * (n % 2)), DC, S(g + "ht_tp"))
                if n:
                    a = n - 1
                    pe.wait_ge(S(g + "ht_ready"), Z("ht_ready") + 2 * n)
                    for j in range(DC):
                        mm = nc.tensor.matmul(PS[:, 7, a * 64:(a + 1) * 64], HT[:, j, a * P:(a + 1) * P], WR[:, j, :], start=j == 0, stop=j == DC - 1)
                    mm.then_inc(S(g + "logits"), 1)
            pe.wait_ge(S(g + "sh_in"), Z("sh_in") + 48)
            for n in range(NT + 1):
                if n < NT:
                    if n >= 2:
                        pe.wait_ge(S(g + "sh_h"), Z("sh_h") + n - 1)
                    for j in range(DC):
                        mm = nc.tensor.matmul(PS[:, 4 + n % 2, :], HT[:, j, n * P:(n + 1) * P], gu_rhs(3, j), start=j == 0, stop=j == DC - 1)
                    mm.then_inc(S(g + "sh_gu"), 1)
                if n:
                    a = n - 1
                    pe.wait_ge(S(g + "sh_h"), Z("sh_h") + a + 1)
                    if a:
                        pe.wait_ge(S(g + "sh_ht"), Z("sh_ht") + a)
                    pe_transposes(HH[a % 2], PS[:, 6, :], FC, S(g + "sh_tp"))
                    pe.wait_ge(S(g + "sh_ht"), Z("sh_ht") + a + 1)
                    if a >= 2:
                        pe.wait_ge(S(g + "so_ready_a"), Z("so_ready_a") + a - 1)
                        pe.wait_ge(S(g + "so_ready_v"), Z("so_ready_v") + a - 1)
                    for half in range(2):
                        for j in range(FC):
                            mm = nc.tensor.matmul(PS[:, 2 * (a % 2) + half, :], HHT[a % 2][:, j, :], dn_rhs(3, j, half), start=j == 0, stop=j == FC - 1)
                    mm.then_inc(S(g + "sh_down"), 1)
            pe.wait_ge(S(g + "mask_ready"), Z("mask_ready") + 1)
            for n in range(NT):
                for b in range(n):
                    nc.tensor.matmul(PS[:, 7, n * 64:(n + 1) * 64], ones_b[:, :], MB16[:, b, :], start=b == 0, stop=False)
                nc.tensor.matmul(PS[:, 7, n * 64:(n + 1) * 64], tri[:, :], MB16[:, n, :], start=n == 0, stop=True)
            for b in range(NT):
                mm = nc.tensor.matmul(PS[:, 7, 384:448], ones_b[:, :], MB16[:, b, :], start=b == 0, stop=b == NT - 1)
            mm.then_inc(S(g + "pos_mm"), 1)
            pe.wait_ge(S(g + "so_ready_a"), Z("so_ready_a") + NT)
            pe.wait_ge(S(g + "so_ready_v"), Z("so_ready_v") + NT)

            def pick(k, e):
                for n in range(NT):
                    mm = nc.tensor.matmul(PS[:, 7, 0:6], OH[k][:, n, :], RH[:, n, bass.ds(e, 1), :].rearrange("p a c -> p (a c)"),
                                          start=n == 0, stop=n == NT - 1)
                return mm

            def gate_up(xt, u, b):
                for j in range(DC):
                    mm = nc.tensor.matmul(PS[:, b, :], xt[:, j, :], gu_rhs(u, j), start=j == 0, stop=j == DC - 1)
                return mm

            def down(hht, u):
                for half in range(2):
                    for j in range(FC):
                        mm = nc.tensor.matmul(PS[:, 4 + half, :], hht[:, j, :], dn_rhs(u, j, half), start=j == 0, stop=j == FC - 1)
                return mm

            for e in range(2):
                pe.wait_ge(S(g + "oh_ready"), Z("oh_ready") + e + 1)
                if e:
                    pe.wait_ge(S(g + "idx_ready"), Z("idx_ready") + e)
                pick(e % 2, e).then_inc(S(g + "idx_mm"), 1)
            pe.wait_ge(S(g + "xg_in0"), Z("xg_in0") + 16)
            pe_transposes(XG[0], bank2(0), DC, S(g + "xt_tp"))

            pe.wait_ge(S(g + "words_ready"), Z("words_ready") + 1)
            with pe.Fori(0, N_EXP // NSLOT) as eb:
                word = pe.value_load(words[0:1, bass.ds(eb, 1)], min_val=0, max_val=8 ** NSLOT - 1)
                for u in range(NSLOT):
                    e = eb * NSLOT + u
                    pe.wait_ge(S(g + f"w_in{u}"), Z(f"w_in{u}") + eb * 48 + 48)
                    pe.wait_ge(S(g + "xt_ready"), Z("xt_ready") + e + 1)
                    pe.wait_ge(S(g + "h_ready2"), Z("h_ready2") + e)
                    gate_up(XT[u % 2], u, 2 + u % 2).then_inc(S(g + "gu_mm"), 1)
                    pe.wait_ge(S(g + "oh_ready"), Z("oh_ready") + e + 3)
                    pe.wait_ge(S(g + "idx_ready"), Z("idx_ready") + e + 2)
                    pick(u % 2, pe.snap(e + 2, min_val=0, max_val=EPAD - 1)).then_inc(S(g + "idx_mm"), 1)
                    pe.wait_ge(S(g + f"xg_in{(u + 1) % 2}"), Z(f"xg_in{(u + 1) % 2}") + (eb * 2 + (u + 1) // 2) * 16 + 16)
                    pe.wait_ge(S(g + "xt_ready"), Z("xt_ready") + e + 1)
                    pe_transposes(XG[(u + 1) % 2], bank2(0), DC, S(g + "xt_tp"))
                    pe.wait_ge(S(g + "h_ready2"), Z("h_ready2") + e + 1)
                    pe.wait_ge(S(g + "hht_ready"), Z("hht_ready") + e)
                    pe_transposes(HH[u % 2], PS[:, 6, :], FC, S(g + "h_tp"))
                    pe.wait_ge(S(g + "hht_ready"), Z("hht_ready") + e + 1)
                    pe.wait_ge(S(g + "out_a"), Z("out_a") + e)
                    pe.wait_ge(S(g + "out_v"), Z("out_v") + e)
                    down(HHT[u % 2], u).then_inc(S(g + "dn_mm"), 1)
                    extra = pe.snap((word >> (3 * u)) & 7, min_val=0, max_val=7)
                    with pe.If(extra > 0):
                        with pe.Fori(1, NT) as b:
                            m = e * (NT - 1) + b
                            with pe.If(extra > b - 1):
                                pe.wait_ge(S(g + "o_oh"), Z("o_oh") + m)
                                pe.wait_ge(S(g + "idx_ready"), Z("idx_ready") + e + 3)
                                pick(u % 2, pe.snap(e, min_val=0, max_val=EPAD - 1)).then_inc(S(g + "o_idx_mm"), 1)
                                pe.wait_ge(S(g + "o_xg"), Z("o_xg") + m)
                                pe.wait_ge(S(g + "xt_ready"), Z("xt_ready") + e + 2)
                                pe_transposes(XGo, bank2(0), DC, S(g + "o_xt_tp"))
                                pe.wait_ge(S(g + "o_xt"), Z("o_xt") + m)
                                gate_up(XT[u % 2], u, 2 + u % 2).then_inc(S(g + "o_gu"), 1)
                                pe.wait_ge(S(g + "o_h"), Z("o_h") + m)
                                pe_transposes(HH[u % 2], PS[:, 6, :], FC, S(g + "o_htp"))
                                pe.wait_ge(S(g + "o_hht"), Z("o_hht") + m)
                                pe.wait_ge(S(g + "out_a"), Z("out_a") + e + 1)
                                pe.wait_ge(S(g + "out_v"), Z("out_v") + e + 1)
                                down(HHT[u % 2], u).then_inc(S(g + "o_dn"), 1)
                                mm = pe.snap(m, min_val=1, max_val=N_EXP * (NT - 1))
                                pe.wait_ge(S(g + "words_ready"), Z("words_ready") + 1)
                                pe.wait_ge(S(g + "o_scat"), Z("o_scat") + mm)
                            with pe.Else():
                                for q in ("o_idx_mm", "o_xt_tp", "o_gu", "o_htp", "o_dn"):
                                    pe.sem_inc(S(g + q), 1)
                    with pe.Else():
                        for q in ("o_idx_mm", "o_xt_tp", "o_gu", "o_htp", "o_dn"):
                            pe.sem_inc(S(g + q), NT - 1)


        def s5_pe(pe):
            pe.wait_ge(S("s_hc_in"), B("s_hc_in") + 32)
            for n in range(GROUPS // 4):
                if n >= 4:
                    pe.wait_ge(S("s_u_ready"), B("s_u_ready") + n - 3)
                pe.wait_ge(S("s_hg_ready"), B("s_hg_ready") + n + 1)
                for k in range(4):
                    mm = nc.tensor.transpose(PS[:, n % 4, k * NCH:(k + 1) * NCH], HG[n % 2][0:NCH, k * P:(k + 1) * P], ident[0:NCH, 0:NCH])
                mm.then_inc(S("s_u_tp"), 1)
            pe.wait_ge(S("s_u_ready"), B("s_u_ready") + GROUPS // 4)
            units = Q // 4
            for n in range(units + 1):
                if n < units:
                    pe.wait_ge(S("s_w_ready"), B("s_w_ready") + n // 2 + 1)
                    if n >= 2:
                        pe.wait_ge(S("s_wt_ready"), B("s_wt_ready") + n - 1)
                    for k in range(4):
                        mm = nc.tensor.transpose(PS[:, 4 + n % 2, k * P:(k + 1) * P], WW[:, (4 * (n % 2) + k) * P:(4 * (n % 2) + k + 1) * P], ident[:, :])
                    mm.then_inc(S("s_w_tp"), 1)
                if n:
                    a = n - 1
                    pe.wait_ge(S("s_wt_ready"), B("s_wt_ready") + n)
                    if a >= 2:
                        pe.wait_ge(S("s_v_ready"), B("s_v_ready") + a - 1)
                    for k in range(4):
                        g = (4 * a + k) % GROUPS
                        mm = nc.tensor.matmul(PS[:, 6 + a % 2, k * NCH:(k + 1) * NCH], WT[:, 4 * (a % 2) + k, :], U[:, g, :], start=True, stop=True)
                    mm.then_inc(S("s_v_mm"), 1)
            pe.wait_ge(S("s_v_ready"), B("s_v_ready") + units)
            for n in range(GROUPS // QB):
                pe.wait_ge(S("s_cc_ready"), B("s_cc_ready") + n + 1)
                if n:
                    pe.wait_ge(S("s_kk_ready"), B("s_kk_ready") + n)
                for k in range(QB):
                    ps = PS[0:GI, k // 2, (k % 2) * 240:(k % 2 + 1) * 240]
                    nc.tensor.matmul(ps[:, 0:112], BB2[:, 1, k, :], CC[:, 1, k, 1:8, :].rearrange("p j i -> p (j i)"), start=True, stop=True)
                    nc.tensor.matmul(ps[:, 112:240], BB2[:, 0, k, :], CC[:, 0, k, 0:8, :].rearrange("p j i -> p (j i)"), start=True, stop=False)
                    mm = nc.tensor.matmul(ps[:, 112:128], BB2[:, 1, k, :], CC[:, 1, k, 8, :], start=False, stop=True)
                mm.then_inc(S("s_kk_mm"), 1)
                if n == 0:
                    pe.wait_ge(S("s_fwd_done"), B("s_fwd_done") + 1)
                    pe.wait_ge(S("s_bwd_done"), B("s_bwd_done") + 1)
                if n >= 2:
                    pe.wait_ge(S("s_y_ready"), B("s_y_ready") + n - 1)
                for k in range(QB):
                    g = n * QB + k
                    ps = PS[0:LC, 4 + 2 * (n % 2) + k // 4, (k % 4) * P:(k % 4 + 1) * P]
                    nc.tensor.matmul(ps, VST[:, 0:LC, g], CC[:, 0, k, 1:9, :].rearrange("p j i -> p (j i)"), start=k % 4 == 0, stop=False, skip_group_check=True)
                    nc.tensor.matmul(ps, VST[:, 2:LC + 2, GROUPS + g], CC[:, 1, k, 0:8, :].rearrange("p j i -> p (j i)"), start=False, stop=False, skip_group_check=True)
                pe.wait_ge(S("s_t_in"), B("s_t_in") + 16 * L * (n + 1))
                for k in range(QB):
                    g = n * QB + k
                    ps = PS[0:LC, 4 + 2 * (n % 2) + k // 4, (k % 4) * P:(k % 4 + 1) * P]
                    mm = nc.tensor.matmul(ps, U[:, g, 0:LC], TZ[:, g, :], start=False, stop=k % 4 == 3, skip_group_check=True)
                mm.then_inc(S("s_y_mm"), 1)
            for t in range(L):
                pe.wait_ge(S("s_gelu"), B("s_gelu") + t + 1)
                if t >= 4:
                    pe.wait_ge(S("s_yt"), B("s_yt") + t - 3)
                for j in range(DC):
                    mm = nc.tensor.transpose(PS[:, t % 4, j * LC:(j + 1) * LC], HC[0:LC, t, j::DC], ident[0:LC, 0:LC])
                mm.then_inc(S("s_yt_tp"), 1)
            pe.wait_ge(S("s_yt"), B("s_yt") + L)
            pe.wait_ge(S("s_y_ready"), B("s_y_ready") + GROUPS // QB)
            for n in range(2 * LT):
                h, m = n // LT, n % LT
                pe.wait_ge(S(f"s_wg_in{h}"), B(f"s_wg_in{h}") + 32)
                if n >= 2:
                    pe.wait_ge(S("s_z"), B("s_z") + n - 1)
                for w in range(2):
                    for j in range(DC):
                        mm = nc.tensor.matmul(PS[:, 4 + 2 * (n % 2) + w, :], YT[:, j, m * P:(m + 1) * P], WG[h][:, j, w, :], start=j == 0, stop=j == DC - 1)
                mm.then_inc(S("s_glu_mm"), 1)
            pe.wait_ge(S("s_z"), B("s_z") + 2 * LT)

        @block.tensor
        def _(pe):
            pe.wait_ge(S("cs_ready"), 1)
            pe.wait_ge(S("const_in"), 5 * 16)
            for n in range(2 * ADA_T):
                pe.wait_ge(S(f"ada_in{n % 4}"), 16 * (n // 4 + 1))
                if n >= 4:
                    pe.wait_ge(S("ada_ev"), n - 3)
                for j in range(DC):
                    mm = nc.tensor.matmul(PS[0:2, n % 4, :], csl[:, j, :], ada_slot(n)[:, j, :], start=j == 0, stop=j == DC - 1)
                mm.then_inc(S("ada_mm"), 1)
            pe.wait_ge(S("ada_ev"), 2 * ADA_T)
            pe.wait_ge(S("w_dqkv_in"), 16)
            for t in range(AT + 2):
                if t < AT:
                    pe.wait_ge(S("a_h_ready"), t + 1)
                    if t >= 1:
                        pe.wait_ge(S("a_ht"), 2 * t)
                    pe_transposes(H[t % 2], bank2(0), DC, S("a_tp"))
                if 1 <= t <= AT:
                    a = t - 1
                    pe.wait_ge(S("a_ht"), 2 * (a + 1))
                    if a >= 2:
                        pe.wait_ge(S("ca_ready"), a - 1)
                    for lo, hi in ((0, 512), (512, AW)):
                        for j in range(DC):
                            mm = nc.tensor.matmul(PS[:, 4 + 2 * (a % 2) + lo // 512, 0:hi - lo], HT[:, j, a * P:(a + 1) * P],
                                                  w_dqkv[:, j, lo:hi], start=j == 0, stop=j == DC - 1)
                    mm.then_inc(S("a_mm"), 1)
                if t >= 2:
                    a = t - 2
                    pe.wait_ge(S("ca_ready"), a + 1)
                    if a >= 1:
                        pe.wait_ge(S("ct_ready"), a)
                    ct = bank2(2)
                    for j in range(QC):
                        nc.tensor.transpose(ct[:, j * P:(j + 1) * P], CA[:, j:QL:QC], ident[:, :])
                    for j in range(KC):
                        nc.tensor.transpose(ct[:, (QC + j) * P:(QC + j + 1) * P], CA[:, QL + j:QL + KVL:KC], ident[:, :])
                    nc.tensor.transpose(ct[0:ROPE, (QC + KC) * P:(QC + KC + 1) * P], CA[:, QL + KVL:AW], ident[:, :])\
                        .then_inc(S("ct_tp"), 1)
            pe.wait_ge(S("ct_ready"), AT)
            pe.wait_ge(S("w_ukv_in"), 16)
            for n in range(2 * AT):
                t, half = n // 2, n % 2
                if n >= 4:
                    pe.wait_ge(S("v_ready_a"), (n - 3 + 1) // 2)
                    pe.wait_ge(S("v_ready_v"), (n - 3) // 2)
                for j in range(KC):
                    rhs = w_ukv[:, j, :].rearrange("p (h x) -> p h x", x=NOPE + VD)[:, 4 * half:4 * half + 4, NOPE:NOPE + VD]
                    mm = nc.tensor.matmul(PS[:, 4 + n % 4, :], CKT[:, j, t * P:(t + 1) * P], rhs, start=j == 0, stop=j == KC - 1)
                mm.then_inc(S("v_mm"), 1)

            def rotate(dst, src, done):
                nc.tensor.matmul(dst[:, 0:512], rot[:, :], src[:, 0:512], start=True, stop=True)
                nc.tensor.matmul(dst[:, 512:N_ALL], rot[:, :], src[:, 512:N_ALL], start=True, stop=True).then_inc(done, 1)

            pe.wait_ge(S("v_ready_a"), AT)
            pe.wait_ge(S("v_ready_v"), AT)
            rotate(bank2(6)[0:ROPE], KPT, S("k_rot"))
            pe.wait_ge(S("w_uq_in"), 16)

            def project(dst, w, col, m, src, n, done):
                for lo, hi in ((0, 512), (512, N_ALL)):
                    for j in range(n):
                        mm = nc.tensor.matmul(dst[0:m, lo:hi], w[:, j, col:col + m], src[:, j, lo:hi], start=j == 0, stop=j == n - 1)
                mm.then_inc(done, 1)

            for h in range(HEADS):
                if h:
                    pe.wait_ge(S("p_ready"), AT * h)
                    pe.wait_ge(S("pt_ready"), AT * h)
                    pe.wait_ge(S("q_rope"), h)
                project(bank2(4), w_uq, h * (NOPE + ROPE) + NOPE, ROPE, CQT, QC, S("qp_mm"))
                project(bank2(0), w_uq, h * (NOPE + ROPE), NOPE, CQT, QC, S("qn_mm"))
                project(bank2(2), w_ukv, h * (NOPE + VD), NOPE, CKT, KC, S("kn_mm"))
                pe.wait_ge(S("qp_ready"), h + 1)
                if h == 0:
                    pe.wait_ge(S("k_rope"), 1)
                if h:
                    pe.wait_ge(S("ot_lat"), h)
                    pe.wait_ge(S("ot_ctx"), h)
                rotate(bank2(6)[0:ROPE], qpT, S("q_rot"))
                pe.wait_ge(S("qn_ready"), h + 1)
                pe.wait_ge(S("kn_ready"), h + 1)
                pe.wait_ge(S("q_rope"), h + 1)
                for t in range(AT + 1):
                    if t < AT:
                        k = h * AT + t
                        if k >= 2:
                            pe.wait_ge(S("p_exp"), k - 1)
                        q0, nk = (N_CTX + t * P, N_ALL) if t < LT else ((t - LT) * P, N_CTX)
                        dst = bank2(2 * (t % 2))
                        for lo, hi in ((0, 512), (512, N_ALL)):
                            hi = min(hi, nk)
                            if lo < hi:
                                nc.tensor.matmul(dst[:, lo:hi], qnT[:, q0:q0 + P], knT[:, lo:hi], start=True, stop=False)
                                mm = nc.tensor.matmul(dst[:, lo:hi], qpR[:, q0:q0 + P], KPR[:, lo:hi], start=False, stop=True)
                        mm.then_inc(S("s_mm"), 1)
                    if t >= 1:
                        k = h * AT + t - 1
                        pe.wait_ge(S("p_ready"), k + 1)
                        if k:
                            pe.wait_ge(S("pt_ready"), k)
                        nk = AT if t - 1 < LT else CT
                        for c in range(nk):
                            mm = nc.tensor.transpose(bank2(4)[:, c * P:(c + 1) * P], PR[(t - 1) % 2][:, c * P:(c + 1) * P], ident[:, :])
                        mm.then_inc(S("p_tp"), 1)
                    if t == LT:
                        pe.wait_ge(S("pt_ready"), h * AT + LT)
                        for c in range(AT):
                            mm = nc.tensor.matmul(PS[:, 6, :], V[:, c, h * P:(h + 1) * P], PT[:, c, :], start=c == 0, stop=c == AT - 1)
                        mm.then_inc(S("pv_lat"), 1)
                pe.wait_ge(S("pt_ready"), (h + 1) * AT)
                for c in range(CT):
                    mm = nc.tensor.matmul(PS[:, 7, 0:N_CTX], V[:, c, h * P:(h + 1) * P], PT[:, c, 0:N_CTX], start=c == 0, stop=c == CT - 1)
                mm.then_inc(S("pv_ctx"), 1)
            pe.wait_ge(S("w_o_in"), 16)
            pe.wait_ge(S("ot_lat"), HEADS)
            pe.wait_ge(S("ot_ctx"), HEADS)
            for t in range(AT):
                if t >= 2:
                    pe.wait_ge(S("o_used"), t - 1)
                for half in range(2):
                    for h in range(HEADS):
                        mm = nc.tensor.matmul(PS[:, 2 * (t % 2) + half, :], OT[:, h, t * P:(t + 1) * P],
                                              w_o[:, h, half * 512:(half + 1) * 512], start=h == 0, stop=h == HEADS - 1)
                mm.then_inc(S("o_mm"), 1)
            pe.wait_ge(S("o_used"), AT)
            moe_pe(pe, 0)
            s5_pe(pe)
            moe_pe(pe, 1)

        def moe_act(act, A, l):
            tiles, NT = TILES[l], len(TILES[l])
            g, Z = "m_", before_moe(l)
            for n in range(NT):
                act.wait_ge(S("x1_ready") if l == 0 else S("x3_ready"), n + 1 + (B("x3_ready") if l else 0))
                A(act.activation(junk[:, :], X[:, n, :], ACT.Square, accum_out=ss[:, n:n + 1]))
            act.activation(sd[:, 0:NT], ss[:, 0:NT], ACT.Sqrt, scale=1.0 / D, bias=eps[:, 0:1]).then_inc(S(g + "sd"), 1)
            for n in range(NT):
                act.wait_ge(S(g + "ht_tp"), Z("ht_tp") + n + 1)
                for k in range(2):
                    act.activation(HT[:, 4 * k:4 * k + 4, n * P:(n + 1) * P],
                                   PS[:, 2 * (n % 2) + k, :].rearrange("p (j n) -> p j n", j=4), ACT.Copy).then_inc(S(g + "ht_ready"), 1)
            act.wait_ge(S(g + "logits"), Z("logits") + NT)
            act.activation(SC[:, 0:NT, :], PS[:, 7, 0:NT * 64].rearrange("p (t e) -> p t e", t=NT), ACT.Sigmoid).then_inc(S(g + "scores"), 1)
            for n in range(NT):
                act.wait_ge(S(g + "sh_gu"), Z("sh_gu") + n + 1)
                if n >= 2:
                    act.wait_ge(S(g + "sh_h"), Z("sh_h") + n - 1)
                act.activation(SG[n % 2], PS[:, 4 + n % 2, 0:FE], ACT.Silu).then_inc(S(g + "sh_silu"), 1)
                act.wait_ge(S(g + "sh_down"), Z("sh_down") + n + 1)
                if n == 0:
                    for k in range(2):
                        act.wait_ge(S(g + f"f_out{k}"), Z(f"f_out{k}") + NT // 2 * 16)
                if n >= 2:
                    act.wait_ge(S(g + f"acc_out{n % 2}"), Z(f"acc_out{n % 2}") + n // 2 * 16)
                act.activation(H[n % 2][:, 0:512], PS[:, 2 * (n % 2), :], ACT.Copy).then_inc(S(g + "so_ready_a"), 1)

            def scaled(dst, k, s):
                act.activation(dst[:, 0:512], PS[:, 4, :], ACT.Copy, scale=gate[:, k:k + 1]).then_inc(s, 1)

            act.wait_ge(S(g + "sh_down"), Z("sh_down") + NT)
            act.wait_ge(S(g + "xt_tp"), Z("xt_tp") + 1)
            act.activation(XT[0], bank2(0).rearrange("p (j n) -> p j n", j=DC), ACT.Copy).then_inc(S(g + "xt_ready"), 1)
            act.wait_ge(S(g + "words_ready"), Z("words_ready") + 1)
            with act.Fori(0, N_EXP // NSLOT) as eb:
                word = act.value_load(words[0:1, bass.ds(eb, 1)], min_val=0, max_val=8 ** NSLOT - 1)
                for u in range(NSLOT):
                    e = eb * NSLOT + u
                    act.wait_ge(S(g + "gu_mm"), Z("gu_mm") + e + 1)
                    act.activation(SG[u % 2], PS[:, 2 + u % 2, 0:FE], ACT.Silu).then_inc(S(g + "silu"), 1)
                    act.wait_ge(S(g + "xt_tp"), Z("xt_tp") + e + 2)
                    act.activation(XT[(u + 1) % 2], bank2(0).rearrange("p (j n) -> p j n", j=DC), ACT.Copy).then_inc(S(g + "xt_ready"), 1)
                    act.wait_ge(S(g + "dn_mm"), Z("dn_mm") + e + 1)
                    act.wait_ge(S(g + "os_free"), Z("os_free") + e + 1)
                    scaled(OS[u % 2], u, S(g + "out_a"))
                    extra = act.snap((word >> (3 * u)) & 7, min_val=0, max_val=7)
                    with act.If(extra > 0):
                        with act.Fori(1, NT) as b:
                            m = e * (NT - 1) + b
                            with act.If(extra > b - 1):
                                act.wait_ge(S(g + "o_xt_tp"), Z("o_xt_tp") + m)
                                act.activation(XT[u % 2], bank2(0).rearrange("p (j n) -> p j n", j=DC), ACT.Copy).then_inc(S(g + "o_xt"), 1)
                                act.wait_ge(S(g + "o_gu"), Z("o_gu") + m)
                                act.activation(SG[u % 2], PS[:, 2 + u % 2, 0:FE], ACT.Silu).then_inc(S(g + "o_silu"), 1)
                                act.wait_ge(S(g + "o_dn"), Z("o_dn") + m)
                                act.wait_ge(S(g + "o_os_free"), Z("o_os_free") + m)
                                scaled(OS[u % 2], 4, S(g + "o_out_a"))
                                mm = act.snap(m, min_val=1, max_val=N_EXP * (NT - 1))
                                act.wait_ge(S(g + "words_ready"), Z("words_ready") + 1)
                                act.wait_ge(S(g + "o_scat"), Z("o_scat") + mm)
                            with act.Else():
                                for q in ("o_xt", "o_silu", "o_out_a"):
                                    act.sem_inc(S(g + q), 1)
                    with act.Else():
                        for q in ("o_xt", "o_silu", "o_out_a"):
                            act.sem_inc(S(g + q), NT - 1)
            for n in range(NT):
                act.wait_ge(S(g + f"acc_in{n % 2}"), Z(f"acc_in{n % 2}") + 16 * (n // 2 + 1))
                A(act.activation(junk[:, :], OS[n % 2], ACT.Square, accum_out=ss[:, n:n + 1]))
                act.activation(sd[:, n:n + 1], ss[:, n:n + 1], ACT.Sqrt, scale=1.0 / D, bias=eps[:, 0:1]).then_inc(S(g + "o_sd"), 1)


        def s5_act(act, A):
            for t in range(AT):
                act.wait_ge(S("m_x_ready"), t + 1)
                A(act.activation(junk[:, :], X[:, t, :], ACT.Square, accum_out=ss[:, t:t + 1]))
            act.activation(sd[:, 0:AT], ss[:, 0:AT], ACT.Sqrt, scale=1.0 / D, bias=eps[:, 0:1]).then_inc(S("s_sd"), 1)
            act.wait_ge(S("s_par_in"), B("s_par_in") + 16)
            act.activation(tEA, LST, ACT.Exp).then_inc(S("s_tab_a"), 1)
            act.wait_ge(S("s_tab_v"), B("s_tab_v") + 1)
            act.activation(tEA, tA, ACT.Exp).then_inc(S("s_tab_a"), 1)
            act.activation(tR, tR, ACT.Sin).then_inc(S("s_tab_a"), 1)
            act.activation(tR2, tR2, ACT.Sin).then_inc(S("s_tab_a"), 1)
            for n in range(GROUPS // 4):
                act.wait_ge(S("s_u_tp"), B("s_u_tp") + n + 1)
                act.activation(U[:, 4 * n:4 * n + 4, :], PS[:, n % 4, 0:4 * NCH].rearrange("p (g c) -> p g c", g=4), ACT.Copy)\
                    .then_inc(S("s_u_ready"), 1)
            units = Q // 4
            for n in range(units + 1):
                if n < units:
                    act.wait_ge(S("s_w_tp"), B("s_w_tp") + n + 1)
                    if n >= 2:
                        act.wait_ge(S("s_v_mm"), B("s_v_mm") + n - 1)
                    act.activation(WT[:, 4 * (n % 2):4 * (n % 2) + 4, :], PS[:, 4 + n % 2, :].rearrange("p (k n) -> p k n", k=4), ACT.Copy)\
                        .then_inc(S("s_wt_ready"), 1)
                if n:
                    a = n - 1
                    act.wait_ge(S("s_v_mm"), B("s_v_mm") + n)
                    act.activation(VST[:, 1:NCH + 1, 4 * a:4 * a + 4].rearrange("p s q -> p q s"),
                                   PS[:, 6 + a % 2, 0:4 * NCH].rearrange("p (q s) -> p q s", q=4), ACT.Copy).then_inc(S("s_v_ready"), 1)
            for n in range(GROUPS // QB):
                act.wait_ge(S("s_kk_mm"), B("s_kk_mm") + n + 1)
                if n == 0:
                    act.wait_ge(S("s_hd"), B("s_hd") + 1)
                else:
                    act.wait_ge(S("s_t_in"), B("s_t_in") + 16 * L * n)
                act.activation(KKS.rearrange("p (b w) n -> p b (w n)", w=2), PS[0:GI, 0:4, 0:480], ACT.Copy).then_inc(S("s_kk_ready"), 1)
            act.wait_ge(S("s_y_ready"), B("s_y_ready") + GROUPS // QB)
            for t in range(L):
                act.activation(HC[0:LC, t, :], HC[0:LC, t, :], ACT.Gelu_apprx_tanh).then_inc(S("s_gelu"), 1)
            for n in range(2 * LT):
                act.wait_ge(S("s_z"), B("s_z") + n + 1)
                act.activation(ZT[n % 2][:, 512:1024], ZT[n % 2][:, 512:1024], ACT.Sigmoid).then_inc(S("s_sig"), 1)
            for m in range(LT):
                act.wait_ge(S("s_oo"), B("s_oo") + LT + m + 1)
                A(act.activation(junk[:, :], OO[:, m, :], ACT.Square, accum_out=ss[:, 8 + m:9 + m]))
                act.activation(sd[:, 8 + m:9 + m], ss[:, 8 + m:9 + m], ACT.Sqrt, scale=1.0 / D, bias=eps[:, 0:1]).then_inc(S("s_osd"), 1)

        @block.scalar
        def _(act):
            A = Steps(act, S("act_step"))
            act.wait_ge(S("const_in"), 5 * 16)
            act.activation(csl[:, :, :], cs[:, :, :], ACT.Silu).then_inc(S("cs_ready"), 1)
            for t in range(AT):
                act.wait_ge(S("x_in"), 16 * AT)
                A(act.activation(junk[:, :], X[:, t, :], ACT.Square, accum_out=ss[:, t:t + 1]))
            act.wait_ge(S("eps_ready"), 1)
            act.activation(sd[:, 0:AT], ss[:, 0:AT], ACT.Sqrt, scale=1.0 / D, bias=eps[:, 0:1]).then_inc(S("a_sd"), 1)
            act.wait_ge(S("mod_out"), 32)
            for t in range(AT + 1):
                if t < AT:
                    act.wait_ge(S("a_tp"), t + 1)
                    for k in range(2):
                        act.activation(HT[:, 4 * k:4 * k + 4, t * P:(t + 1) * P],
                                       PS[:, k, :].rearrange("p (j n) -> p j n", j=4), ACT.Copy).then_inc(S("a_ht"), 1)
                if t:
                    a = t - 1
                    b = 4 + 2 * (a % 2)
                    act.wait_ge(S("a_mm"), a + 1)
                    if a:
                        act.wait_ge(S("c_sd"), a)
                    act.activation(junk[:, 0:QL], bank2(b)[:, 0:QL], ACT.Square, scale=QL ** -0.5, accum_out=ss[:, 0:1])
                    A(act.activation(junk[:, QL:QL + KVL], bank2(b)[:, QL:QL + KVL], ACT.Square, scale=KVL ** -0.5, accum_out=ss[:, 1:2]))
                    if a:
                        act.wait_ge(S("ca_ready"), a)
                    act.activation(sd[:, 6:8], ss[:, 0:2], ACT.Sqrt, bias=eps[:, 0:1]).then_inc(S("c_sd"), 1)
            for n in range(0, 2 * AT, 2):
                act.wait_ge(S("v_mm"), n + 1)
                act.activation(V[:, n // 2, 0:512], PS[:, 4 + n % 4, :], ACT.Copy).then_inc(S("v_ready_a"), 1)
            for h in range(HEADS):
                act.wait_ge(S("qp_mm"), h + 1)
                act.activation(qpT, bank2(4, N_ALL)[0:ROPE], ACT.Copy).then_inc(S("qp_ready"), 1)
                act.wait_ge(S("qn_mm"), h + 1)
                act.activation(qnT, bank2(0, N_ALL), ACT.Copy).then_inc(S("qn_ready"), 1)
                for t in range(AT + 1):
                    if t < AT:
                        k = h * AT + t
                        nk = N_ALL if t < LT else N_CTX
                        act.wait_ge(S("nmax"), k + 1)
                        if k >= 2:
                            act.wait_ge(S("p_tp"), k - 1)
                        act.activation(PR[t % 2][:, 0:nk], bank2(2 * (t % 2), nk), ACT.Exp, bias=mx[:, t % 2:t % 2 + 1],
                                       scale=SCALE, accum_out=sm[:, t % 2:t % 2 + 1]).then_inc(S("p_exp"), 1)
                    if t:
                        k = h * AT + t - 1
                        nk = AT if t - 1 < LT else CT
                        act.wait_ge(S("p_tp"), k + 1)
                        if t - 1 == 0 and h:
                            act.wait_ge(S("pv_ctx"), h)
                        if t - 1 == LT:
                            act.wait_ge(S("pv_lat"), h + 1)
                        q0 = (t - 1) * P if t - 1 < LT else (t - 1 - LT) * P
                        act.activation(PT[:, 0:nk, q0:q0 + P], bank2(4, nk * P).rearrange("p (c q) -> p c q", c=nk), ACT.Copy)\
                            .then_inc(S("pt_ready"), 1)
                act.wait_ge(S("pv_lat"), h + 1)
                act.activation(OT[:, h, N_CTX:N_ALL], PS[:, 6, :], ACT.Copy).then_inc(S("ot_lat"), 1)
                act.wait_ge(S("pv_ctx"), h + 1)
                act.activation(OT[:, h, 0:N_CTX], PS[:, 7, 0:N_CTX], ACT.Copy).then_inc(S("ot_ctx"), 1)
            for t in range(AT):
                act.wait_ge(S("o_mm"), t + 1)
                A(act.activation(junk[:, :], bank2(2 * (t % 2)), ACT.Square, accum_out=ss[:, 2 + t:3 + t]))
                act.activation(sd[:, 8 + t:9 + t], ss[:, 2 + t:3 + t], ACT.Sqrt, scale=1.0 / D, bias=eps[:, 0:1]).then_inc(S("o_sd"), 1)
            moe_act(act, A, 0)
            s5_act(act, A)
            moe_act(act, A, 1)

        def moe_dve(v, W, modulated, l):
            tiles, NT = TILES[l], len(TILES[l])
            g, Z = "m_", before_moe(l)
            v.wait_ge(S(g + "sd"), Z("sd") + 1)
            W(v.reciprocal(rs[:, 0:NT], sd[:, 0:NT]))
            v.wait_ge(S("rows_m") if l == 0 else S("s_rown"), 64 if l == 0 else B("s_rown") + 32)

            def h_free(n):
                v.wait_ge(S(g + "ht_tp"), Z("ht_tp") + n - 1)
                v.wait_ge(S(g + f"f_out{n % 2}"), Z(f"f_out{n % 2}") + n // 2 * 16)

            for n, t in enumerate(tiles):
                modulated(n, t, stream[t] if l == 0 else 0, h_free, S(g + "h_ready"))
            v.wait_ge(S(g + "h_ready"), Z("h_ready") + NT)
            W(v.memset(row(0), 0.0))
            v.sem_inc(S(g + "zero_ready"), 1)
            v.memset(GS[:, :, 8:16], BIG)
            v.memset(TR[:, :, 4:8], BIG)
            v.memset(POSM[:, :, N_EXP:EPAD], -1.0)
            v.memset(RH[:, :, N_EXP:EPAD, :], 0.0)
            v.memset(RH[:, :, 0:N_EXP, 0:1], 1.0)
            for n in range(NT):
                v.memset(RH[:, n, 0:N_EXP, 2:3], float(n))
            v.tensor_copy(RH[:, 0:NT, 0:N_EXP, 1:2], cst[:, 0:1].unsqueeze(2).unsqueeze(3).to_broadcast((P, NT, N_EXP, 1)))
            v.wait_ge(S(g + "scores"), Z("scores") + 1)
            N = slice(0, NT)
            W(v.tensor_tensor(BI[:, N], SC[:, N], BROW[:, :].unsqueeze(1).to_broadcast((P, NT, N_EXP)), ALU.add))
            for n in range(NT):
                for q in range(8):
                    ins = v.max(M8[:, n, q, :], BI[:, n, q * 8:(q + 1) * 8])
            W(ins)
            W(v.tensor_tensor(GS[:, N, 0:8], M8[:, N, :, 0], M8[:, N, :, 1], ALU.add))
            for n in range(NT):
                ins = v.max(G8[:, n, :], GS[:, n, 0:8])
            W(ins)
            W(v.tensor_copy(TR[:, N, 0:4], G8[:, N, 0:4]))
            for n in range(NT):
                ins = v.match_replace(GR[:, n, :], TR[:, n, :], GS[:, n, :], -BIG)
            W(ins)
            W(v.tensor_scalar(GM[:, N], GR[:, N, 0:8], -BIG, None, ALU.is_equal))
            W(v.tensor_scalar(TB[:, N], GM[:, N], BIG, -BIG, ALU.mult, ALU.add))
            for n in range(NT):
                b3 = BI[:, n, :].rearrange("p (q k) -> p q k", q=8)
                ins = v.tensor_tensor(b3, b3, GM[:, n, :].unsqueeze(2).to_broadcast((P, 8, 8)), ALU.mult)
            W(ins)
            for n in range(NT):
                b3 = BI[:, n, :].rearrange("p (q k) -> p q k", q=8)
                ins = v.tensor_tensor(b3, b3, TB[:, n, :].unsqueeze(2).to_broadcast((P, 8, 8)), ALU.add)
            W(ins)
            for n in range(NT):
                ins = v.max(E8[:, n, :], BI[:, n, :])
            W(ins)
            for n in range(NT):
                ins = v.match_replace(MR[:, n, :], E8[:, n, :], BI[:, n, :], -2 * BIG)
            W(ins)
            W(v.tensor_scalar(MR[:, N], MR[:, N], -2 * BIG, None, ALU.is_equal))
            W(v.tensor_copy(MB16[:, N], MR[:, N]))
            v.sem_inc(S(g + "mask_ready"), 1)
            W(v.tensor_tensor(GTE[:, N], SC[:, N], MR[:, N], ALU.mult))
            W(v.tensor_reduce(sm[:, 0:NT], GTE[:, N], AX_X, ALU.add))
            W(v.reciprocal(sm[:, 0:NT], sm[:, 0:NT]))
            W(v.tensor_tensor(GTE[:, N], GTE[:, N], sm[:, 0:NT].unsqueeze(2).to_broadcast((P, NT, N_EXP)), ALU.mult))
            W(v.tensor_scalar(GTE[:, N], GTE[:, N], ROUTED, None, ALU.mult))
            for c in (3, 4, 5):
                W(v.tensor_copy(RH[:, N, 0:N_EXP, c], GTE[:, N]))
                if c < 5:
                    W(v.tensor_tensor(GTE[:, N], GTE[:, N], RH[:, N, 0:N_EXP, c], ALU.subtract))
            for n in range(NT):
                v.wait_ge(S(g + "sh_silu"), Z("sh_silu") + n + 1)
                if n >= 2:
                    v.wait_ge(S(g + "sh_tp"), Z("sh_tp") + n - 1)
                v.tensor_tensor(HH[n % 2], SG[n % 2], PS[:, 4 + n % 2, FE:2 * FE], ALU.mult).then_inc(S(g + "sh_h"), 1)
                v.wait_ge(S(g + "sh_tp"), Z("sh_tp") + n + 1)
                if n >= 2:
                    v.wait_ge(S(g + "sh_down"), Z("sh_down") + n - 1)
                v.tensor_copy(HHT[n % 2], PS[:, 6, 0:FE].rearrange("p (j n) -> p j n", j=FC)).then_inc(S(g + "sh_ht"), 1)
                v.wait_ge(S(g + "sh_down"), Z("sh_down") + n + 1)
                if n == 0:
                    for k in range(2):
                        v.wait_ge(S(g + f"f_out{k}"), Z(f"f_out{k}") + NT // 2 * 16)
                if n >= 2:
                    v.wait_ge(S(g + f"acc_out{n % 2}"), Z(f"acc_out{n % 2}") + n // 2 * 16)
                v.tensor_copy(H[n % 2][:, 512:1024], PS[:, 2 * (n % 2) + 1, :]).then_inc(S(g + "so_ready_v"), 1)

            v.wait_ge(S(g + "pos_mm"), Z("pos_mm") + 1)
            pos = PS[:, 7, 0:NT * 64].rearrange("p (t e) -> p t e", t=NT)
            W(v.scalar_tensor_tensor(POSM[:, N, 0:N_EXP], pos, 1.0, MR[:, N], ALU.add, ALU.mult))
            W(v.tensor_scalar(POSM[:, N, 0:N_EXP], POSM[:, N, 0:N_EXP], -1.0, None, ALU.add))
            W(v.tensor_copy(CNT[0:1, :], PS[0:1, 7, 384:448]))
            W(v.tensor_scalar(NB[0:1, :], CNT[0:1, :], float(P), None, ALU.is_gt))
            for b in range(2, NT):
                W(v.scalar_tensor_tensor(NB[0:1, :], CNT[0:1, :], float(P * b), NB[0:1, :], ALU.is_gt, ALU.add))
            W(v.tensor_tensor_scan(CNT[0:1, :], cst[0:1, 72:73].to_broadcast((1, N_EXP)), NB[0:1, :], 0.0, ALU.mult, ALU.add))
            W(v.tensor_tensor(CNT[0:1, :], CNT[0:1, :], NB[0:1, :], ALU.subtract))
            W(v.tensor_copy(befores[0:1, :], CNT[0:1, :]))
            W(v.tensor_tensor(NB[0:1, :], NB[0:1, :], cst[0:1, 8:72], ALU.mult))
            W(v.tensor_reduce(CNT[0:1, 0:16], NB[0:1, :].rearrange("p (a b) -> p a b", b=NSLOT), AX_X, ALU.add))
            W(v.tensor_copy(words[0:1, :], CNT[0:1, 0:16]))
            v.sem_inc(S(g + "words_ready"), 1)
            trash = 2 + l

            def slots(u, done, W):
                W(v.tensor_copy(it[:, 0:6], PS[:, 7, 0:6]))
                W(v.scalar_tensor_tensor(it[:, 6:7], it[:, 2:3], float(P), it[:, 1:2], ALU.mult, ALU.add))
                W(v.scalar_tensor_tensor(it[:, 6:7], it[:, 0:1], cst[:, trash + 2:trash + 3], it[:, 6:7], ALU.mult, ALU.add))
                v.tensor_tensor(it[:, 7:8], it[:, 4:5], it[:, 5:6], ALU.add)
                W(v.tensor_scalar(idxu[:, u:u + 1], it[:, 6:7], cst[:, trash:trash + 1], None, ALU.add))
                v.tensor_tensor(gate[:, u:u + 1], it[:, 7:8], it[:, 3:4], ALU.add).then_inc(done, 1)

            def one_hot(k, col, done):
                for n in range(NT):
                    ins = v.tensor_scalar(OH[k][:, n, :], iota_b[:, :], col(n), None, ALU.is_equal)
                ins.then_inc(done, 1)

            for e in range(2):
                one_hot(e, lambda n: POSM[:, n, e:e + 1], S(g + "oh_ready"))
                v.wait_ge(S(g + "idx_mm"), Z("idx_mm") + e + 1)
                slots(e, S(g + "idx_ready"), W)
            with v.Fori(0, N_EXP // NSLOT) as eb:
                word = v.value_load(words[0:1, bass.ds(eb, 1)], min_val=0, max_val=8 ** NSLOT - 1)
                W.enter(eb, NSLOT * 4)
                for u in range(NSLOT):
                    e = eb * NSLOT + u
                    v.wait_ge(S(g + "idx_mm"), Z("idx_mm") + e + 1)
                    e2 = v.snap(e + 2, min_val=0, max_val=EPAD - 1)
                    one_hot(u % 2, lambda n: POSM[:, n, bass.ds(e2, 1)], S(g + "oh_ready"))
                    v.wait_ge(S(g + "silu"), Z("silu") + e + 1)
                    v.tensor_tensor(HH[u % 2], SG[u % 2], PS[:, 2 + u % 2, FE:2 * FE], ALU.mult).then_inc(S(g + "h_ready2"), 1)
                    v.wait_ge(S(g + "idx_mm"), Z("idx_mm") + e + 3)
                    v.wait_ge(S(g + "os_free"), Z("os_free") + e + 1)
                    slots((u + 2) % NSLOT, S(g + "idx_ready"), W)
                    v.wait_ge(S(g + "h_tp"), Z("h_tp") + e + 1)
                    v.tensor_copy(HHT[u % 2], PS[:, 6, 0:FE].rearrange("p (j n) -> p j n", j=FC)).then_inc(S(g + "hht_ready"), 1)
                    v.wait_ge(S(g + "dn_mm"), Z("dn_mm") + e + 1)
                    v.wait_ge(S(g + "os_free"), Z("os_free") + e + 1)
                    v.tensor_scalar(OS[u % 2][:, 512:1024], PS[:, 5, :], gate[:, u:u + 1], None, ALU.mult).then_inc(S(g + "out_v"), 1)
                    extra = v.snap((word >> (3 * u)) & 7, min_val=0, max_val=7)
                    with v.If(extra > 0):
                        with v.Fori(1, NT) as b:
                            m = e * (NT - 1) + b
                            with v.If(extra > b - 1):
                                e1 = v.snap(e, min_val=0, max_val=EPAD - 1)
                                v.tensor_scalar(POSM[:, 0:NT, bass.ds(e1, 1)].rearrange("p t a -> p (t a)"),
                                                POSM[:, 0:NT, bass.ds(e1, 1)].rearrange("p t a -> p (t a)"),
                                                -float(P), None, ALU.add).then_inc(S(g + "o_pos"), 1)
                                v.wait_ge(S(g + "o_pos"), Z("o_pos") + m)
                                v.wait_ge(S(g + "idx_mm"), Z("idx_mm") + e + 3)
                                one_hot(u % 2, lambda n: POSM[:, n, bass.ds(e1, 1)], S(g + "o_oh"))
                                v.wait_ge(S(g + "o_idx_mm"), Z("o_idx_mm") + m)
                                OW = Steps(v, S(g + "o_step"))
                                OW.off = Z("o_step") + (m - 1) * 4
                                slots(4, S(g + "o_idx"), OW)
                                v.wait_ge(S(g + "o_silu"), Z("o_silu") + m)
                                v.tensor_tensor(HH[u % 2], SG[u % 2], PS[:, 2 + u % 2, FE:2 * FE], ALU.mult).then_inc(S(g + "o_h"), 1)
                                v.wait_ge(S(g + "o_htp"), Z("o_htp") + m)
                                v.tensor_copy(HHT[u % 2], PS[:, 6, 0:FE].rearrange("p (j n) -> p j n", j=FC)).then_inc(S(g + "o_hht"), 1)
                                v.wait_ge(S(g + "o_dn"), Z("o_dn") + m)
                                v.wait_ge(S(g + "o_os_free"), Z("o_os_free") + m)
                                v.tensor_scalar(OS[u % 2][:, 512:1024], PS[:, 5, :], gate[:, 4:5], None, ALU.mult).then_inc(S(g + "o_out_v"), 1)
                                mm = v.snap(m, min_val=1, max_val=N_EXP * (NT - 1))
                                v.wait_ge(S(g + "words_ready"), Z("words_ready") + 1)
                                v.wait_ge(S(g + "o_scat"), Z("o_scat") + mm)
                            with v.Else():
                                for q in ("o_pos", "o_oh", "o_idx", "o_h", "o_hht", "o_out_v"):
                                    v.sem_inc(S(g + q), 1)
                                v.sem_inc(S(g + "o_step"), 4)
                    with v.Else():
                        for q in ("o_pos", "o_oh", "o_idx", "o_h", "o_hht", "o_out_v"):
                            v.sem_inc(S(g + q), NT - 1)
                        v.sem_inc(S(g + "o_step"), 4 * (NT - 1))
                W.leave(N_EXP // NSLOT)
            v.wait_ge(S(g + "rows_in"), Z("rows_in") + 32 if l == 0 else 16)
            for n, t in enumerate(tiles):
                v.wait_ge(S(g + "o_sd"), Z("o_sd") + n + 1)
                W(v.reciprocal(rs[:, n:n + 1], sd[:, n:n + 1]))
                W(v.scalar_tensor_tensor(OS[n % 2], OS[n % 2], rs[:, n:n + 1], row(stream[t] if l == 0 else 0), ALU.mult, ALU.mult))
                v.tensor_tensor(X[:, t, :], X[:, t, :], OS[n % 2], ALU.add).then_inc(S(g + "x_ready"), 1)


        def s5_dve(v, W, modulated):
            v.wait_ge(S("s_sd"), B("s_sd") + 1)
            W(v.reciprocal(rs[:, 0:AT], sd[:, 0:AT]))
            v.wait_ge(S("s_rows"), B("s_rows") + 64)
            for t in range(AT):
                modulated(t, t, stream[t], lambda n: v.wait_ge(S(f"s_h_out{n % 2}"), B(f"s_h_out{n % 2}") + n // 2 * 16), S("s_h_ready"))
            v.wait_ge(S("s_tab_a"), B("s_tab_a") + 1)
            v.tensor_tensor(tA, LRE, tEA, ALU.mult)
            W(v.tensor_tensor(tTH, LIM, tEA, ALU.mult))
            W(v.tensor_scalar(tK, tTH, 1.0 / TWO_PI, ROUND, ALU.mult, ALU.add))
            W(v.tensor_scalar(tK, tK, -ROUND, None, ALU.add))
            W(v.scalar_tensor_tensor(tR, tK, -PI_A, tTH, ALU.mult, ALU.add))
            W(v.scalar_tensor_tensor(tR, tK, -PI_B, tR, ALU.mult, ALU.add))
            W(v.scalar_tensor_tensor(tR, tK, -PI_C, tR, ALU.mult, ALU.add))
            W(v.tensor_scalar(tR2, tR, 0.5 * np.pi, None, ALU.add))
            W(v.tensor_scalar(tM, tR2, float(np.pi), -TWO_PI, ALU.is_gt, ALU.mult))
            W(v.tensor_tensor(tR2, tR2, tM, ALU.add))
            v.tensor_scalar(tR, tR, 3.1415925, -3.1415925, ALU.min, ALU.max)
            W(v.tensor_scalar(tR2, tR2, 3.1415925, -3.1415925, ALU.min, ALU.max))
            v.sem_inc(S("s_tab_v"), 1)
            v.memset(NR[:, 0, :], 1.0)
            v.memset(NI[:, 0, :], 0.0)
            v.wait_ge(S("s_tab_a"), B("s_tab_a") + 4)
            v.tensor_tensor(NR[:, 1, :], tEA, tR2, ALU.mult)
            W(v.tensor_tensor(NI[:, 1, :], tEA, tR, ALU.mult))

            def cmul(dr, di, ar, ai, br, bi, t1, t2):
                v.tensor_tensor(dr, ar, br, ALU.mult)
                v.tensor_tensor(t1, ai, bi, ALU.mult)
                v.tensor_tensor(di, ar, bi, ALU.mult)
                W(v.tensor_tensor(t2, ai, br, ALU.mult))
                v.tensor_tensor(dr, dr, t1, ALU.subtract)
                W(v.tensor_tensor(di, di, t2, ALU.add))

            for k in range(2, L + 1):
                cmul(NR[:, k, :], NI[:, k, :], NR[:, k - 1, :], NI[:, k - 1, :], NR[:, 1, :], NI[:, 1, :], tM, tN)
            v.tensor_scalar(tK, NR[:, 1, :], -1.0, None, ALU.add)
            v.tensor_tensor(tR, LRE, LRE, ALU.mult)
            W(v.tensor_tensor(tR2, LIM, LIM, ALU.mult))
            W(v.tensor_tensor(tR, tR, tR2, ALU.add))
            W(v.reciprocal(tR, tR))
            v.tensor_tensor(tFR, tK, LRE, ALU.mult)
            v.tensor_tensor(tM, NI[:, 1, :], LIM, ALU.mult)
            v.tensor_tensor(tFI, NI[:, 1, :], LRE, ALU.mult)
            W(v.tensor_tensor(tN, tK, LIM, ALU.mult))
            v.tensor_tensor(tFR, tFR, tM, ALU.add)
            W(v.tensor_tensor(tFI, tFI, tN, ALU.subtract))
            v.tensor_tensor(tFR, tFR, tR, ALU.mult)
            W(v.tensor_tensor(tFI, tFI, tR, ALU.mult))
            n8 = slice(0, L)
            tm = TMP[:, 0:1024].rearrange("p (j q) -> p j q", q=Q)

            def wide(t):
                return t.unsqueeze(1).to_broadcast((P, L, Q))

            v.tensor_tensor(GR_, NR[:, n8], wide(tFR), ALU.mult)
            v.tensor_tensor(GI_, NR[:, n8], wide(tFI), ALU.mult)
            W(v.tensor_tensor(tm, NI[:, n8], wide(tFI), ALU.mult))
            W(v.tensor_tensor(GR_, GR_, tm, ALU.subtract))
            W(v.tensor_tensor(tm, NI[:, n8], wide(tFR), ALU.mult))
            W(v.tensor_tensor(GI_, GI_, tm, ALU.add))
            mt, mb, nmt, nmb = (cst[:, k:k + 1] for k in (6, 7, 73, 74))

            def halves(dst, a, a_scale, b, b_scale):
                W(v.tensor_scalar(dst, a, a_scale, None, ALU.mult))
                W(v.scalar_tensor_tensor(dst, b, b_scale, dst, ALU.mult, ALU.add))

            f, b = slice(0, GROUPS), slice(GROUPS, Q)
            for d, q, step in ((X1, f, 1), (X1, b, -1)):
                halves(X1[:, :, q], NR[:, ::step, q], mt, NI[:, ::step, q], nmb)
                halves(X2[:, :, q], NI[:, ::step, q], nmt, NR[:, ::step, q], nmb)
                halves(Y1[:, :, q], GR_[:, ::-step, q], mt, GI_[:, ::-step, q], mb)
                halves(Y2[:, :, q], GI_[:, ::-step, q], nmt, GR_[:, ::-step, q], mb)
            halves(F1, tFR, mt, tFI, mb)
            halves(F2, tFI, nmt, tFR, mb)
            halves(tSMI, NI[:, L, :], mt, NI[:, L, :], nmb)
            v.sem_inc(S("s_tab_ready"), 1)

            def scaled_sum(dst, tmp, a0, a1, b0, b1):
                v.tensor_tensor(dst, a0, a1, ALU.mult)
                W(v.tensor_tensor(tmp, b0, b1, ALU.mult))
                return v.tensor_tensor(dst, dst, tmp, ALU.add)

            for n in range(Q // QB):
                v.wait_ge(S(f"s_b_in{n % 2}"), B(f"s_b_in{n % 2}") + 16 * (n // 2 + 1))
                if n:
                    v.wait_ge(S("s_w_tp"), B("s_w_tp") + 2 * n)
                q = slice(n * QB, (n + 1) * QB)
                shape = (P, QB, L, GI)
                w4 = WW.rearrange("p (q s i) -> p q s i", q=QB, s=L)
                t4 = TMP[:, 0:1024].rearrange("p (q s i) -> p q s i", q=QB, s=L)
                y1, y2 = (y[:, :, q].rearrange("p s q -> p q s").unsqueeze(3).to_broadcast(shape) for y in (Y1, Y2))
                br, bi = (BB[n % 2][:, c].unsqueeze(2).to_broadcast(shape) for c in range(2))
                scaled_sum(w4, t4, br, y1, bi, y2).then_inc(S("s_w_ready"), 1)
                v.wait_ge(S("s_w_ready"), B("s_w_ready") + n + 1)
            v.wait_ge(S("s_v_ready"), B("s_v_ready") + Q // 4)
            fwd_turn = scan_turn(v, W, 0)
            with v.Fori(LC + 2, NCH + 1) as i:
                W.enter(i - (LC + 2), 4)
                fwd_turn(i, -1)
                W.leave(NCH - LC - 1)
            W(v.tensor_copy(VST[:, 0, 0:GROUPS], VST[:, NCH, 0:GROUPS]))
            with v.Fori(1, LC + 1) as i:
                W.enter(i - 1, 4)
                fwd_turn(i, -1)
                W.leave(LC)
            v.sem_inc(S("s_fwd_done"), 1)
            v.wait_ge(S("s_d_in"), B("s_d_in") + 16)
            W(v.tensor_tensor(HC[0:LC], HC[0:LC], DROW[0:LC].unsqueeze(1).to_broadcast((LC, L, D)), ALU.mult))
            v.sem_inc(S("s_hd"), 1)

            def y_add(n):
                v.wait_ge(S("s_y_mm"), B("s_y_mm") + n + 1)
                for k in range(2):
                    c = slice((n * QB + 4 * k) * GI, (n * QB + 4 * k + 4) * GI)
                    y = HC[0:LC, :, c].rearrange("p t (g i) -> p g t i", g=4)
                    ins = v.tensor_tensor(y, PS[0:LC, 4 + 2 * (n % 2) + k, :].rearrange("p (g t i) -> p g t i", g=4, t=L), y, ALU.add)
                ins.then_inc(S("s_y_ready"), 1)

            for n in range(GROUPS // QB):
                v.wait_ge(S("s_c_in"), B("s_c_in") + 64 * (n + 1))
                if n:
                    v.wait_ge(S("s_y_mm"), B("s_y_mm") + n)
                for d in range(2):
                    q = slice(d * GROUPS + n * QB, d * GROUPS + (n + 1) * QB)
                    shape = (P, QB, L + 1, GI)
                    t4 = TMP.rearrange("p (q s i) -> p q s i", q=QB, s=L + 1)
                    x1, x2 = (x[:, :, q].rearrange("p s q -> p q s").unsqueeze(3).to_broadcast(shape) for x in (X1, X2))
                    cr, ci = (CB[:, d, c].unsqueeze(2).to_broadcast(shape) for c in range(2))
                    W(scaled_sum(CC[:, d], t4, cr, x1, ci, x2))
                    shape = (P, QB, GI)
                    f1, f2 = (x[:, q].unsqueeze(2).to_broadcast(shape) for x in (F1, F2))
                    W(scaled_sum(BB2[:, d], TMP[:, 0:QB * GI].rearrange("p (q i) -> p q i", q=QB), BD[:, d, 0], f1, BD[:, d, 1], f2))
                v.sem_inc(S("s_cc_ready"), 1)
                if n:
                    y_add(n - 1)
            y_add(GROUPS // QB - 1)
            for t in range(L):
                v.wait_ge(S("s_yt_tp"), B("s_yt_tp") + t + 1)
                v.tensor_copy(YT[:, :, t * LC:(t + 1) * LC], PS[:, t % 4, :].rearrange("p (j c) -> p j c", j=DC)).then_inc(S("s_yt"), 1)
            v.wait_ge(S("s_bg_in"), B("s_bg_in") + 16)
            for n in range(2 * LT + 1):
                if n < 2 * LT:
                    h, b = n // LT, 4 + 2 * (n % 2)
                    v.wait_ge(S("s_glu_mm"), B("s_glu_mm") + n + 1)
                    if n >= 2:
                        v.wait_ge(S("s_oo"), B("s_oo") + n - 1)
                    v.tensor_tensor(ZT[n % 2][:, 0:512], PS[:, b, :], BG[:, h * 512:(h + 1) * 512], ALU.add)
                    v.tensor_tensor(ZT[n % 2][:, 512:1024], PS[:, b + 1, :], BG[:, D + h * 512:D + (h + 1) * 512], ALU.add).then_inc(S("s_z"), 1)
                if n:
                    a = n - 1
                    h, m = a // LT, a % LT
                    v.wait_ge(S("s_sig"), B("s_sig") + n)
                    v.tensor_tensor(OO[:, m, h * 512:(h + 1) * 512], ZT[a % 2][:, 0:512], ZT[a % 2][:, 512:1024], ALU.mult).then_inc(S("s_oo"), 1)
            v.wait_ge(S("s_rowg"), B("s_rowg") + 16)
            v.wait_ge(S("s_xr_in"), B("s_xr_in") + 16 * L)
            for m in range(LT):
                v.wait_ge(S("s_osd"), B("s_osd") + m + 1)
                W(v.reciprocal(rs[:, 8 + m:9 + m], sd[:, 8 + m:9 + m]))
                W(v.scalar_tensor_tensor(OO[:, m, :], OO[:, m, :], rs[:, 8 + m:9 + m], row(0), ALU.mult, ALU.mult))
                v.tensor_tensor(X[:, m, :], X[:, m, :], OO[:, m, :], ALU.add).then_inc(S("x3_ready"), 1)

        @block.vector
        def _(v):
            W = Steps(v, S("dve_step"))
            v.wait_ge(S("const_in"), 5 * 16)
            v.wait_ge(S("tri_in"), 32)
            v.tensor_copy(tri[:, :], work(0, P))
            v.tensor_copy(iota_b[:, :], work(P, P))
            v.memset(ones_b[:, :], 1.0)
            W(v.memset(eps[:, :], EPS))
            v.sem_inc(S("eps_ready"), 1)
            for l in range(2):
                v.wait_ge(S("modb_in"), 32 * (l + 1))
                if l:
                    v.wait_ge(S("mod_free"), 1)
                for m in range(ADA_T):
                    n = l * ADA_T + m
                    v.wait_ge(S("ada_mm"), n + 1)
                    c = slice(m * 512, (m + 1) * 512)
                    v.tensor_tensor(MOD[:, c], PS[0:2, n % 4, :], MODB[:, c], ALU.add).then_inc(S("ada_ev"), 1)
                v.wait_ge(S("ada_ev"), ADA_T * (l + 1))
                for q in (1, 4):
                    c = slice(q * D, (q + 1) * D)
                    k = 0 if q == 1 else 2
                    v.scalar_tensor_tensor(MOD[:, c], MOD[:, c], 1.0, NG[:, k * D:(k + 1) * D], ALU.add, ALU.mult)
                for q in (2, 5):
                    c = slice(q * D, (q + 1) * D)
                    k = 1 if q == 2 else 3
                    ins = v.tensor_tensor(MOD[:, c], MOD[:, c], NG[:, k * D:(k + 1) * D], ALU.mult)
                W(ins)
                v.sem_inc(S("mod_ready"), 1)
            v.wait_ge(S("a_sd"), 1)
            W(v.reciprocal(rs[:, 0:AT], sd[:, 0:AT]))
            v.wait_ge(S("rows_a"), 64)
            v.wait_ge(S("mod_out"), 32)

            def modulated(n, t, lat_ctx, free, ready):
                k = 2 * lat_ctx
                if n >= 2:
                    free(n)
                W(v.scalar_tensor_tensor(H[n % 2], X[:, t, :], rs[:, n:n + 1], row(k), ALU.mult, ALU.mult))
                v.tensor_tensor(H[n % 2], H[n % 2], row(k + 1), ALU.add).then_inc(ready, 1)

            for t in range(AT + 2):
                if t < AT:
                    modulated(t, t, stream[t], lambda n: v.wait_ge(S("a_tp"), n - 1), S("a_h_ready"))
                if t >= 2:
                    a = t - 2
                    ps = bank2(4 + 2 * (a % 2))
                    v.wait_ge(S("c_sd"), a + 1)
                    W(v.reciprocal(rs[:, 6:8], sd[:, 6:8]))
                    if a:
                        v.wait_ge(S("ct_tp"), a)
                    v.tensor_scalar(CA[:, 0:QL], ps[:, 0:QL], rs[:, 6:7], None, ALU.mult)
                    v.tensor_scalar(CA[:, QL:QL + KVL], ps[:, QL:QL + KVL], rs[:, 7:8], None, ALU.mult)
                    v.tensor_copy(CA[:, QL + KVL:AW], ps[:, QL + KVL:AW]).then_inc(S("ca_ready"), 1)
                    v.wait_ge(S("ct_tp"), a + 1)
                    c = slice(a * P, (a + 1) * P)
                    ct = bank2(2)
                    for j in range(QC):
                        v.tensor_scalar(CQT[:, j, c], ct[:, j * P:(j + 1) * P], gcol[:, j:j + 1], None, ALU.mult)
                    for j in range(KC):
                        v.tensor_scalar(CKT[:, j, c], ct[:, (QC + j) * P:(QC + j + 1) * P], gcol[:, QC + j:QC + j + 1], None, ALU.mult)
                    v.tensor_copy(KPT[:, c], ct[0:ROPE, (QC + KC) * P:(QC + KC + 1) * P]).then_inc(S("ct_ready"), 1)
            for n in range(1, 2 * AT, 2):
                v.wait_ge(S("v_mm"), n + 1)
                v.tensor_copy(V[:, n // 2, 512:1024], PS[:, 4 + n % 4, :]).then_inc(S("v_ready_v"), 1)

            def rope(dst, src, ps, done):
                v.tensor_tensor(dst, src, cosT, ALU.mult)
                W(v.tensor_tensor(ps, ps, sinT, ALU.mult))
                v.tensor_tensor(dst, dst, ps, ALU.add).then_inc(done, 1)

            v.wait_ge(S("rope_in"), 32)
            v.wait_ge(S("k_rot"), 1)
            rope(KPR, KPT, bank2(6, N_ALL)[0:ROPE], S("k_rope"))
            for h in range(HEADS):
                v.wait_ge(S("kn_mm"), h + 1)
                v.tensor_copy(knT, bank2(2, N_ALL)).then_inc(S("kn_ready"), 1)
                v.wait_ge(S("q_rot"), h + 1)
                if h:
                    v.wait_ge(S("s_mm"), h * AT)
                rope(qpR, qpT, bank2(6, N_ALL)[0:ROPE], S("q_rope"))
                for t in range(AT + 1):
                    if t < AT:
                        k = h * AT + t
                        nk = N_ALL if t < LT else N_CTX
                        v.wait_ge(S("s_mm"), k + 1)
                        if k >= 2:
                            v.wait_ge(S("p_exp"), k - 1)
                        W(v.reduce_max(mx[:, t % 2:t % 2 + 1], bank2(2 * (t % 2), nk), AX_X))
                        v.tensor_scalar(mx[:, t % 2:t % 2 + 1], mx[:, t % 2:t % 2 + 1], -SCALE, None, ALU.mult).then_inc(S("nmax"), 1)
                    if t:
                        k = h * AT + t - 1
                        c = (t - 1) % 2
                        nk = N_ALL if t - 1 < LT else N_CTX
                        v.wait_ge(S("p_exp"), k + 1)
                        W(v.reciprocal(sm[:, 2 + c:3 + c], sm[:, c:c + 1]))
                        v.tensor_scalar(PR[c][:, 0:nk], PR[c][:, 0:nk], sm[:, 2 + c:3 + c], None, ALU.mult).then_inc(S("p_ready"), 1)
            v.wait_ge(S("rows_g"), 32)
            for t in range(AT):
                v.wait_ge(S("o_sd"), t + 1)
                W(v.reciprocal(rs[:, 8 + t:9 + t], sd[:, 8 + t:9 + t]))
                W(v.scalar_tensor_tensor(H[t % 2], bank2(2 * (t % 2)), rs[:, 8 + t:9 + t], row(stream[t]), ALU.mult, ALU.mult))
                v.sem_inc(S("o_used"), 1)
                v.tensor_tensor(X[:, t, :], X[:, t, :], H[t % 2], ALU.add).then_inc(S("x1_ready"), 1)
            moe_dve(v, W, modulated, 0)
            s5_dve(v, W, modulated)
            moe_dve(v, W, modulated, 1)

        def moe_pool(pool, l):
            NT = len(TILES[l])
            g, Z = "m_", before_moe(l)

            def gather(dst, u, done):
                pool.sem_inc(S("pool_starts"), 1)
                pool.indirect_dma_start(out=dst, out_offset=None, in_=f_d[l][:, :],
                                        in_offset=bass.IndirectOffsetOnAxis(ap=idxu[:, u:u + 1], axis=0)).then_inc(done, 16)

            def scatter(src, u, done):
                pool.sem_inc(S("pool_starts"), 1)
                pool.indirect_dma_start(out=acc_d[l][:, :], out_offset=bass.IndirectOffsetOnAxis(ap=idxu[:, u:u + 1], axis=0),
                                        in_=src, in_offset=None, compute_op=ALU.add).then_inc(done, 16)

            for k in range(2):
                pool.wait_ge(S(g + f"f_out{k}"), Z(f"f_out{k}") + NT // 2 * 16)
            pool.wait_ge(S(g + "f_trash"), Z("f_trash") + 16)
            pool.wait_ge(S(g + "sh_down"), Z("sh_down") + NT)
            for e in range(2):
                pool.wait_ge(S(g + "idx_ready"), Z("idx_ready") + e + 1)
                gather(XG[e], e, S(g + f"xg_in{e}"))
            for k in range(2):
                pool.wait_ge(S(g + f"acc_out{k}"), Z(f"acc_out{k}") + NT // 2 * 16)
            pool.wait_ge(S(g + "acc_out2"), Z("acc_out2") + 16)
            pool.wait_ge(S(g + "words_ready"), Z("words_ready") + 1)
            with pool.Fori(0, N_EXP // NSLOT) as eb:
                word = pool.value_load(words[0:1, bass.ds(eb, 1)], min_val=0, max_val=8 ** NSLOT - 1)
                for u in range(NSLOT):
                    e = eb * NSLOT + u
                    pool.wait_ge(S(g + f"scat{u % 2}"), Z(f"scat{u % 2}") + (eb * 2 + u // 2) * 16)
                    pool.sem_inc(S(g + "os_free"), 1)
                    e1 = pool.snap(e + 1, min_val=1, max_val=N_EXP)
                    pool.wait_ge(S(g + "idx_ready"), Z("idx_ready") + e + 3)
                    pool.wait_ge(S(g + "xt_tp"), Z("xt_tp") + e1)
                    gather(XG[u % 2], (u + 2) % NSLOT, S(g + f"xg_in{u % 2}"))
                    pool.wait_ge(S(g + f"scat{(u + 1) % 2}"), Z(f"scat{(u + 1) % 2}") + (eb * 2 + (u + 1) // 2) * 16)
                    pool.wait_ge(S(g + "out_a"), Z("out_a") + e1)
                    pool.wait_ge(S(g + "out_v"), Z("out_v") + e1)
                    scatter(OS[u % 2], u, S(g + f"scat{u % 2}"))
                    extra = pool.snap((word >> (3 * u)) & 7, min_val=0, max_val=7)
                    with pool.If(extra > 0):
                        before = pool.value_load(befores[0:1, bass.ds(e, 1)], min_val=0, max_val=N_EXP * (NT - 1))
                        with pool.Fori(1, NT) as b:
                            m = e * (NT - 1) + b
                            with pool.If(extra > b - 1):
                                pool.wait_ge(S(g + f"scat{u % 2}"), Z(f"scat{u % 2}") + (eb * 2 + u // 2) * 16 + 16)
                                pool.sem_inc(S(g + "o_os_free"), 1)
                                mm = pool.snap(m, min_val=1, max_val=N_EXP * (NT - 1))
                                pool.wait_ge(S(g + "o_idx"), Z("o_idx") + mm)
                                gather(XGo, 4, S(f"o_dma{l}"))
                                pool.wait_ge(S(f"o_dma{l}"), (before + b) * 32 - 16)
                                pool.sem_inc(S(g + "o_xg"), 1)
                                pool.wait_ge(S(g + "o_out_a"), Z("o_out_a") + m)
                                pool.wait_ge(S(g + "o_out_v"), Z("o_out_v") + mm)
                                scatter(OS[u % 2], 4, S(f"o_dma{l}"))
                                pool.wait_ge(S(f"o_dma{l}"), (before + b) * 32)
                                pool.sem_inc(S(g + "o_scat"), 1)
                            with pool.Else():
                                pool.sem_inc(S(g + "o_os_free"), 1)
                                pool.sem_inc(S(g + "o_xg"), 1)
                                pool.sem_inc(S(g + "o_scat"), 1)
                    with pool.Else():
                        pool.sem_inc(S(g + "o_os_free"), NT - 1)
                        pool.sem_inc(S(g + "o_xg"), NT - 1)
                        pool.sem_inc(S(g + "o_scat"), NT - 1)
            for k in range(2):
                pool.wait_ge(S(g + f"scat{k}"), Z(f"scat{k}") + N_EXP // 2 * 16)
            for k in range(2):
                pool.wait_ge(S(g + f"xg_in{k}"), Z(f"xg_in{k}") + (N_EXP // 2 + 1) * 16)
            pool.sem_inc(S(g + "all_scattered"), 1)


        def s5_pool(pool):
            G = Steps(pool, S("pool_step"))
            pool.wait_ge(S("s_hc_in"), B("s_hc_in") + 32)
            for n in range(GROUPS // 4):
                if n >= 2:
                    pool.wait_ge(S("s_u_tp"), B("s_u_tp") + n - 1)
                pool.tensor_copy(HG[n % 2][0:NCH].rearrange("p (g t i) -> p g t i", g=4, t=L),
                                 HC[0:NCH, :, n * 64:n * 64 + 64].rearrange("p t (g i) -> p g t i", g=4)).then_inc(S("s_hg_ready"), 1)
            pool.wait_ge(S("s_tab_ready"), B("s_tab_ready") + 1)
            pool.wait_ge(S("s_v_ready"), B("s_v_ready") + Q // 4)
            turn = scan_turn(pool, G, 1)
            with pool.Fori(1, NCH) as i:
                G.enter(i - 1, 4)
                turn(NCH - i, 1)
                G.leave(NCH - 1)
            pool.sem_inc(S("s_bwd_done"), 1)

        @block.gpsimd
        def _(pool):
            moe_pool(pool, 0)
            s5_pool(pool)
            moe_pool(pool, 1)


def constants():
    k = np.arange(P)
    cst = np.zeros((P, 80), np.float32)
    cst[:, 0] = k
    cst[:, 2], cst[:, 3] = N_ALL + k, N_LAT + k
    cst[:, 4], cst[:, 5] = -(N_ALL + k), -(N_LAT + k)
    cst[:, 6], cst[:, 7] = k < ST, k >= ST
    cst[:, 8:72] = 8.0 ** (np.arange(N_EXP) % NSLOT)
    cst[:, 72] = 1.0
    cst[:, 73], cst[:, 74] = -cst[:, 6], -cst[:, 7]
    rot = np.zeros((ROPE, ROPE), np.float32)
    for i in range(ROPE // 2):
        rot[2 * i + 1, 2 * i], rot[2 * i, 2 * i + 1] = -1, 1
    t = np.arange(N_LAT)
    inv = (10000.0 ** (-np.arange(16, dtype=np.float32) / 16)).astype(np.float32)
    ang = np.concatenate([(t // 64).astype(np.float32)[:, None] * inv, (t % 64).astype(np.float32)[:, None] * inv], -1)
    cos = np.concatenate([np.ones((N_CTX, ROPE // 2), np.float32), np.cos(ang)])
    sin = np.concatenate([np.zeros((N_CTX, ROPE // 2), np.float32), np.sin(ang)])
    return dict(ident=np.eye(P, dtype=np.float32), tri=(k[:, None] < k[None, :]).astype(np.float32),
                iota=np.broadcast_to(k.astype(np.float32), (P, P)), cst=cst, rot=rot,
                cosT=np.repeat(cos, 2, 1).T, sinT=np.repeat(sin, 2, 1).T)


def laid_out(a):
    def by_state(x):
        return np.concatenate([x, x], 0)

    r = constants()
    r.update(x=a["x"][0], ctx=a["ctx"][0], cs=np.stack([a["c"][0], a["c_ctx"]], -1).reshape(P, DC, 2),
             ada_w=a["ada_w"], ada_b=a["ada_b"], norm_g=a["norm_g"].reshape(2, 4 * D),
             gcol=np.concatenate([a["mla_g_q"][0].reshape(P, QC), a["mla_g_kv"][0].reshape(P, KC)], 1),
             w_dqkv=a["mla_w_dqkv"][0], w_uq=a["mla_w_uq"][0], w_ukv=a["mla_w_ukv"][0], w_o=a["mla_w_o"][0],
             w_router=a["moe_w_router"], moe_bias=a["moe_bias"], w_gate=a["moe_w_gate"], w_up=a["moe_w_up"],
             w_down=a["moe_w_down"], sh_gate=a["sh_w_gate"], sh_up=a["sh_w_up"], sh_down=a["sh_w_down"],
             s5_d=a["s5_d"], w_glu=a["s5_w_glu"][0], b_glu=a["s5_b_glu"])
    lam_re, lam_im = (a[k][0].transpose(2, 0, 1).reshape(ST, Q) for k in ("s5_lam_re", "s5_lam_im"))
    log_step = np.broadcast_to(a["s5_log_step"][0].reshape(1, Q), (ST, Q))
    r["s5_par"] = by_state(np.concatenate([lam_re, lam_im, log_step], 1))
    r["s5_b"] = by_state(np.stack([a[k][0].transpose(2, 0, 1, 3).reshape(ST, Q, GI) for k in ("s5_b_re", "s5_b_im")], 1))
    r["s5_c"] = by_state(np.stack([a[k][0].transpose(3, 0, 1, 2).reshape(ST, Q, GI) for k in ("s5_c_re", "s5_c_im")], 1))
    return {k: np.ascontiguousarray(v) for k, v in r.items()}


def kernel(**inputs):
    import concourse.bacc as _bacc
    from concourse.bass_utils import run_bass_kernel_spmd as _run

    nc = _bacc.Bacc("TRN2", target_bir_lowering=False, num_devices=1)
    arrays = laid_out({k: np.asarray(v) for k, v in inputs.items()})
    I = {k: nc.dram_tensor(k, v.shape, F32, kind="ExternalInput").ap() for k, v in arrays.items()}
    O = {"out": nc.dram_tensor("out", (N_LAT, D), F32, kind="ExternalOutput").ap()}
    build(nc, I, O)
    r = _run(nc, [arrays], core_ids=[0])
    return np.asarray(r.results[0]["out"]).reshape(1, N_LAT, D)
```

```python
from contextlib import ExitStack

import numpy as np

import concourse.bass as bass
from concourse import mybir

F32 = mybir.dt.float32
BF16 = mybir.dt.bfloat16
U32 = mybir.dt.uint32
I32 = mybir.dt.int32
ALU = mybir.AluOpType
ACT = mybir.ActivationFunctionType
AX_X = mybir.AxisListType.X

P = 128
D = 1024
DC = D // P
N_LAT, N_CTX = 512, 256
N_ALL = N_LAT + N_CTX
CT, LT = N_CTX // P, N_LAT // P
AT = CT + LT
EPS = 1e-6
HEADS, NOPE, ROPE, VD = 8, 128, 64, 128
QL, KVL = 384, 256
QC, KC = QL // P, KVL // P
AW = QL + KVL + ROPE
QW, KVW = HEADS * (NOPE + ROPE), HEADS * (NOPE + VD)
SCALE = float(NOPE + ROPE) ** -0.5
N_EXP, FE = 64, 256
EPAD = N_EXP + 1
FC = FE // P
ROUTED = 2.5
TOP_K = 8
BIG = 1.0e30
SLOT = 2 * DC * FE + FC * D
NSLOT = 4
GROUPS, GI, ST = 64, 16, 64
L = 8
LC, CC_ = N_LAT // L, N_CTX // L
NCH = LC + CC_
Q = 2 * GROUPS
QB = 8
TWO_PI = float(2.0 * np.pi)
ROUND = 12582912.0
PI_A, PI_B = 6.28125, 0.0019350051879882812
PI_C = TWO_PI - PI_A - PI_B
ADA_T = 6 * D // 512


class Steps:

    def __init__(self, eng, sem):
        self.eng, self.sem, self.n, self.off = eng, sem, 0, None

    def __call__(self, ins):
        self.n += 1
        ins.then_inc(self.sem, 1)
        self.eng.wait_ge(self.sem, self.n if self.off is None else self.off + self.n)

    def enter(self, i, per):
        self.start, self.per, self.off = self.n, per, i * per

    def leave(self, turns):
        assert self.n - self.start == self.per, self.n - self.start
        self.n, self.off = self.start + self.per * turns, None


def build(nc, I, O):
    ctx = ExitStack()
    with ctx:
        def sb(name, shape, dt=F32):
            return ctx.enter_context(nc.sbuf_tensor("sb_" + name, shape, dt))

        def dram(name, shape):
            return nc.dram_tensor("scratch_" + name, shape, F32).ap()

        sems = {}

        def S(name):
            if name not in sems:
                sems[name] = ctx.enter_context(nc.semaphore(name))
            return sems[name]

        RING = sb("ring", [P, NSLOT * SLOT])
        X = sb("x", [P, AT, D])
        ROWS = sb("rows", [P, 4, D])
        WORK = sb("work", [P, 16384])
        ident = sb("ident", [P, P])
        rot = sb("rot", [ROPE, ROPE])
        cst = sb("cst", [P, 80])
        tri = sb("tri", [P, P], BF16)
        ones_b = sb("ones_b", [P, P], BF16)
        iota_b = sb("iota_b", [P, P], BF16)
        cs = sb("cs", [P, DC, 2])
        csl = sb("csl", [P, DC, 2])
        gcol = sb("gcol", [P, QC + KC])
        eps = sb("eps", [P, 1])
        junk = sb("junk", [P, D], BF16)
        ss = sb("ss", [P, 16])
        sd = sb("sd", [P, 16])
        rs = sb("rs", [P, 16])
        sm = sb("sm", [P, 8])
        mx = sb("mx", [P, 2])
        words = sb("words", [1, P // 2], I32)
        ends = sb("ends", [1, N_EXP], I32)
        idxg = sb("idxg", [P, 2], U32)
        gateg = sb("gateg", [P, 2])
        idxs = sb("idxs", [P, 2], U32)
        gates = sb("gates", [P, 2])
        it = sb("it", [P, 8])
        sc = sb("sc", [P, 4, GROUPS])
        spare = sb("spare", [P, 2])
        PS = ctx.enter_context(nc.psum_tensor("ps", [P, 8, 512], F32))

        mod_d = dram("mod", (2, 2, 6 * D))
        f_d = [dram("f0", (N_ALL + P, D)), dram("f1", (N_LAT + P, D))]
        acc_d = [dram("acc0", (N_ALL + P, D)), dram("acc1", (N_LAT + P, D))]

        def work(a, n):
            return WORK[:, a:a + n]

        def bank2(b, n=1024):
            return PS[:, b:b + 2, :].rearrange("p b n -> p (b n)")[:, 0:n]

        ring = RING[:, :]
        w_dqkv = ring[:, 0:DC * AW].rearrange("p (j n) -> p j n", j=DC)
        OT = ring[:, 0:HEADS * N_ALL].rearrange("p (h n) -> p h n", h=HEADS)
        w_uq = ring[:, 7680:7680 + QC * QW].rearrange("p (j n) -> p j n", j=QC)
        w_ukv = ring[:, 12288:12288 + KC * KVW].rearrange("p (j n) -> p j n", j=KC)
        w_o = ring[:, 16384:24576].rearrange("p (h n) -> p h n", h=HEADS)
        HT = work(0, DC * N_ALL).rearrange("p (j n) -> p j n", j=DC)
        V = work(0, AT * D).rearrange("p (t n) -> p t n", t=AT)
        CQT = work(6144, QC * N_ALL).rearrange("p (j n) -> p j n", j=QC)
        CKT = work(8448, KC * N_ALL).rearrange("p (j n) -> p j n", j=KC)
        KPT = work(9984, N_ALL)[0:ROPE, :]
        KPR = work(10752, N_ALL)[0:ROPE, :]
        H = [work(11520, D), work(12544, D)]
        CA = work(13568, AW)
        qnT = work(11520, N_ALL)
        knT = work(12288, N_ALL)
        qpT = work(13056, N_ALL)[0:ROPE, :]
        qpR = work(13824, N_ALL)[0:ROPE, :]
        cosT = work(14592, N_ALL)[0:ROPE, :]
        sinT = work(15360, N_ALL)[0:ROPE, :]
        rows1 = ROWS[:, :, :].rearrange("p a b -> p (a b)")
        PR = [rows1[:, 0:N_ALL], work(9984, N_ALL)]
        PT = rows1[:, N_ALL:N_ALL + AT * N_LAT].rearrange("p (k q) -> p k q", k=AT)
        MOD = work(0, 6 * D)[0:2, :]
        MODB = work(6144, 6 * D)[0:2, :]
        NG = work(12288, 4 * D)[0:2, :]

        def ada_slot(n):
            return ring[:, (n % 4) * SLOT:(n % 4) * SLOT + DC * 512].rearrange("p (j n) -> p j n", j=DC)

        def slot(u):
            return ring[:, u * SLOT:(u + 1) * SLOT]

        RING4 = ring.rearrange("p (s n) -> p s n", s=NSLOT)

        def gu_rhs(u, j):
            return slot(u)[:, 0:2 * DC * FE].rearrange("p (w j n) -> p w j n", w=2, j=DC)[:, :, j, :]

        def dn_rhs(u, j, h):
            return slot(u)[:, 2 * DC * FE + j * D + h * 512:2 * DC * FE + j * D + h * 512 + 512]

        XG = [work(0, D), work(1024, D)]
        XT = [work(2048, D).rearrange("p (j n) -> p j n", j=DC), work(3072, D).rearrange("p (j n) -> p j n", j=DC)]
        OS = [work(4096, D), work(5120, D)]
        XGo = work(6144, D)
        SG = [work(7168, FE), work(7424, FE)]
        HH = [work(7680, FE), work(7936, FE)]
        HHT = [work(8192, FE).rearrange("p (j n) -> p j n", j=FC), work(8448, FE).rearrange("p (j n) -> p j n", j=FC)]
        OH = [work(8704 + 384 * k, 384).bitcast(BF16).rearrange("p (t n) -> p t n", t=AT) for k in range(2)]
        POSM = work(9472, AT * EPAD).rearrange("p (t e) -> p t e", t=AT)
        RH = work(9872, AT * EPAD * 3).bitcast(BF16).rearrange("p (t e c) -> p t e c", t=AT, c=6)
        MB16 = work(11064, 192).bitcast(BF16).rearrange("p (t e) -> p t e", t=AT)
        at = [13568]

        def temp(n):
            at[0] += n
            assert at[0] <= 16384
            return work(at[0] - n, n)

        def t_e(n):
            return temp(AT * n).rearrange("p (t e) -> p t e", t=AT)

        SC, BI, MR = t_e(64), t_e(64), t_e(64)
        GTE = t_e(64)
        M8 = work(6656, AT * 64).rearrange("p (t g k) -> p t g k", t=AT, g=8)
        GS, GR, G8, TR, GM, TB, E8 = t_e(16), t_e(16), t_e(8), t_e(8), t_e(8), t_e(8), t_e(8)
        WR = work(6144, DC * N_EXP).rearrange("p (j e) -> p j e", j=DC)
        BROW = temp(N_EXP)
        POSJ = temp(8)
        CNT, NB, END = temp(64), temp(64), temp(64)
        SHIFT = temp(P)
        TAB = temp(4)
        DG = temp(P).bitcast(BF16)


        x_rows = [I["ctx"][k * P:(k + 1) * P, :] for k in range(CT)] + [I["x"][k * P:(k + 1) * P, :] for k in range(LT)]
        stream = [1] * CT + [0] * LT
        TILES = [list(range(AT)), list(range(LT))]

        def row(k):
            return ROWS[:, k, :]

        def pe_transposes(src, dst, n, done):
            for j in range(n):
                ins = nc.tensor.transpose(dst[:, j * P:j * P + src.shape[0]], src[:, j::n], ident[0:src.shape[0], 0:src.shape[0]])
            ins.then_inc(done, 1)

        h1_d, x2_d = dram("h1", (N_ALL, D)), dram("x2", (N_LAT, D))
        left = {}

        def again(name, old, count):
            sems[name], left[name] = S(old), count

        for name, old, count in (
                ("s_rows", "rows_a", 64), ("s_h_out0", "ada_in0", 96), ("s_h_out1", "ada_in1", 96), ("s_x_out", "x_in", 16 * AT),
                ("s_hc_in", "w_dqkv_in", 16), ("s_par_in", "w_ukv_in", 16), ("s_b_in0", "w_uq_in", 16), ("s_b_in1", "w_o_in", 16),
                ("s_c_in", "ada_in2", 96), ("s_t_in", "ada_in3", 96), ("s_d_in", "rope_in", 32), ("s_wg_in0", "rows_m", 64),
                ("s_wg_in1", "const_in", 80), ("s_bg_in", "modb_in", 64), ("s_rowg", "rows_g", 32), ("s_xr_in", "mod_out", 32),
                ("s_rown", "tri_in", 32),
                ("s_hg_ready", "a_mm", AT), ("s_sd", "a_sd", 1), ("s_h_ready", "a_h_ready", AT), ("s_u_tp", "a_tp", AT), ("s_u_ready", "a_ht", 2 * AT),
                ("s_tab_v", "ca_ready", AT), ("s_tab_a", "c_sd", AT), ("s_tab_ready", "k_rope", 1), ("s_w_ready", "qn_ready", HEADS),
                ("s_w_tp", "qn_mm", HEADS), ("s_wt_ready", "qp_ready", HEADS), ("s_v_mm", "kn_mm", HEADS),
                ("s_v_ready", "ot_lat", HEADS), ("s_fwd_done", "kn_ready", HEADS), ("s_bwd_done", "mod_free", 1),
                ("s_cc_ready", "q_rope", HEADS), ("s_kk_mm", "qp_mm", HEADS), ("s_kk_ready", "ot_ctx", HEADS),
                ("s_y_mm", "q_rot", HEADS), ("s_y_ready", "p_ready", HEADS * AT), ("s_hd", "mod_ready", 2),
                ("s_gelu", "p_exp", HEADS * AT), ("s_yt_tp", "p_tp", HEADS * AT), ("s_yt", "nmax", HEADS * AT),
                ("s_glu_mm", "s_mm", HEADS * AT), ("s_z", "ct_ready", AT), ("s_sig", "pt_ready", HEADS * AT),
                ("s_oo", "o_used", AT), ("s_osd", "v_ready_a", AT), ("x3_ready", "v_ready_v", AT)):
            again(name, old, count)

        def B(name):
            return left[name]

        VST = ring[:, 0:(NCH + 1) * Q].rearrange("p (s q) -> p s q", q=Q)
        HC = ring[:, 12416:12416 + L * D].rearrange("p (t n) -> p t n", t=L)
        TEMP = ring[:, 20608:24576]
        U = work(0, GROUPS * NCH).rearrange("p (g c) -> p g c", g=GROUPS)
        TZ = work(6144, GROUPS * P).rearrange("p (g n) -> p g n", g=GROUPS)
        KKS = work(14336, 8 * 240)[0:GI, :].rearrange("p (g n) -> p g n", g=8)
        DROW = work(14336, D)
        tx = X[:, :, :].rearrange("p a b -> p (a b)")
        X1, X2 = (tx[:, a:a + 1152].rearrange("p (j q) -> p j q", q=Q) for a in (0, 1152))
        Y1, Y2 = (tx[:, a:a + 1024].rearrange("p (j q) -> p j q", q=Q) for a in (2304, 3328))
        LRE, LIM, LST = (tx[:, 4352 + k * Q:4352 + (k + 1) * Q] for k in range(3))
        tA, tTH, tEA, tK, tR, tR2, tFR, tFI, tSMI, tM, tN = (tx[:, 4736 + k * Q:4736 + (k + 1) * Q] for k in range(11))
        F1, F2 = tA, tTH
        NR, NI = (rows1[:, a:a + 1152].rearrange("p (j q) -> p j q", q=Q) for a in (0, 1152))
        TMP = rows1[:, 2304:3456]
        GR_, GI_ = (TEMP[:, a:a + 1024].rearrange("p (j q) -> p j q", q=Q) for a in (0, 1024))
        WW = TEMP[:, 0:1024]
        WT = TEMP[:, 1024:2048].rearrange("p (k n) -> p k n", k=8)
        BB = [TEMP[:, 2048 + k * 256:2304 + k * 256].rearrange("p (c q i) -> p c q i", c=2, q=QB) for k in range(2)]
        HG = [TEMP[:, 2560 + k * 512:3072 + k * 512] for k in range(2)]
        CB = TEMP[:, 0:512].rearrange("p (d c q i) -> p d c q i", d=2, c=2, q=QB)
        BD = TEMP[:, 512:1024].rearrange("p (d c q i) -> p d c q i", d=2, c=2, q=QB)
        BB2 = TEMP[:, 1024:1280].rearrange("p (d q i) -> p d q i", d=2, q=QB)
        CC = TEMP[:, 1280:3584].rearrange("p (d q j i) -> p d q j i", d=2, q=QB, i=GI)
        YT = work(0, DC * N_LAT).rearrange("p (j n) -> p j n", j=DC)
        OO = work(6144, LT * D).rearrange("p (t n) -> p t n", t=LT)
        BG = work(10240, 2 * D)
        ZT = [work(12288, D), work(13312, D)]
        WG = [ring[:, k * 8192:(k + 1) * 8192].rearrange("p (j w n) -> p j w n", j=DC, w=2) for k in range(2)]

        def scan_turn(eng, W, d):
            q = slice(d * GROUPS, (d + 1) * GROUPS)
            t1, t2 = (sc[:, k, :] for k in (2 * d, 2 * d + 1))
            half = ST

            def turn(i, step):
                cur = VST[:, bass.ds(i, 1), q].rearrange("p a q -> p (a q)")
                last = VST[:, bass.ds(i + step, 1), q].rearrange("p a q -> p (a q)")
                W(eng.tensor_tensor(t1, last, NR[:, L, q], ALU.mult))
                eng.tensor_tensor(t2[0:half], last[half:P], tSMI[half:P, q], ALU.mult)
                W(eng.tensor_tensor(t2[half:P], last[0:half], tSMI[0:half, q], ALU.mult))
                W(eng.tensor_tensor(t2, t2, t1, ALU.add))
                W(eng.tensor_tensor(cur, cur, t2, ALU.add))

            return turn

        def before_moe(l):
            n0 = AT
            left = dict(
                wr_in=32, sh_in=48, w_in0=768, w_in1=768, w_in2=768, w_in3=768, f_out0=n0 // 2 * 16, f_out1=n0 // 2 * 16,
                f_trash=16, acc_out0=n0 // 2 * 16, acc_out1=n0 // 2 * 16, acc_out2=16, rows_in=32,
                acc_in0=n0 // 2 * 16, acc_in1=n0 // 2 * 16, h_ready=n0, zero_ready=1, so_ready_a=n0, so_ready_v=n0,
                sh_down=n0, ht_tp=n0, ht_ready=2 * n0, logits=n0, sh_gu=n0, sh_h=n0, sh_tp=n0, sh_ht=n0, mask_ready=1,
                pos_mm=1, ends_ready=1, tab_mm=1, tab_ready=1, all_scattered=1, o_sd=n0, x_ready=n0, scores=1, sd=1, sh_silu=n0)
            return lambda name: l * left[name]

        def pairs_of(eng, l):
            most = N_EXP + len(TILES[l]) * TOP_K
            total = eng.value_load(ends[0:1, N_EXP - 1:N_EXP], min_val=N_EXP, max_val=most)
            return eng.snap((total + 1) >> 1, min_val=N_EXP // 2, max_val=most // 2), most // 2

        def expert_of(eng, word, u):
            return nc.s_assert_within(eng.snap((word >> (7 * u)) & 127), 0, N_EXP,
                                      skip_runtime_bounds_check_because="the table holds experts' numbers")

        block = ctx.enter_context(nc.Block())

        def moe_sp(sp, l):
            tiles, NT = TILES[l], len(TILES[l])
            T = NT * P
            g, Z = "m_", before_moe(l)
            sp.dma_start(WR, I["w_router"][l].rearrange("(p j) e -> p j e", j=DC)).then_inc(S(g + "wr_in"), 16)
            sp.dma_start(BROW, I["moe_bias"][l:l + 1, :].to_broadcast((P, N_EXP))).then_inc(S(g + "wr_in"), 16)

            def load(u, gate_w, up_w, down_w, s):
                w = slot(u)
                sp.dma_start(w[:, 0:DC * FE], gate_w.rearrange("(p j) n -> p (j n)", j=DC)).then_inc(s, 16)
                sp.dma_start(w[:, DC * FE:2 * DC * FE], up_w.rearrange("(p j) n -> p (j n)", j=DC)).then_inc(s, 16)
                sp.dma_start(w[:, 2 * DC * FE:SLOT], down_w.rearrange("(p j) n -> p (j n)", j=FC)).then_inc(s, 16)

            if l == 0:
                sp.wait_ge(S("o_mm"), AT)
            load(3, I["sh_gate"][l], I["sh_up"][l], I["sh_down"][l], S(g + "sh_in"))
            for u in range(3):
                load(u, I["w_gate"][l, u], I["w_up"][l, u], I["w_down"][l, u], S(g + f"w_in{u}"))
            for n in range(len(tiles)):
                sp.wait_ge(S(g + "h_ready"), Z("h_ready") + n + 1)
                sp.dma_start(f_d[l][n * P:(n + 1) * P, :], H[n % 2]).then_inc(S(g + f"f_out{n % 2}"), 16)
            sp.wait_ge(S(g + "zero_ready"), Z("zero_ready") + 1)
            sp.dma_start(f_d[l][T:T + P, :], ROWS[:, 0, :]).then_inc(S(g + "f_trash"), 16)
            sp.dma_start(acc_d[l][T:T + P, :], ROWS[:, 0, :]).then_inc(S(g + "acc_out2"), 16)
            for n in range(len(tiles)):
                sp.wait_ge(S(g + "so_ready_a"), Z("so_ready_a") + n + 1)
                sp.wait_ge(S(g + "so_ready_v"), Z("so_ready_v") + n + 1)
                sp.dma_start(acc_d[l][n * P:(n + 1) * P, :], H[n % 2]).then_inc(S(g + f"acc_out{n % 2}"), 16)
            sp.wait_ge(S(g + "sh_down"), Z("sh_down") + len(tiles))
            load(3, I["w_gate"][l, 3], I["w_up"][l, 3], I["w_down"][l, 3], S(g + "w_in3"))
            wg = I["w_gate"][l].rearrange("e (p j) n -> p e (j n)", j=DC)
            wu = I["w_up"][l].rearrange("e (p j) n -> p e (j n)", j=DC)
            wd = I["w_down"][l].rearrange("e (p j) n -> p e (j n)", j=FC)
            sp.wait_ge(S(g + "ends_ready"), Z("ends_ready") + 1)
            sp.wait_ge(S(g + "w_in0"), Z("w_in0") + 48)
            sp.sem_inc(S(f"w_ready{l}"), 1)
            with sp.Fori(1, N_EXP // NSLOT) as eb:
                for u in range(NSLOT):
                    e = sp.snap(eb * NSLOT + u, min_val=0, max_val=N_EXP - 1)
                    k = (u + 1) % NSLOT
                    there = sp.snap(eb * 48 + (Z(f"w_in{k}") + 48 * (u + 1 == NSLOT)), min_val=1, max_val=4096)
                    sp.wait_ge(S(g + f"w_in{k}"), there)
                    sp.sem_inc(S(f"w_ready{l}"), 1)
                    blocks = sp.value_load(ends[0:1, bass.ds(eb * NSLOT + (u - NSLOT), 1)], min_val=1, max_val=N_EXP + NT * TOP_K)
                    sp.wait_ge(S(f"dn_mm{l}"), blocks)
                    sp.sem_inc(S("sp_starts"), 1)
                    w = slot(u)
                    sp.dma_start(w[:, 0:DC * FE], wg[:, bass.ds(e, 1), :].rearrange("p a n -> p (a n)")).then_inc(S(g + f"w_in{u}"), 16)
                    sp.dma_start(w[:, DC * FE:2 * DC * FE], wu[:, bass.ds(e, 1), :].rearrange("p a n -> p (a n)")).then_inc(S(g + f"w_in{u}"), 16)
                    sp.dma_start(w[:, 2 * DC * FE:SLOT], wd[:, bass.ds(e, 1), :].rearrange("p a n -> p (a n)")).then_inc(S(g + f"w_in{u}"), 16)
            for u in range(1, NSLOT):
                sp.wait_ge(S(g + f"w_in{u}"), Z(f"w_in{u}") + 48 * N_EXP // NSLOT)
                sp.sem_inc(S(f"w_ready{l}"), 1)
            sp.sem_inc(S(f"w_ready{l}"), 1)
            sp.wait_ge(S(g + "f_trash"), Z("f_trash") + 16)
            sp.wait_ge(S(g + "acc_out2"), Z("acc_out2") + 16)
            for k in range(2 if l == 0 else 1):
                sp.dma_start(row(k), mod_d[l, k:k + 1, 5 * D:6 * D].to_broadcast((P, D))).then_inc(S(g + "rows_in"), 16)
            sp.wait_ge(S(g + "all_scattered"), Z("all_scattered") + 1)
            for n in range(len(tiles)):
                if n >= 2:
                    sp.wait_ge(S(g + "x_ready"), Z("x_ready") + n - 1)
                sp.dma_start(OS[n % 2], acc_d[l][n * P:(n + 1) * P, :]).then_inc(S(g + f"acc_in{n % 2}"), 16)


        def s5_sp(sp):
            sp.wait_ge(S("m_x_ready"), AT)
            for t in range(LT):
                sp.dma_start(x2_d[t * P:(t + 1) * P, :], X[:, CT + t, :]).then_inc(S("s_x_out"), 16)
            for k, (q, r) in enumerate([(1, 0), (0, 0), (1, 1), (0, 1)]):
                sp.dma_start(row(k), mod_d[1, r:r + 1, q * D:(q + 1) * D].to_broadcast((P, D))).then_inc(S("s_rows"), 16)
            for t in range(AT):
                sp.wait_ge(S("s_h_ready"), B("s_h_ready") + t + 1)
                sp.dma_start(h1_d[t * P:(t + 1) * P, :], H[t % 2]).then_inc(S(f"s_h_out{t % 2}"), 16)
            for k in range(2):
                sp.wait_ge(S(f"s_h_out{k}"), B(f"s_h_out{k}") + AT // 2 * 16)
            sp.dma_start(HC[0:LC, :, :], h1_d[N_CTX:N_ALL, :].rearrange("(c t) n -> c t n", t=L)).then_inc(S("s_hc_in"), 16)
            sp.dma_start(HC[LC:NCH, :, :], h1_d[0:N_CTX, :].rearrange("(c t) n -> c t n", t=L)).then_inc(S("s_hc_in"), 16)
            sp.wait_ge(S("s_x_out"), B("s_x_out") + 16 * LT)
            sp.dma_start(tx[:, 4352:4736], I["s5_par"]).then_inc(S("s_par_in"), 16)
            sp.wait_ge(S("s_tab_ready"), B("s_tab_ready") + 1)
            for n in range(Q // QB):
                if n >= 2:
                    sp.wait_ge(S("s_w_ready"), B("s_w_ready") + n - 1)
                sp.dma_start(BB[n % 2], I["s5_b"][:, :, n * QB:(n + 1) * QB, :]).then_inc(S(f"s_b_in{n % 2}"), 16)
            sp.dma_start(DROW, I["s5_d"].to_broadcast((P, D))).then_inc(S("s_d_in"), 16)
            sp.wait_ge(S("s_v_mm"), B("s_v_mm") + Q // 4)
            for n in range(GROUPS // QB):
                if n:
                    sp.wait_ge(S("s_cc_ready"), B("s_cc_ready") + n)
                for d in range(2):
                    c = slice(d * GROUPS + n * QB, d * GROUPS + (n + 1) * QB)
                    sp.dma_start(CB[:, d], I["s5_c"][:, :, c, :]).then_inc(S("s_c_in"), 16)
                    sp.dma_start(BD[:, d], I["s5_b"][:, :, c, :]).then_inc(S("s_c_in"), 16)
                sp.wait_ge(S("s_kk_ready"), B("s_kk_ready") + n + 1)
                for k in range(L):
                    sp.dma_start(TZ[k * GI:(k + 1) * GI, n * QB:(n + 1) * QB, :],
                                 KKS[:, :, (L - 1 - k) * GI:(L - 1 - k) * GI + P]).then_inc(S("s_t_in"), 16)
            sp.wait_ge(S("s_y_mm"), B("s_y_mm") + GROUPS // QB)
            wg = I["w_glu"].rearrange("(p j) (w h n) -> p j w h n", j=DC, w=2, h=2)
            sp.dma_start(BG, I["b_glu"].to_broadcast((P, 2 * D))).then_inc(S("s_bg_in"), 16)
            for w in range(2):
                sp.dma_start(WG[0][:, :, w, :], wg[:, :, w, 0, :]).then_inc(S("s_wg_in0"), 16)
            sp.dma_start(row(0), mod_d[1, 0:1, 2 * D:3 * D].to_broadcast((P, D))).then_inc(S("s_rowg"), 16)
            xr = x2_d.rearrange("(c t) n -> t c n", t=L)
            for t in range(L):
                sp.dma_start(X[(t % 2) * LC:(t % 2 + 1) * LC, t // 2, :], xr[t]).then_inc(S("s_xr_in"), 16)
            sp.wait_ge(S("s_yt_tp"), B("s_yt_tp") + L)
            for w in range(2):
                sp.dma_start(WG[1][:, :, w, :], wg[:, :, w, 1, :]).then_inc(S("s_wg_in1"), 16)
            sp.wait_ge(S("x3_ready"), B("x3_ready") + LT)
            for k, q in enumerate((4, 3)):
                sp.dma_start(row(k), mod_d[1, 0:1, q * D:(q + 1) * D].to_broadcast((P, D))).then_inc(S("s_rown"), 16)

        @block.sync
        def _(sp):
            for name, dst in (("ident", ident[:, :]), ("rot", rot[:, :]), ("cst", cst[:, :]), ("cs", cs[:, :, :]),
                              ("gcol", gcol[:, :])):
                sp.dma_start(dst, I[name]).then_inc(S("const_in"), 16)
            sp.dma_start(work(0, P), I["tri"]).then_inc(S("tri_in"), 16)
            sp.dma_start(work(P, P), I["iota"]).then_inc(S("tri_in"), 16)
            for l in range(2):
                w = I["ada_w"][l].rearrange("(p j) n -> p j n", j=DC)
                if l == 1:
                    sp.wait_ge(S("mod_ready"), 1)
                sp.dma_start(MODB, I["ada_b"][l:l + 1, :].to_broadcast((2, 6 * D))).then_inc(S("modb_in"), 16)
                sp.dma_start(NG, I["norm_g"][l:l + 1, :].to_broadcast((2, 4 * D))).then_inc(S("modb_in"), 16)
                for m in range(ADA_T):
                    n = l * ADA_T + m
                    if n >= 4:
                        sp.wait_ge(S("ada_mm"), n - 3)
                    sp.dma_start(ada_slot(n), w[:, :, m * 512:(m + 1) * 512]).then_inc(S(f"ada_in{n % 4}"), 16)
                if l == 0:
                    for t in range(AT):
                        sp.dma_start(X[:, t, :], x_rows[t]).then_inc(S("x_in"), 16)
                sp.wait_ge(S("mod_ready"), l + 1)
                sp.dma_start(mod_d[l], MOD).then_inc(S("mod_out"), 16)
                if l == 0:
                    sp.wait_ge(S("mod_out"), 16)
                    sp.sem_inc(S("mod_free"), 1)
            sp.wait_ge(S("mod_out"), 32)

            def load_rows(l, vectors, tag):
                for k, (v, r) in enumerate(vectors):
                    sp.dma_start(row(k), mod_d[l, r:r + 1, v * D:(v + 1) * D].to_broadcast((P, D))).then_inc(S(tag), 16)

            load_rows(0, [(1, 0), (0, 0), (1, 1), (0, 1)], "rows_a")
            sp.wait_ge(S("ada_mm"), 2 * ADA_T)
            sp.dma_start(w_dqkv, I["w_dqkv"].rearrange("(p j) n -> p j n", j=DC)).then_inc(S("w_dqkv_in"), 16)
            sp.dma_start(w_ukv, I["w_ukv"].rearrange("(p j) n -> p j n", j=KC)).then_inc(S("w_ukv_in"), 16)
            sp.dma_start(w_uq, I["w_uq"].rearrange("(p j) n -> p j n", j=QC)).then_inc(S("w_uq_in"), 16)
            sp.dma_start(w_o, I["w_o"].rearrange("(h p) n -> p h n", p=P)).then_inc(S("w_o_in"), 16)
            sp.dma_start(cosT, I["cosT"]).then_inc(S("rope_in"), 16)
            sp.dma_start(sinT, I["sinT"]).then_inc(S("rope_in"), 16)
            sp.wait_ge(S("pv_ctx"), HEADS)
            sp.wait_ge(S("pv_lat"), HEADS)
            load_rows(0, [(2, 0), (2, 1)], "rows_g")
            sp.wait_ge(S("x1_ready"), AT)
            load_rows(0, [(4, 0), (3, 0), (4, 1), (3, 1)], "rows_m")
            moe_sp(sp, 0)
            s5_sp(sp)
            moe_sp(sp, 1)
            out = O["out"].rearrange("(c t) n -> t c n", t=L)
            for m in range(LT):
                sp.wait_ge(S("m_x_ready"), AT + m + 1)
                for k in range(2):
                    sp.dma_start(out[2 * m + k], X[k * LC:(k + 1) * LC, m, :]).then_inc(S("out_done"), 16)
            sp.wait_ge(S("out_done"), 16 * L)

        def moe_pe(pe, l):
            tiles, NT = TILES[l], len(TILES[l])
            g, Z = "m_", before_moe(l)
            pe.wait_ge(S(g + "wr_in"), Z("wr_in") + 32)
            for n in range(NT + 1):
                if n < NT:
                    pe.wait_ge(S(g + "h_ready"), Z("h_ready") + n + 1)
                    if n >= 2:
                        pe.wait_ge(S(g + "ht_ready"), Z("ht_ready") + 2 * (n - 1))
                    pe_transposes(H[n % 2], bank2(2 * (n % 2)), DC, S(g + "ht_tp"))
                if n:
                    a = n - 1
                    pe.wait_ge(S(g + "ht_ready"), Z("ht_ready") + 2 * n)
                    for j in range(DC):
                        mm = nc.tensor.matmul(PS[:, 7, a * 64:(a + 1) * 64], HT[:, j, a * P:(a + 1) * P], WR[:, j, :], start=j == 0, stop=j == DC - 1)
                    mm.then_inc(S(g + "logits"), 1)
            pe.wait_ge(S(g + "sh_in"), Z("sh_in") + 48)
            for n in range(NT + 1):
                if n < NT:
                    if n >= 2:
                        pe.wait_ge(S(g + "sh_h"), Z("sh_h") + n - 1)
                    for j in range(DC):
                        mm = nc.tensor.matmul(PS[:, 4 + n % 2, :], HT[:, j, n * P:(n + 1) * P], gu_rhs(3, j), start=j == 0, stop=j == DC - 1)
                    mm.then_inc(S(g + "sh_gu"), 1)
                if n:
                    a = n - 1
                    pe.wait_ge(S(g + "sh_h"), Z("sh_h") + a + 1)
                    if a:
                        pe.wait_ge(S(g + "sh_ht"), Z("sh_ht") + a)
                    pe_transposes(HH[a % 2], PS[:, 6, :], FC, S(g + "sh_tp"))
                    pe.wait_ge(S(g + "sh_ht"), Z("sh_ht") + a + 1)
                    if a >= 2:
                        pe.wait_ge(S(g + "so_ready_a"), Z("so_ready_a") + a - 1)
                        pe.wait_ge(S(g + "so_ready_v"), Z("so_ready_v") + a - 1)
                    for half in range(2):
                        for j in range(FC):
                            mm = nc.tensor.matmul(PS[:, 2 * (a % 2) + half, :], HHT[a % 2][:, j, :], dn_rhs(3, j, half), start=j == 0, stop=j == FC - 1)
                    mm.then_inc(S(g + "sh_down"), 1)
            pe.wait_ge(S(g + "mask_ready"), Z("mask_ready") + 1)
            for n in range(NT):
                for b in range(n):
                    nc.tensor.matmul(PS[:, 7, n * 64:(n + 1) * 64], ones_b[:, :], MB16[:, b, :], start=b == 0, stop=False)
                nc.tensor.matmul(PS[:, 7, n * 64:(n + 1) * 64], tri[:, :], MB16[:, n, :], start=n == 0, stop=True)
            for b in range(NT):
                mm = nc.tensor.matmul(PS[:, 7, 384:448], ones_b[:, :], MB16[:, b, :], start=b == 0, stop=b == NT - 1)
            mm.then_inc(S(g + "pos_mm"), 1)
            pe.wait_ge(S(g + "so_ready_a"), Z("so_ready_a") + NT)
            pe.wait_ge(S(g + "so_ready_v"), Z("so_ready_v") + NT)

            pe.wait_ge(S(g + "ends_ready"), Z("ends_ready") + 1)
            nc.tensor.matmul(PS[:, 7, 0:2 * P], ones_b[:, :], DG, start=True, stop=True).then_inc(S(g + "tab_mm"), 1)

            def pick(k, e):
                for n in range(NT):
                    mm = nc.tensor.matmul(PS[:, 7, 0:6], OH[k][:, n, :], RH[:, n, bass.ds(e, 1), :].rearrange("p a c -> p (a c)"),
                                          start=n == 0, stop=n == NT - 1)
                return mm

            pe.wait_ge(S(g + "tab_ready"), Z("tab_ready") + 1)
            pairs, most = pairs_of(pe, l)
            word = pe.value_load(words[0:1, 0:1], min_val=0, max_val=2 ** 14 - 1)
            for b in range(2):
                pe.wait_ge(S(f"oh_ready{l}"), b + 1)
                if b:
                    pe.wait_ge(S(f"idx_ready{l}"), b)
                pick(b, expert_of(pe, word, b)).then_inc(S(f"idx_mm{l}"), 1)
            pe.wait_ge(S(f"xg_in0_{l}"), 16)
            pe_transposes(XG[0], bank2(0), DC, S(f"xt_tp{l}"))
            with pe.Fori(0, most) as i:
                with pe.If(pairs - i > 0):
                    word = pe.value_load(words[0:1, bass.ds(i, 1)], min_val=0, max_val=2 ** 14 - 1)
                    ahead = pe.value_load(words[0:1, bass.ds(i + 1, 1)], min_val=0, max_val=2 ** 14 - 1)
                    for u in range(2):
                        b = i * 2 + u
                        e, e2 = expert_of(pe, word, u), expert_of(pe, ahead, u)
                        s = pe.snap(e & (NSLOT - 1), min_val=0, max_val=NSLOT - 1)
                        pe.wait_ge(S(f"w_ready{l}"), pe.snap(e + 1, min_val=1, max_val=EPAD))
                        pe.wait_ge(S(f"xt_ready{l}"), b + 1)
                        pe.wait_ge(S(f"h_ready{l}"), b + 1)
                        gu = RING4[:, bass.ds(s, 1), 0:2 * DC * FE].rearrange("p a (w j n) -> p (a w) j n", w=2, j=DC)
                        for j in range(DC):
                            mm = nc.tensor.matmul(PS[:, 2 + u, :], XT[u][:, j, :], gu[:, :, j, :], start=j == 0, stop=j == DC - 1)
                        mm.then_inc(S(f"gu_mm{l}"), 1)
                        pe.wait_ge(S(f"oh_ready{l}"), b + 3)
                        pe.wait_ge(S(f"idx_ready{l}"), b + 2)
                        pick(u, e2).then_inc(S(f"idx_mm{l}"), 1)
                        pe.wait_ge(S(f"xg_in{1 - u}_{l}"), i * 16 + 16 * (1 + u))
                        pe_transposes(XG[1 - u], bank2(0), DC, S(f"xt_tp{l}"))
                        pe.wait_ge(S(f"h_ready{l}"), b + 3)
                        pe.wait_ge(S(f"hht_ready{l}"), b + 1)
                        pe_transposes(HH[u], PS[:, 6, :], FC, S(f"h_tp{l}"))
                        pe.wait_ge(S(f"hht_ready{l}"), b + 2)
                        pe.wait_ge(S(f"out_a{l}"), b + 1)
                        pe.wait_ge(S(f"out_v{l}"), b + 1)
                        dn = RING4[:, bass.ds(s, 1), 2 * DC * FE:SLOT].rearrange("p a (j n) -> p (a j) n", j=FC)
                        for half in range(2):
                            for j in range(FC):
                                mm = nc.tensor.matmul(PS[:, 4 + half, :], HHT[u][:, j, :], dn[:, j, half * 512:(half + 1) * 512],
                                                      start=j == 0, stop=j == FC - 1)
                        mm.then_inc(S(f"dn_mm{l}"), 1)


        def s5_pe(pe):
            pe.wait_ge(S("s_hc_in"), B("s_hc_in") + 32)
            for n in range(GROUPS // 4):
                if n >= 4:
                    pe.wait_ge(S("s_u_ready"), B("s_u_ready") + n - 3)
                pe.wait_ge(S("s_hg_ready"), B("s_hg_ready") + n + 1)
                for k in range(4):
                    mm = nc.tensor.transpose(PS[:, n % 4, k * NCH:(k + 1) * NCH], HG[n % 2][0:NCH, k * P:(k + 1) * P], ident[0:NCH, 0:NCH])
                mm.then_inc(S("s_u_tp"), 1)
            pe.wait_ge(S("s_u_ready"), B("s_u_ready") + GROUPS // 4)
            units = Q // 4
            for n in range(units + 1):
                if n < units:
                    pe.wait_ge(S("s_w_ready"), B("s_w_ready") + n // 2 + 1)
                    if n >= 2:
                        pe.wait_ge(S("s_wt_ready"), B("s_wt_ready") + n - 1)
                    for k in range(4):
                        mm = nc.tensor.transpose(PS[:, 4 + n % 2, k * P:(k + 1) * P], WW[:, (4 * (n % 2) + k) * P:(4 * (n % 2) + k + 1) * P], ident[:, :])
                    mm.then_inc(S("s_w_tp"), 1)
                if n:
                    a = n - 1
                    pe.wait_ge(S("s_wt_ready"), B("s_wt_ready") + n)
                    if a >= 2:
                        pe.wait_ge(S("s_v_ready"), B("s_v_ready") + a - 1)
                    for k in range(4):
                        g = (4 * a + k) % GROUPS
                        mm = nc.tensor.matmul(PS[:, 6 + a % 2, k * NCH:(k + 1) * NCH], WT[:, 4 * (a % 2) + k, :], U[:, g, :], start=True, stop=True)
                    mm.then_inc(S("s_v_mm"), 1)
            pe.wait_ge(S("s_v_ready"), B("s_v_ready") + units)
            for n in range(GROUPS // QB):
                pe.wait_ge(S("s_cc_ready"), B("s_cc_ready") + n + 1)
                if n:
                    pe.wait_ge(S("s_kk_ready"), B("s_kk_ready") + n)
                for k in range(QB):
                    ps = PS[0:GI, k // 2, (k % 2) * 240:(k % 2 + 1) * 240]
                    nc.tensor.matmul(ps[:, 0:112], BB2[:, 1, k, :], CC[:, 1, k, 1:8, :].rearrange("p j i -> p (j i)"), start=True, stop=True)
                    nc.tensor.matmul(ps[:, 112:240], BB2[:, 0, k, :], CC[:, 0, k, 0:8, :].rearrange("p j i -> p (j i)"), start=True, stop=False)
                    mm = nc.tensor.matmul(ps[:, 112:128], BB2[:, 1, k, :], CC[:, 1, k, 8, :], start=False, stop=True)
                mm.then_inc(S("s_kk_mm"), 1)
                if n == 0:
                    pe.wait_ge(S("s_fwd_done"), B("s_fwd_done") + 1)
                    pe.wait_ge(S("s_bwd_done"), B("s_bwd_done") + 1)
                if n >= 2:
                    pe.wait_ge(S("s_y_ready"), B("s_y_ready") + n - 1)
                for k in range(QB):
                    g = n * QB + k
                    ps = PS[0:LC, 4 + 2 * (n % 2) + k // 4, (k % 4) * P:(k % 4 + 1) * P]
                    nc.tensor.matmul(ps, VST[:, 0:LC, g], CC[:, 0, k, 1:9, :].rearrange("p j i -> p (j i)"), start=k % 4 == 0, stop=False, skip_group_check=True)
                    nc.tensor.matmul(ps, VST[:, 2:LC + 2, GROUPS + g], CC[:, 1, k, 0:8, :].rearrange("p j i -> p (j i)"), start=False, stop=False, skip_group_check=True)
                pe.wait_ge(S("s_t_in"), B("s_t_in") + 16 * L * (n + 1))
                for k in range(QB):
                    g = n * QB + k
                    ps = PS[0:LC, 4 + 2 * (n % 2) + k // 4, (k % 4) * P:(k % 4 + 1) * P]
                    mm = nc.tensor.matmul(ps, U[:, g, 0:LC], TZ[:, g, :], start=False, stop=k % 4 == 3, skip_group_check=True)
                mm.then_inc(S("s_y_mm"), 1)
            for t in range(L):
                pe.wait_ge(S("s_gelu"), B("s_gelu") + t + 1)
                if t >= 4:
                    pe.wait_ge(S("s_yt"), B("s_yt") + t - 3)
                for j in range(DC):
                    mm = nc.tensor.transpose(PS[:, t % 4, j * LC:(j + 1) * LC], HC[0:LC, t, j::DC], ident[0:LC, 0:LC])
                mm.then_inc(S("s_yt_tp"), 1)
            pe.wait_ge(S("s_yt"), B("s_yt") + L)
            pe.wait_ge(S("s_y_ready"), B("s_y_ready") + GROUPS // QB)
            for n in range(2 * LT):
                h, m = n // LT, n % LT
                pe.wait_ge(S(f"s_wg_in{h}"), B(f"s_wg_in{h}") + 32)
                if n >= 2:
                    pe.wait_ge(S("s_z"), B("s_z") + n - 1)
                for w in range(2):
                    for j in range(DC):
                        mm = nc.tensor.matmul(PS[:, 4 + 2 * (n % 2) + w, :], YT[:, j, m * P:(m + 1) * P], WG[h][:, j, w, :], start=j == 0, stop=j == DC - 1)
                mm.then_inc(S("s_glu_mm"), 1)
            pe.wait_ge(S("s_z"), B("s_z") + 2 * LT)

        @block.tensor
        def _(pe):
            pe.wait_ge(S("cs_ready"), 1)
            pe.wait_ge(S("const_in"), 5 * 16)
            for n in range(2 * ADA_T):
                pe.wait_ge(S(f"ada_in{n % 4}"), 16 * (n // 4 + 1))
                if n >= 4:
                    pe.wait_ge(S("ada_ev"), n - 3)
                for j in range(DC):
                    mm = nc.tensor.matmul(PS[0:2, n % 4, :], csl[:, j, :], ada_slot(n)[:, j, :], start=j == 0, stop=j == DC - 1)
                mm.then_inc(S("ada_mm"), 1)
            pe.wait_ge(S("ada_ev"), 2 * ADA_T)
            pe.wait_ge(S("w_dqkv_in"), 16)
            for t in range(AT + 2):
                if t < AT:
                    pe.wait_ge(S("a_h_ready"), t + 1)
                    if t >= 1:
                        pe.wait_ge(S("a_ht"), 2 * t)
                    pe_transposes(H[t % 2], bank2(0), DC, S("a_tp"))
                if 1 <= t <= AT:
                    a = t - 1
                    pe.wait_ge(S("a_ht"), 2 * (a + 1))
                    if a >= 2:
                        pe.wait_ge(S("ca_ready"), a - 1)
                    for lo, hi in ((0, 512), (512, AW)):
                        for j in range(DC):
                            mm = nc.tensor.matmul(PS[:, 4 + 2 * (a % 2) + lo // 512, 0:hi - lo], HT[:, j, a * P:(a + 1) * P],
                                                  w_dqkv[:, j, lo:hi], start=j == 0, stop=j == DC - 1)
                    mm.then_inc(S("a_mm"), 1)
                if t >= 2:
                    a = t - 2
                    pe.wait_ge(S("ca_ready"), a + 1)
                    if a >= 1:
                        pe.wait_ge(S("ct_ready"), a)
                    ct = bank2(2)
                    for j in range(QC):
                        nc.tensor.transpose(ct[:, j * P:(j + 1) * P], CA[:, j:QL:QC], ident[:, :])
                    for j in range(KC):
                        nc.tensor.transpose(ct[:, (QC + j) * P:(QC + j + 1) * P], CA[:, QL + j:QL + KVL:KC], ident[:, :])
                    nc.tensor.transpose(ct[0:ROPE, (QC + KC) * P:(QC + KC + 1) * P], CA[:, QL + KVL:AW], ident[:, :])\
                        .then_inc(S("ct_tp"), 1)
            pe.wait_ge(S("ct_ready"), AT)
            pe.wait_ge(S("w_ukv_in"), 16)
            for n in range(2 * AT):
                t, half = n // 2, n % 2
                if n >= 4:
                    pe.wait_ge(S("v_ready_a"), (n - 3 + 1) // 2)
                    pe.wait_ge(S("v_ready_v"), (n - 3) // 2)
                for j in range(KC):
                    rhs = w_ukv[:, j, :].rearrange("p (h x) -> p h x", x=NOPE + VD)[:, 4 * half:4 * half + 4, NOPE:NOPE + VD]
                    mm = nc.tensor.matmul(PS[:, 4 + n % 4, :], CKT[:, j, t * P:(t + 1) * P], rhs, start=j == 0, stop=j == KC - 1)
                mm.then_inc(S("v_mm"), 1)

            def rotate(dst, src, done):
                nc.tensor.matmul(dst[:, 0:512], rot[:, :], src[:, 0:512], start=True, stop=True)
                nc.tensor.matmul(dst[:, 512:N_ALL], rot[:, :], src[:, 512:N_ALL], start=True, stop=True).then_inc(done, 1)

            pe.wait_ge(S("v_ready_a"), AT)
            pe.wait_ge(S("v_ready_v"), AT)
            rotate(bank2(6)[0:ROPE], KPT, S("k_rot"))
            pe.wait_ge(S("w_uq_in"), 16)

            def project(dst, w, col, m, src, n, done):
                for lo, hi in ((0, 512), (512, N_ALL)):
                    for j in range(n):
                        mm = nc.tensor.matmul(dst[0:m, lo:hi], w[:, j, col:col + m], src[:, j, lo:hi], start=j == 0, stop=j == n - 1)
                mm.then_inc(done, 1)

            for h in range(HEADS):
                if h:
                    pe.wait_ge(S("p_ready"), AT * h)
                    pe.wait_ge(S("pt_ready"), AT * h)
                    pe.wait_ge(S("q_rope"), h)
                project(bank2(4), w_uq, h * (NOPE + ROPE) + NOPE, ROPE, CQT, QC, S("qp_mm"))
                project(bank2(0), w_uq, h * (NOPE + ROPE), NOPE, CQT, QC, S("qn_mm"))
                project(bank2(2), w_ukv, h * (NOPE + VD), NOPE, CKT, KC, S("kn_mm"))
                pe.wait_ge(S("qp_ready"), h + 1)
                if h == 0:
                    pe.wait_ge(S("k_rope"), 1)
                if h:
                    pe.wait_ge(S("ot_lat"), h)
                    pe.wait_ge(S("ot_ctx"), h)
                rotate(bank2(6)[0:ROPE], qpT, S("q_rot"))
                pe.wait_ge(S("qn_ready"), h + 1)
                pe.wait_ge(S("kn_ready"), h + 1)
                pe.wait_ge(S("q_rope"), h + 1)
                for t in range(AT + 1):
                    if t < AT:
                        k = h * AT + t
                        if k >= 2:
                            pe.wait_ge(S("p_exp"), k - 1)
                        q0, nk = (N_CTX + t * P, N_ALL) if t < LT else ((t - LT) * P, N_CTX)
                        dst = bank2(2 * (t % 2))
                        for lo, hi in ((0, 512), (512, N_ALL)):
                            hi = min(hi, nk)
                            if lo < hi:
                                nc.tensor.matmul(dst[:, lo:hi], qnT[:, q0:q0 + P], knT[:, lo:hi], start=True, stop=False)
                                mm = nc.tensor.matmul(dst[:, lo:hi], qpR[:, q0:q0 + P], KPR[:, lo:hi], start=False, stop=True)
                        mm.then_inc(S("s_mm"), 1)
                    if t >= 1:
                        k = h * AT + t - 1
                        pe.wait_ge(S("p_ready"), k + 1)
                        if k:
                            pe.wait_ge(S("pt_ready"), k)
                        nk = AT if t - 1 < LT else CT
                        for c in range(nk):
                            mm = nc.tensor.transpose(bank2(4)[:, c * P:(c + 1) * P], PR[(t - 1) % 2][:, c * P:(c + 1) * P], ident[:, :])
                        mm.then_inc(S("p_tp"), 1)
                    if t == LT:
                        pe.wait_ge(S("pt_ready"), h * AT + LT)
                        for c in range(AT):
                            mm = nc.tensor.matmul(PS[:, 6, :], V[:, c, h * P:(h + 1) * P], PT[:, c, :], start=c == 0, stop=c == AT - 1)
                        mm.then_inc(S("pv_lat"), 1)
                pe.wait_ge(S("pt_ready"), (h + 1) * AT)
                for c in range(CT):
                    mm = nc.tensor.matmul(PS[:, 7, 0:N_CTX], V[:, c, h * P:(h + 1) * P], PT[:, c, 0:N_CTX], start=c == 0, stop=c == CT - 1)
                mm.then_inc(S("pv_ctx"), 1)
            pe.wait_ge(S("w_o_in"), 16)
            pe.wait_ge(S("ot_lat"), HEADS)
            pe.wait_ge(S("ot_ctx"), HEADS)
            for t in range(AT):
                if t >= 2:
                    pe.wait_ge(S("o_used"), t - 1)
                for half in range(2):
                    for h in range(HEADS):
                        mm = nc.tensor.matmul(PS[:, 2 * (t % 2) + half, :], OT[:, h, t * P:(t + 1) * P],
                                              w_o[:, h, half * 512:(half + 1) * 512], start=h == 0, stop=h == HEADS - 1)
                mm.then_inc(S("o_mm"), 1)
            pe.wait_ge(S("o_used"), AT)
            moe_pe(pe, 0)
            s5_pe(pe)
            moe_pe(pe, 1)

        def moe_act(act, A, l):
            tiles, NT = TILES[l], len(TILES[l])
            g, Z = "m_", before_moe(l)
            for n in range(NT):
                act.wait_ge(S("x1_ready") if l == 0 else S("x3_ready"), n + 1 + (B("x3_ready") if l else 0))
                A(act.activation(junk[:, :], X[:, n, :], ACT.Square, accum_out=ss[:, n:n + 1]))
            act.activation(sd[:, 0:NT], ss[:, 0:NT], ACT.Sqrt, scale=1.0 / D, bias=eps[:, 0:1]).then_inc(S(g + "sd"), 1)
            for n in range(NT):
                act.wait_ge(S(g + "ht_tp"), Z("ht_tp") + n + 1)
                for k in range(2):
                    act.activation(HT[:, 4 * k:4 * k + 4, n * P:(n + 1) * P],
                                   PS[:, 2 * (n % 2) + k, :].rearrange("p (j n) -> p j n", j=4), ACT.Copy).then_inc(S(g + "ht_ready"), 1)
            act.wait_ge(S(g + "logits"), Z("logits") + NT)
            act.activation(SC[:, 0:NT, :], PS[:, 7, 0:NT * 64].rearrange("p (t e) -> p t e", t=NT), ACT.Sigmoid).then_inc(S(g + "scores"), 1)
            for n in range(NT):
                act.wait_ge(S(g + "sh_gu"), Z("sh_gu") + n + 1)
                if n >= 2:
                    act.wait_ge(S(g + "sh_h"), Z("sh_h") + n - 1)
                act.activation(SG[n % 2], PS[:, 4 + n % 2, 0:FE], ACT.Silu).then_inc(S(g + "sh_silu"), 1)
                act.wait_ge(S(g + "sh_down"), Z("sh_down") + n + 1)
                if n == 0:
                    for k in range(2):
                        act.wait_ge(S(g + f"f_out{k}"), Z(f"f_out{k}") + NT // 2 * 16)
                if n >= 2:
                    act.wait_ge(S(g + f"acc_out{n % 2}"), Z(f"acc_out{n % 2}") + n // 2 * 16)
                act.activation(H[n % 2][:, 0:512], PS[:, 2 * (n % 2), :], ACT.Copy).then_inc(S(g + "so_ready_a"), 1)

            act.sem_inc(S(f"out_a{l}"), 1)
            act.wait_ge(S(g + "sh_down"), Z("sh_down") + NT)
            act.wait_ge(S(f"xt_tp{l}"), 1)
            act.activation(XT[0], bank2(0).rearrange("p (j n) -> p j n", j=DC), ACT.Copy).then_inc(S(f"xt_ready{l}"), 1)
            pairs, most = pairs_of(act, l)
            with act.Fori(0, most) as i:
                with act.If(pairs - i > 0):
                    for u in range(2):
                        b = i * 2 + u
                        act.wait_ge(S(f"gu_mm{l}"), b + 1)
                        act.activation(SG[u], PS[:, 2 + u, 0:FE], ACT.Silu).then_inc(S(f"silu{l}"), 1)
                        act.wait_ge(S(f"xt_tp{l}"), b + 2)
                        act.activation(XT[1 - u], bank2(0).rearrange("p (j n) -> p j n", j=DC), ACT.Copy).then_inc(S(f"xt_ready{l}"), 1)
                        act.wait_ge(S(f"dn_mm{l}"), b + 1)
                        act.wait_ge(S(f"kept{l}"), b + 1)
                        act.activation(OS[u][:, 0:512], PS[:, 4, :], ACT.Copy, scale=gates[:, u:u + 1]).then_inc(S(f"out_a{l}"), 1)
            for n in range(NT):
                act.wait_ge(S(g + f"acc_in{n % 2}"), Z(f"acc_in{n % 2}") + 16 * (n // 2 + 1))
                A(act.activation(junk[:, :], OS[n % 2], ACT.Square, accum_out=ss[:, n:n + 1]))
                act.activation(sd[:, n:n + 1], ss[:, n:n + 1], ACT.Sqrt, scale=1.0 / D, bias=eps[:, 0:1]).then_inc(S(g + "o_sd"), 1)


        def s5_act(act, A):
            for t in range(AT):
                act.wait_ge(S("m_x_ready"), t + 1)
                A(act.activation(junk[:, :], X[:, t, :], ACT.Square, accum_out=ss[:, t:t + 1]))
            act.activation(sd[:, 0:AT], ss[:, 0:AT], ACT.Sqrt, scale=1.0 / D, bias=eps[:, 0:1]).then_inc(S("s_sd"), 1)
            act.wait_ge(S("s_par_in"), B("s_par_in") + 16)
            act.activation(tEA, LST, ACT.Exp).then_inc(S("s_tab_a"), 1)
            act.wait_ge(S("s_tab_v"), B("s_tab_v") + 1)
            act.activation(tEA, tA, ACT.Exp).then_inc(S("s_tab_a"), 1)
            act.activation(tR, tR, ACT.Sin).then_inc(S("s_tab_a"), 1)
            act.activation(tR2, tR2, ACT.Sin).then_inc(S("s_tab_a"), 1)
            for n in range(GROUPS // 4):
                act.wait_ge(S("s_u_tp"), B("s_u_tp") + n + 1)
                act.activation(U[:, 4 * n:4 * n + 4, :], PS[:, n % 4, 0:4 * NCH].rearrange("p (g c) -> p g c", g=4), ACT.Copy)\
                    .then_inc(S("s_u_ready"), 1)
            units = Q // 4
            for n in range(units + 1):
                if n < units:
                    act.wait_ge(S("s_w_tp"), B("s_w_tp") + n + 1)
                    if n >= 2:
                        act.wait_ge(S("s_v_mm"), B("s_v_mm") + n - 1)
                    act.activation(WT[:, 4 * (n % 2):4 * (n % 2) + 4, :], PS[:, 4 + n % 2, :].rearrange("p (k n) -> p k n", k=4), ACT.Copy)\
                        .then_inc(S("s_wt_ready"), 1)
                if n:
                    a = n - 1
                    act.wait_ge(S("s_v_mm"), B("s_v_mm") + n)
                    act.activation(VST[:, 1:NCH + 1, 4 * a:4 * a + 4].rearrange("p s q -> p q s"),
                                   PS[:, 6 + a % 2, 0:4 * NCH].rearrange("p (q s) -> p q s", q=4), ACT.Copy).then_inc(S("s_v_ready"), 1)
            for n in range(GROUPS // QB):
                act.wait_ge(S("s_kk_mm"), B("s_kk_mm") + n + 1)
                if n == 0:
                    act.wait_ge(S("s_hd"), B("s_hd") + 1)
                else:
                    act.wait_ge(S("s_t_in"), B("s_t_in") + 16 * L * n)
                act.activation(KKS.rearrange("p (b w) n -> p b (w n)", w=2), PS[0:GI, 0:4, 0:480], ACT.Copy).then_inc(S("s_kk_ready"), 1)
            act.wait_ge(S("s_y_ready"), B("s_y_ready") + GROUPS // QB)
            for t in range(L):
                act.activation(HC[0:LC, t, :], HC[0:LC, t, :], ACT.Gelu_apprx_tanh).then_inc(S("s_gelu"), 1)
            for n in range(2 * LT):
                act.wait_ge(S("s_z"), B("s_z") + n + 1)
                act.activation(ZT[n % 2][:, 512:1024], ZT[n % 2][:, 512:1024], ACT.Sigmoid).then_inc(S("s_sig"), 1)
            for m in range(LT):
                act.wait_ge(S("s_oo"), B("s_oo") + LT + m + 1)
                A(act.activation(junk[:, :], OO[:, m, :], ACT.Square, accum_out=ss[:, 8 + m:9 + m]))
                act.activation(sd[:, 8 + m:9 + m], ss[:, 8 + m:9 + m], ACT.Sqrt, scale=1.0 / D, bias=eps[:, 0:1]).then_inc(S("s_osd"), 1)

        @block.scalar
        def _(act):
            A = Steps(act, S("act_step"))
            act.wait_ge(S("const_in"), 5 * 16)
            act.activation(csl[:, :, :], cs[:, :, :], ACT.Silu).then_inc(S("cs_ready"), 1)
            for t in range(AT):
                act.wait_ge(S("x_in"), 16 * AT)
                A(act.activation(junk[:, :], X[:, t, :], ACT.Square, accum_out=ss[:, t:t + 1]))
            act.wait_ge(S("eps_ready"), 1)
            act.activation(sd[:, 0:AT], ss[:, 0:AT], ACT.Sqrt, scale=1.0 / D, bias=eps[:, 0:1]).then_inc(S("a_sd"), 1)
            act.wait_ge(S("mod_out"), 32)
            for t in range(AT + 1):
                if t < AT:
                    act.wait_ge(S("a_tp"), t + 1)
                    for k in range(2):
                        act.activation(HT[:, 4 * k:4 * k + 4, t * P:(t + 1) * P],
                                       PS[:, k, :].rearrange("p (j n) -> p j n", j=4), ACT.Copy).then_inc(S("a_ht"), 1)
                if t:
                    a = t - 1
                    b = 4 + 2 * (a % 2)
                    act.wait_ge(S("a_mm"), a + 1)
                    if a:
                        act.wait_ge(S("c_sd"), a)
                    act.activation(junk[:, 0:QL], bank2(b)[:, 0:QL], ACT.Square, scale=QL ** -0.5, accum_out=ss[:, 0:1])
                    A(act.activation(junk[:, QL:QL + KVL], bank2(b)[:, QL:QL + KVL], ACT.Square, scale=KVL ** -0.5, accum_out=ss[:, 1:2]))
                    if a:
                        act.wait_ge(S("ca_ready"), a)
                    act.activation(sd[:, 6:8], ss[:, 0:2], ACT.Sqrt, bias=eps[:, 0:1]).then_inc(S("c_sd"), 1)
            for n in range(0, 2 * AT, 2):
                act.wait_ge(S("v_mm"), n + 1)
                act.activation(V[:, n // 2, 0:512], PS[:, 4 + n % 4, :], ACT.Copy).then_inc(S("v_ready_a"), 1)
            for h in range(HEADS):
                act.wait_ge(S("qp_mm"), h + 1)
                act.activation(qpT, bank2(4, N_ALL)[0:ROPE], ACT.Copy).then_inc(S("qp_ready"), 1)
                act.wait_ge(S("qn_mm"), h + 1)
                act.activation(qnT, bank2(0, N_ALL), ACT.Copy).then_inc(S("qn_ready"), 1)
                for t in range(AT + 1):
                    if t < AT:
                        k = h * AT + t
                        nk = N_ALL if t < LT else N_CTX
                        act.wait_ge(S("nmax"), k + 1)
                        if k >= 2:
                            act.wait_ge(S("p_tp"), k - 1)
                        act.activation(PR[t % 2][:, 0:nk], bank2(2 * (t % 2), nk), ACT.Exp, bias=mx[:, t % 2:t % 2 + 1],
                                       scale=SCALE, accum_out=sm[:, t % 2:t % 2 + 1]).then_inc(S("p_exp"), 1)
                    if t:
                        k = h * AT + t - 1
                        nk = AT if t - 1 < LT else CT
                        act.wait_ge(S("p_tp"), k + 1)
                        if t - 1 == 0 and h:
                            act.wait_ge(S("pv_ctx"), h)
                        if t - 1 == LT:
                            act.wait_ge(S("pv_lat"), h + 1)
                        q0 = (t - 1) * P if t - 1 < LT else (t - 1 - LT) * P
                        act.activation(PT[:, 0:nk, q0:q0 + P], bank2(4, nk * P).rearrange("p (c q) -> p c q", c=nk), ACT.Copy)\
                            .then_inc(S("pt_ready"), 1)
                act.wait_ge(S("pv_lat"), h + 1)
                act.activation(OT[:, h, N_CTX:N_ALL], PS[:, 6, :], ACT.Copy).then_inc(S("ot_lat"), 1)
                act.wait_ge(S("pv_ctx"), h + 1)
                act.activation(OT[:, h, 0:N_CTX], PS[:, 7, 0:N_CTX], ACT.Copy).then_inc(S("ot_ctx"), 1)
            for t in range(AT):
                act.wait_ge(S("o_mm"), t + 1)
                A(act.activation(junk[:, :], bank2(2 * (t % 2)), ACT.Square, accum_out=ss[:, 2 + t:3 + t]))
                act.activation(sd[:, 8 + t:9 + t], ss[:, 2 + t:3 + t], ACT.Sqrt, scale=1.0 / D, bias=eps[:, 0:1]).then_inc(S("o_sd"), 1)
            moe_act(act, A, 0)
            s5_act(act, A)
            moe_act(act, A, 1)

        def moe_dve(v, W, modulated, l):
            tiles, NT = TILES[l], len(TILES[l])
            g, Z = "m_", before_moe(l)
            v.wait_ge(S(g + "sd"), Z("sd") + 1)
            W(v.reciprocal(rs[:, 0:NT], sd[:, 0:NT]))
            v.wait_ge(S("rows_m") if l == 0 else S("s_rown"), 64 if l == 0 else B("s_rown") + 32)

            def h_free(n):
                v.wait_ge(S(g + "ht_tp"), Z("ht_tp") + n - 1)
                v.wait_ge(S(g + f"f_out{n % 2}"), Z(f"f_out{n % 2}") + n // 2 * 16)

            for n, t in enumerate(tiles):
                modulated(n, t, stream[t] if l == 0 else 0, h_free, S(g + "h_ready"))
            v.wait_ge(S(g + "h_ready"), Z("h_ready") + NT)
            W(v.memset(row(0), 0.0))
            v.sem_inc(S(g + "zero_ready"), 1)
            v.memset(GS[:, :, 8:16], BIG)
            v.memset(TR[:, :, 4:8], BIG)
            v.memset(POSM[:, :, N_EXP:EPAD], -1.0)
            v.memset(RH[:, :, N_EXP:EPAD, :], 0.0)
            v.memset(RH[:, :, 0:N_EXP, 0:1], 1.0)
            for n in range(NT):
                v.memset(RH[:, n, 0:N_EXP, 2:3], float(n))
            v.tensor_copy(RH[:, 0:NT, 0:N_EXP, 1:2], cst[:, 0:1].unsqueeze(2).unsqueeze(3).to_broadcast((P, NT, N_EXP, 1)))
            v.wait_ge(S(g + "scores"), Z("scores") + 1)
            N = slice(0, NT)
            W(v.tensor_tensor(BI[:, N], SC[:, N], BROW[:, :].unsqueeze(1).to_broadcast((P, NT, N_EXP)), ALU.add))
            for n in range(NT):
                for q in range(8):
                    ins = v.max(M8[:, n, q, :], BI[:, n, q * 8:(q + 1) * 8])
            W(ins)
            W(v.tensor_tensor(GS[:, N, 0:8], M8[:, N, :, 0], M8[:, N, :, 1], ALU.add))
            for n in range(NT):
                ins = v.max(G8[:, n, :], GS[:, n, 0:8])
            W(ins)
            W(v.tensor_copy(TR[:, N, 0:4], G8[:, N, 0:4]))
            for n in range(NT):
                ins = v.match_replace(GR[:, n, :], TR[:, n, :], GS[:, n, :], -BIG)
            W(ins)
            W(v.tensor_scalar(GM[:, N], GR[:, N, 0:8], -BIG, None, ALU.is_equal))
            W(v.tensor_scalar(TB[:, N], GM[:, N], BIG, -BIG, ALU.mult, ALU.add))
            for n in range(NT):
                b3 = BI[:, n, :].rearrange("p (q k) -> p q k", q=8)
                ins = v.tensor_tensor(b3, b3, GM[:, n, :].unsqueeze(2).to_broadcast((P, 8, 8)), ALU.mult)
            W(ins)
            for n in range(NT):
                b3 = BI[:, n, :].rearrange("p (q k) -> p q k", q=8)
                ins = v.tensor_tensor(b3, b3, TB[:, n, :].unsqueeze(2).to_broadcast((P, 8, 8)), ALU.add)
            W(ins)
            for n in range(NT):
                ins = v.max(E8[:, n, :], BI[:, n, :])
            W(ins)
            for n in range(NT):
                ins = v.match_replace(MR[:, n, :], E8[:, n, :], BI[:, n, :], -2 * BIG)
            W(ins)
            W(v.tensor_scalar(MR[:, N], MR[:, N], -2 * BIG, None, ALU.is_equal))
            W(v.tensor_copy(MB16[:, N], MR[:, N]))
            v.sem_inc(S(g + "mask_ready"), 1)
            W(v.tensor_tensor(GTE[:, N], SC[:, N], MR[:, N], ALU.mult))
            W(v.tensor_reduce(sm[:, 0:NT], GTE[:, N], AX_X, ALU.add))
            W(v.reciprocal(sm[:, 0:NT], sm[:, 0:NT]))
            W(v.tensor_tensor(GTE[:, N], GTE[:, N], sm[:, 0:NT].unsqueeze(2).to_broadcast((P, NT, N_EXP)), ALU.mult))
            W(v.tensor_scalar(GTE[:, N], GTE[:, N], ROUTED, None, ALU.mult))
            for c in (3, 4, 5):
                W(v.tensor_copy(RH[:, N, 0:N_EXP, c], GTE[:, N]))
                if c < 5:
                    W(v.tensor_tensor(GTE[:, N], GTE[:, N], RH[:, N, 0:N_EXP, c], ALU.subtract))
            for n in range(NT):
                v.wait_ge(S(g + "sh_silu"), Z("sh_silu") + n + 1)
                if n >= 2:
                    v.wait_ge(S(g + "sh_tp"), Z("sh_tp") + n - 1)
                v.tensor_tensor(HH[n % 2], SG[n % 2], PS[:, 4 + n % 2, FE:2 * FE], ALU.mult).then_inc(S(g + "sh_h"), 1)
                v.wait_ge(S(g + "sh_tp"), Z("sh_tp") + n + 1)
                if n >= 2:
                    v.wait_ge(S(g + "sh_down"), Z("sh_down") + n - 1)
                v.tensor_copy(HHT[n % 2], PS[:, 6, 0:FE].rearrange("p (j n) -> p j n", j=FC)).then_inc(S(g + "sh_ht"), 1)
                v.wait_ge(S(g + "sh_down"), Z("sh_down") + n + 1)
                if n == 0:
                    for k in range(2):
                        v.wait_ge(S(g + f"f_out{k}"), Z(f"f_out{k}") + NT // 2 * 16)
                if n >= 2:
                    v.wait_ge(S(g + f"acc_out{n % 2}"), Z(f"acc_out{n % 2}") + n // 2 * 16)
                v.tensor_copy(H[n % 2][:, 512:1024], PS[:, 2 * (n % 2) + 1, :]).then_inc(S(g + "so_ready_v"), 1)

            v.wait_ge(S(g + "pos_mm"), Z("pos_mm") + 1)
            pos = PS[:, 7, 0:NT * 64].rearrange("p (t e) -> p t e", t=NT)
            W(v.scalar_tensor_tensor(POSM[:, N, 0:N_EXP], pos, 1.0, MR[:, N], ALU.add, ALU.mult))
            W(v.tensor_scalar(POSM[:, N, 0:N_EXP], POSM[:, N, 0:N_EXP], -1.0, None, ALU.add))
            W(v.tensor_copy(CNT, PS[:, 7, 384:448]))
            W(v.tensor_scalar(NB, CNT, float(P), 1.0, ALU.is_gt, ALU.add))
            for b in range(2, NT):
                W(v.scalar_tensor_tensor(NB, CNT, float(P * b), NB, ALU.is_gt, ALU.add))
            W(v.tensor_tensor_scan(END, cst[:, 72:73].to_broadcast((P, N_EXP)), NB, 0.0, ALU.mult, ALU.add))
            v.tensor_copy(ends[0:1, :], END[0:1, :])
            W(v.tensor_scalar(CNT, END, cst[:, 0:1], None, ALU.is_le))
            v.tensor_reduce(TAB[:, 0:1], CNT, AX_X, ALU.add)
            W(v.tensor_tensor(CNT, CNT, NB, ALU.mult))
            W(v.tensor_reduce(TAB[:, 1:2], CNT, AX_X, ALU.add))
            W(v.tensor_scalar(TAB[:, 1:2], TAB[:, 1:2], cst[:, 0:1], -float(P), ALU.subtract, ALU.mult))
            v.tensor_scalar(DG[:, 0:P], ident[:, :], TAB[:, 0:1], None, ALU.mult)
            W(v.tensor_scalar(DG[:, P:2 * P], ident[:, :], TAB[:, 1:2], None, ALU.mult))
            v.sem_inc(S(g + "ends_ready"), 1)
            v.wait_ge(S(g + "tab_mm"), Z("tab_mm") + 1)
            v.tensor_copy(SHIFT, PS[:, 7, P:2 * P])
            experts = PS[0:1, 7, 0:P].rearrange("p (a b) -> p a b", b=2)
            W(v.tensor_copy(CNT[0:1, :], experts[:, :, 0]))
            W(v.scalar_tensor_tensor(CNT[0:1, :], experts[:, :, 1], float(P), CNT[0:1, :], ALU.mult, ALU.add))
            W(v.tensor_copy(words[0:1, :], CNT[0:1, :]))
            v.sem_inc(S(g + "tab_ready"), 1)
            trash = 2 + l

            def slots(u, done, W):
                W(v.tensor_copy(it[:, 0:6], PS[:, 7, 0:6]))
                W(v.scalar_tensor_tensor(it[:, 6:7], it[:, 2:3], float(P), it[:, 1:2], ALU.mult, ALU.add))
                W(v.scalar_tensor_tensor(it[:, 6:7], it[:, 0:1], cst[:, trash + 2:trash + 3], it[:, 6:7], ALU.mult, ALU.add))
                v.tensor_tensor(it[:, 7:8], it[:, 4:5], it[:, 5:6], ALU.add)
                W(v.tensor_scalar(idxg[:, u:u + 1], it[:, 6:7], cst[:, trash:trash + 1], None, ALU.add))
                v.tensor_tensor(gateg[:, u:u + 1], it[:, 7:8], it[:, 3:4], ALU.add).then_inc(done, 1)

            def one_hot(k, e, b):
                for n in range(NT):
                    ins = v.tensor_scalar(OH[k][:, n, :], iota_b[:, :], SHIFT[:, bass.ds(b, 1)], POSM[:, n, bass.ds(e, 1)], ALU.add, ALU.is_equal)
                ins.then_inc(S(f"oh_ready{l}"), 1)

            v.sem_inc(S(f"h_ready{l}"), 2)
            v.sem_inc(S(f"hht_ready{l}"), 1)
            v.sem_inc(S(f"out_v{l}"), 1)
            pairs, most = pairs_of(v, l)
            word = v.value_load(words[0:1, 0:1], min_val=0, max_val=2 ** 14 - 1)
            for b in range(2):
                one_hot(b, expert_of(v, word, b), b)
                v.wait_ge(S(f"idx_mm{l}"), b + 1)
                slots(b, S(f"idx_ready{l}"), W)
            LW = Steps(v, S(f"slot_step{l}"))
            with v.Fori(0, most) as i:
                with v.If(pairs - i > 0):
                    ahead = v.value_load(words[0:1, bass.ds(i + 1, 1)], min_val=0, max_val=2 ** 14 - 1)
                    LW.enter(i, 10)
                    for u in range(2):
                        b = i * 2 + u
                        e2 = expert_of(v, ahead, u)
                        b2 = v.snap(b + 2, min_val=2, max_val=P - 1)
                        v.wait_ge(S(f"idx_mm{l}"), b + 1)
                        one_hot(u, e2, b2)
                        v.wait_ge(S(f"silu{l}"), b + 1)
                        v.tensor_tensor(HH[u], SG[u], PS[:, 2 + u, FE:2 * FE], ALU.mult).then_inc(S(f"h_ready{l}"), 1)
                        v.wait_ge(S(f"h_tp{l}"), b + 1)
                        v.tensor_copy(HHT[u], PS[:, 6, 0:FE].rearrange("p (j n) -> p j n", j=FC)).then_inc(S(f"hht_ready{l}"), 1)
                        v.wait_ge(S(f"os_free{l}"), b + 1)
                        v.wait_ge(S(f"idx_ready{l}"), b + 1)
                        v.tensor_copy(idxs[:, u:u + 1], idxg[:, u:u + 1])
                        LW(v.tensor_copy(gates[:, u:u + 1], gateg[:, u:u + 1]))
                        v.sem_inc(S(f"kept{l}"), 1)
                        v.wait_ge(S(f"idx_mm{l}"), b + 3)
                        v.wait_ge(S(f"xt_tp{l}"), b + 1)
                        slots(u, S(f"idx_ready{l}"), LW)
                        v.wait_ge(S(f"dn_mm{l}"), b + 1)
                        v.tensor_scalar(OS[u][:, 512:1024], PS[:, 5, :], gates[:, u:u + 1], None, ALU.mult).then_inc(S(f"out_v{l}"), 1)
            v.wait_ge(S(g + "rows_in"), Z("rows_in") + 32 if l == 0 else 16)
            for n, t in enumerate(tiles):
                v.wait_ge(S(g + "o_sd"), Z("o_sd") + n + 1)
                W(v.reciprocal(rs[:, n:n + 1], sd[:, n:n + 1]))
                W(v.scalar_tensor_tensor(OS[n % 2], OS[n % 2], rs[:, n:n + 1], row(stream[t] if l == 0 else 0), ALU.mult, ALU.mult))
                v.tensor_tensor(X[:, t, :], X[:, t, :], OS[n % 2], ALU.add).then_inc(S(g + "x_ready"), 1)


        def s5_dve(v, W, modulated):
            v.wait_ge(S("s_sd"), B("s_sd") + 1)
            W(v.reciprocal(rs[:, 0:AT], sd[:, 0:AT]))
            v.wait_ge(S("s_rows"), B("s_rows") + 64)
            for t in range(AT):
                modulated(t, t, stream[t], lambda n: v.wait_ge(S(f"s_h_out{n % 2}"), B(f"s_h_out{n % 2}") + n // 2 * 16), S("s_h_ready"))
            v.wait_ge(S("s_tab_a"), B("s_tab_a") + 1)
            v.tensor_tensor(tA, LRE, tEA, ALU.mult)
            W(v.tensor_tensor(tTH, LIM, tEA, ALU.mult))
            W(v.tensor_scalar(tK, tTH, 1.0 / TWO_PI, ROUND, ALU.mult, ALU.add))
            W(v.tensor_scalar(tK, tK, -ROUND, None, ALU.add))
            W(v.scalar_tensor_tensor(tR, tK, -PI_A, tTH, ALU.mult, ALU.add))
            W(v.scalar_tensor_tensor(tR, tK, -PI_B, tR, ALU.mult, ALU.add))
            W(v.scalar_tensor_tensor(tR, tK, -PI_C, tR, ALU.mult, ALU.add))
            W(v.tensor_scalar(tR2, tR, 0.5 * np.pi, None, ALU.add))
            W(v.tensor_scalar(tM, tR2, float(np.pi), -TWO_PI, ALU.is_gt, ALU.mult))
            W(v.tensor_tensor(tR2, tR2, tM, ALU.add))
            v.tensor_scalar(tR, tR, 3.1415925, -3.1415925, ALU.min, ALU.max)
            W(v.tensor_scalar(tR2, tR2, 3.1415925, -3.1415925, ALU.min, ALU.max))
            v.sem_inc(S("s_tab_v"), 1)
            v.memset(NR[:, 0, :], 1.0)
            v.memset(NI[:, 0, :], 0.0)
            v.wait_ge(S("s_tab_a"), B("s_tab_a") + 4)
            v.tensor_tensor(NR[:, 1, :], tEA, tR2, ALU.mult)
            W(v.tensor_tensor(NI[:, 1, :], tEA, tR, ALU.mult))

            def cmul(dr, di, ar, ai, br, bi, t1, t2):
                v.tensor_tensor(dr, ar, br, ALU.mult)
                v.tensor_tensor(t1, ai, bi, ALU.mult)
                v.tensor_tensor(di, ar, bi, ALU.mult)
                W(v.tensor_tensor(t2, ai, br, ALU.mult))
                v.tensor_tensor(dr, dr, t1, ALU.subtract)
                W(v.tensor_tensor(di, di, t2, ALU.add))

            for k in range(2, L + 1):
                cmul(NR[:, k, :], NI[:, k, :], NR[:, k - 1, :], NI[:, k - 1, :], NR[:, 1, :], NI[:, 1, :], tM, tN)
            v.tensor_scalar(tK, NR[:, 1, :], -1.0, None, ALU.add)
            v.tensor_tensor(tR, LRE, LRE, ALU.mult)
            W(v.tensor_tensor(tR2, LIM, LIM, ALU.mult))
            W(v.tensor_tensor(tR, tR, tR2, ALU.add))
            W(v.reciprocal(tR, tR))
            v.tensor_tensor(tFR, tK, LRE, ALU.mult)
            v.tensor_tensor(tM, NI[:, 1, :], LIM, ALU.mult)
            v.tensor_tensor(tFI, NI[:, 1, :], LRE, ALU.mult)
            W(v.tensor_tensor(tN, tK, LIM, ALU.mult))
            v.tensor_tensor(tFR, tFR, tM, ALU.add)
            W(v.tensor_tensor(tFI, tFI, tN, ALU.subtract))
            v.tensor_tensor(tFR, tFR, tR, ALU.mult)
            W(v.tensor_tensor(tFI, tFI, tR, ALU.mult))
            n8 = slice(0, L)
            tm = TMP[:, 0:1024].rearrange("p (j q) -> p j q", q=Q)

            def wide(t):
                return t.unsqueeze(1).to_broadcast((P, L, Q))

            v.tensor_tensor(GR_, NR[:, n8], wide(tFR), ALU.mult)
            v.tensor_tensor(GI_, NR[:, n8], wide(tFI), ALU.mult)
            W(v.tensor_tensor(tm, NI[:, n8], wide(tFI), ALU.mult))
            W(v.tensor_tensor(GR_, GR_, tm, ALU.subtract))
            W(v.tensor_tensor(tm, NI[:, n8], wide(tFR), ALU.mult))
            W(v.tensor_tensor(GI_, GI_, tm, ALU.add))
            mt, mb, nmt, nmb = (cst[:, k:k + 1] for k in (6, 7, 73, 74))

            def halves(dst, a, a_scale, b, b_scale):
                W(v.tensor_scalar(dst, a, a_scale, None, ALU.mult))
                W(v.scalar_tensor_tensor(dst, b, b_scale, dst, ALU.mult, ALU.add))

            f, b = slice(0, GROUPS), slice(GROUPS, Q)
            for d, q, step in ((X1, f, 1), (X1, b, -1)):
                halves(X1[:, :, q], NR[:, ::step, q], mt, NI[:, ::step, q], nmb)
                halves(X2[:, :, q], NI[:, ::step, q], nmt, NR[:, ::step, q], nmb)
                halves(Y1[:, :, q], GR_[:, ::-step, q], mt, GI_[:, ::-step, q], mb)
                halves(Y2[:, :, q], GI_[:, ::-step, q], nmt, GR_[:, ::-step, q], mb)
            halves(F1, tFR, mt, tFI, mb)
            halves(F2, tFI, nmt, tFR, mb)
            halves(tSMI, NI[:, L, :], mt, NI[:, L, :], nmb)
            v.sem_inc(S("s_tab_ready"), 1)

            def scaled_sum(dst, tmp, a0, a1, b0, b1):
                v.tensor_tensor(dst, a0, a1, ALU.mult)
                W(v.tensor_tensor(tmp, b0, b1, ALU.mult))
                return v.tensor_tensor(dst, dst, tmp, ALU.add)

            for n in range(Q // QB):
                v.wait_ge(S(f"s_b_in{n % 2}"), B(f"s_b_in{n % 2}") + 16 * (n // 2 + 1))
                if n:
                    v.wait_ge(S("s_w_tp"), B("s_w_tp") + 2 * n)
                q = slice(n * QB, (n + 1) * QB)
                shape = (P, QB, L, GI)
                w4 = WW.rearrange("p (q s i) -> p q s i", q=QB, s=L)
                t4 = TMP[:, 0:1024].rearrange("p (q s i) -> p q s i", q=QB, s=L)
                y1, y2 = (y[:, :, q].rearrange("p s q -> p q s").unsqueeze(3).to_broadcast(shape) for y in (Y1, Y2))
                br, bi = (BB[n % 2][:, c].unsqueeze(2).to_broadcast(shape) for c in range(2))
                scaled_sum(w4, t4, br, y1, bi, y2).then_inc(S("s_w_ready"), 1)
                v.wait_ge(S("s_w_ready"), B("s_w_ready") + n + 1)
            v.wait_ge(S("s_v_ready"), B("s_v_ready") + Q // 4)
            fwd_turn = scan_turn(v, W, 0)
            with v.Fori(LC + 2, NCH + 1) as i:
                W.enter(i - (LC + 2), 4)
                fwd_turn(i, -1)
                W.leave(NCH - LC - 1)
            W(v.tensor_copy(VST[:, 0, 0:GROUPS], VST[:, NCH, 0:GROUPS]))
            with v.Fori(1, LC + 1) as i:
                W.enter(i - 1, 4)
                fwd_turn(i, -1)
                W.leave(LC)
            v.sem_inc(S("s_fwd_done"), 1)
            v.wait_ge(S("s_d_in"), B("s_d_in") + 16)
            W(v.tensor_tensor(HC[0:LC], HC[0:LC], DROW[0:LC].unsqueeze(1).to_broadcast((LC, L, D)), ALU.mult))
            v.sem_inc(S("s_hd"), 1)

            def y_add(n):
                v.wait_ge(S("s_y_mm"), B("s_y_mm") + n + 1)
                for k in range(2):
                    c = slice((n * QB + 4 * k) * GI, (n * QB + 4 * k + 4) * GI)
                    y = HC[0:LC, :, c].rearrange("p t (g i) -> p g t i", g=4)
                    ins = v.tensor_tensor(y, PS[0:LC, 4 + 2 * (n % 2) + k, :].rearrange("p (g t i) -> p g t i", g=4, t=L), y, ALU.add)
                ins.then_inc(S("s_y_ready"), 1)

            for n in range(GROUPS // QB):
                v.wait_ge(S("s_c_in"), B("s_c_in") + 64 * (n + 1))
                if n:
                    v.wait_ge(S("s_y_mm"), B("s_y_mm") + n)
                for d in range(2):
                    q = slice(d * GROUPS + n * QB, d * GROUPS + (n + 1) * QB)
                    shape = (P, QB, L + 1, GI)
                    t4 = TMP.rearrange("p (q s i) -> p q s i", q=QB, s=L + 1)
                    x1, x2 = (x[:, :, q].rearrange("p s q -> p q s").unsqueeze(3).to_broadcast(shape) for x in (X1, X2))
                    cr, ci = (CB[:, d, c].unsqueeze(2).to_broadcast(shape) for c in range(2))
                    W(scaled_sum(CC[:, d], t4, cr, x1, ci, x2))
                    shape = (P, QB, GI)
                    f1, f2 = (x[:, q].unsqueeze(2).to_broadcast(shape) for x in (F1, F2))
                    W(scaled_sum(BB2[:, d], TMP[:, 0:QB * GI].rearrange("p (q i) -> p q i", q=QB), BD[:, d, 0], f1, BD[:, d, 1], f2))
                v.sem_inc(S("s_cc_ready"), 1)
                if n:
                    y_add(n - 1)
            y_add(GROUPS // QB - 1)
            for t in range(L):
                v.wait_ge(S("s_yt_tp"), B("s_yt_tp") + t + 1)
                v.tensor_copy(YT[:, :, t * LC:(t + 1) * LC], PS[:, t % 4, :].rearrange("p (j c) -> p j c", j=DC)).then_inc(S("s_yt"), 1)
            v.wait_ge(S("s_bg_in"), B("s_bg_in") + 16)
            for n in range(2 * LT + 1):
                if n < 2 * LT:
                    h, b = n // LT, 4 + 2 * (n % 2)
                    v.wait_ge(S("s_glu_mm"), B("s_glu_mm") + n + 1)
                    if n >= 2:
                        v.wait_ge(S("s_oo"), B("s_oo") + n - 1)
                    v.tensor_tensor(ZT[n % 2][:, 0:512], PS[:, b, :], BG[:, h * 512:(h + 1) * 512], ALU.add)
                    v.tensor_tensor(ZT[n % 2][:, 512:1024], PS[:, b + 1, :], BG[:, D + h * 512:D + (h + 1) * 512], ALU.add).then_inc(S("s_z"), 1)
                if n:
                    a = n - 1
                    h, m = a // LT, a % LT
                    v.wait_ge(S("s_sig"), B("s_sig") + n)
                    v.tensor_tensor(OO[:, m, h * 512:(h + 1) * 512], ZT[a % 2][:, 0:512], ZT[a % 2][:, 512:1024], ALU.mult).then_inc(S("s_oo"), 1)
            v.wait_ge(S("s_rowg"), B("s_rowg") + 16)
            v.wait_ge(S("s_xr_in"), B("s_xr_in") + 16 * L)
            for m in range(LT):
                v.wait_ge(S("s_osd"), B("s_osd") + m + 1)
                W(v.reciprocal(rs[:, 8 + m:9 + m], sd[:, 8 + m:9 + m]))
                W(v.scalar_tensor_tensor(OO[:, m, :], OO[:, m, :], rs[:, 8 + m:9 + m], row(0), ALU.mult, ALU.mult))
                v.tensor_tensor(X[:, m, :], X[:, m, :], OO[:, m, :], ALU.add).then_inc(S("x3_ready"), 1)

        @block.vector
        def _(v):
            W = Steps(v, S("dve_step"))
            v.wait_ge(S("const_in"), 5 * 16)
            v.wait_ge(S("tri_in"), 32)
            v.tensor_copy(tri[:, :], work(0, P))
            v.tensor_copy(iota_b[:, :], work(P, P))
            v.memset(ones_b[:, :], 1.0)
            W(v.memset(eps[:, :], EPS))
            v.sem_inc(S("eps_ready"), 1)
            for l in range(2):
                v.wait_ge(S("modb_in"), 32 * (l + 1))
                if l:
                    v.wait_ge(S("mod_free"), 1)
                for m in range(ADA_T):
                    n = l * ADA_T + m
                    v.wait_ge(S("ada_mm"), n + 1)
                    c = slice(m * 512, (m + 1) * 512)
                    v.tensor_tensor(MOD[:, c], PS[0:2, n % 4, :], MODB[:, c], ALU.add).then_inc(S("ada_ev"), 1)
                v.wait_ge(S("ada_ev"), ADA_T * (l + 1))
                for q in (1, 4):
                    c = slice(q * D, (q + 1) * D)
                    k = 0 if q == 1 else 2
                    v.scalar_tensor_tensor(MOD[:, c], MOD[:, c], 1.0, NG[:, k * D:(k + 1) * D], ALU.add, ALU.mult)
                for q in (2, 5):
                    c = slice(q * D, (q + 1) * D)
                    k = 1 if q == 2 else 3
                    ins = v.tensor_tensor(MOD[:, c], MOD[:, c], NG[:, k * D:(k + 1) * D], ALU.mult)
                W(ins)
                v.sem_inc(S("mod_ready"), 1)
            v.wait_ge(S("a_sd"), 1)
            W(v.reciprocal(rs[:, 0:AT], sd[:, 0:AT]))
            v.wait_ge(S("rows_a"), 64)
            v.wait_ge(S("mod_out"), 32)

            def modulated(n, t, lat_ctx, free, ready):
                k = 2 * lat_ctx
                if n >= 2:
                    free(n)
                W(v.scalar_tensor_tensor(H[n % 2], X[:, t, :], rs[:, n:n + 1], row(k), ALU.mult, ALU.mult))
                v.tensor_tensor(H[n % 2], H[n % 2], row(k + 1), ALU.add).then_inc(ready, 1)

            for t in range(AT + 2):
                if t < AT:
                    modulated(t, t, stream[t], lambda n: v.wait_ge(S("a_tp"), n - 1), S("a_h_ready"))
                if t >= 2:
                    a = t - 2
                    ps = bank2(4 + 2 * (a % 2))
                    v.wait_ge(S("c_sd"), a + 1)
                    W(v.reciprocal(rs[:, 6:8], sd[:, 6:8]))
                    if a:
                        v.wait_ge(S("ct_tp"), a)
                    v.tensor_scalar(CA[:, 0:QL], ps[:, 0:QL], rs[:, 6:7], None, ALU.mult)
                    v.tensor_scalar(CA[:, QL:QL + KVL], ps[:, QL:QL + KVL], rs[:, 7:8], None, ALU.mult)
                    v.tensor_copy(CA[:, QL + KVL:AW], ps[:, QL + KVL:AW]).then_inc(S("ca_ready"), 1)
                    v.wait_ge(S("ct_tp"), a + 1)
                    c = slice(a * P, (a + 1) * P)
                    ct = bank2(2)
                    for j in range(QC):
                        v.tensor_scalar(CQT[:, j, c], ct[:, j * P:(j + 1) * P], gcol[:, j:j + 1], None, ALU.mult)
                    for j in range(KC):
                        v.tensor_scalar(CKT[:, j, c], ct[:, (QC + j) * P:(QC + j + 1) * P], gcol[:, QC + j:QC + j + 1], None, ALU.mult)
                    v.tensor_copy(KPT[:, c], ct[0:ROPE, (QC + KC) * P:(QC + KC + 1) * P]).then_inc(S("ct_ready"), 1)
            for n in range(1, 2 * AT, 2):
                v.wait_ge(S("v_mm"), n + 1)
                v.tensor_copy(V[:, n // 2, 512:1024], PS[:, 4 + n % 4, :]).then_inc(S("v_ready_v"), 1)

            def rope(dst, src, ps, done):
                v.tensor_tensor(dst, src, cosT, ALU.mult)
                W(v.tensor_tensor(ps, ps, sinT, ALU.mult))
                v.tensor_tensor(dst, dst, ps, ALU.add).then_inc(done, 1)

            v.wait_ge(S("rope_in"), 32)
            v.wait_ge(S("k_rot"), 1)
            rope(KPR, KPT, bank2(6, N_ALL)[0:ROPE], S("k_rope"))
            for h in range(HEADS):
                v.wait_ge(S("kn_mm"), h + 1)
                v.tensor_copy(knT, bank2(2, N_ALL)).then_inc(S("kn_ready"), 1)
                v.wait_ge(S("q_rot"), h + 1)
                if h:
                    v.wait_ge(S("s_mm"), h * AT)
                rope(qpR, qpT, bank2(6, N_ALL)[0:ROPE], S("q_rope"))
                for t in range(AT + 1):
                    if t < AT:
                        k = h * AT + t
                        nk = N_ALL if t < LT else N_CTX
                        v.wait_ge(S("s_mm"), k + 1)
                        if k >= 2:
                            v.wait_ge(S("p_exp"), k - 1)
                        W(v.reduce_max(mx[:, t % 2:t % 2 + 1], bank2(2 * (t % 2), nk), AX_X))
                        v.tensor_scalar(mx[:, t % 2:t % 2 + 1], mx[:, t % 2:t % 2 + 1], -SCALE, None, ALU.mult).then_inc(S("nmax"), 1)
                    if t:
                        k = h * AT + t - 1
                        c = (t - 1) % 2
                        nk = N_ALL if t - 1 < LT else N_CTX
                        v.wait_ge(S("p_exp"), k + 1)
                        W(v.reciprocal(sm[:, 2 + c:3 + c], sm[:, c:c + 1]))
                        v.tensor_scalar(PR[c][:, 0:nk], PR[c][:, 0:nk], sm[:, 2 + c:3 + c], None, ALU.mult).then_inc(S("p_ready"), 1)
            v.wait_ge(S("rows_g"), 32)
            for t in range(AT):
                v.wait_ge(S("o_sd"), t + 1)
                W(v.reciprocal(rs[:, 8 + t:9 + t], sd[:, 8 + t:9 + t]))
                W(v.scalar_tensor_tensor(H[t % 2], bank2(2 * (t % 2)), rs[:, 8 + t:9 + t], row(stream[t]), ALU.mult, ALU.mult))
                v.sem_inc(S("o_used"), 1)
                v.tensor_tensor(X[:, t, :], X[:, t, :], H[t % 2], ALU.add).then_inc(S("x1_ready"), 1)
            moe_dve(v, W, modulated, 0)
            s5_dve(v, W, modulated)
            moe_dve(v, W, modulated, 1)

        def moe_pool(pool, l):
            NT = len(TILES[l])
            g, Z = "m_", before_moe(l)

            def gather(dst, u, done):
                pool.sem_inc(S("pool_starts"), 1)
                pool.indirect_dma_start(out=dst, out_offset=None, in_=f_d[l][:, :],
                                        in_offset=bass.IndirectOffsetOnAxis(ap=idxg[:, u:u + 1], axis=0)).then_inc(done, 16)

            def scatter(src, u, done):
                pool.sem_inc(S("pool_starts"), 1)
                pool.indirect_dma_start(out=acc_d[l][:, :], out_offset=bass.IndirectOffsetOnAxis(ap=idxs[:, u:u + 1], axis=0),
                                        in_=src, in_offset=None, compute_op=ALU.add).then_inc(done, 16)

            for k in range(2):
                pool.wait_ge(S(g + f"f_out{k}"), Z(f"f_out{k}") + NT // 2 * 16)
            pool.wait_ge(S(g + "f_trash"), Z("f_trash") + 16)
            pool.wait_ge(S(g + "sh_down"), Z("sh_down") + NT)
            for b in range(2):
                pool.dma_start(spare[:, b:b + 1], cst[:, 0:1]).then_inc(S(f"scat{b}_{l}"), 16)
            for b in range(2):
                pool.wait_ge(S(f"idx_ready{l}"), b + 1)
                gather(XG[b], b, S(f"xg_in{b}_{l}"))
            for k in range(2):
                pool.wait_ge(S(g + f"acc_out{k}"), Z(f"acc_out{k}") + NT // 2 * 16)
            pool.wait_ge(S(g + "acc_out2"), Z("acc_out2") + 16)
            pairs, most = pairs_of(pool, l)
            with pool.Fori(0, most) as i:
                with pool.If(pairs - i > 0):
                    for u in range(2):
                        b = i * 2 + u
                        pool.wait_ge(S(f"scat{u}_{l}"), i * 16 + 16)
                        pool.sem_inc(S(f"os_free{l}"), 1)
                        pool.wait_ge(S(f"idx_ready{l}"), b + 3)
                        pool.wait_ge(S(f"xt_tp{l}"), b + 1)
                        gather(XG[u], u, S(f"xg_in{u}_{l}"))
                        pool.wait_ge(S(f"scat{1 - u}_{l}"), i * 16 + 16 * (1 + u))
                        pool.wait_ge(S(f"out_a{l}"), b + 2)
                        pool.wait_ge(S(f"out_v{l}"), b + 2)
                        scatter(OS[u], u, S(f"scat{u}_{l}"))
            done = pool.snap(pairs * 16 + 16, min_val=16, max_val=most * 16 + 16)
            for k in range(2):
                pool.wait_ge(S(f"scat{k}_{l}"), done)
                pool.wait_ge(S(f"xg_in{k}_{l}"), done)
                pool.sem_inc(S("pool_starts"), 1)
            pool.sem_inc(S(g + "all_scattered"), 1)


        def s5_pool(pool):
            G = Steps(pool, S("pool_step"))
            pool.wait_ge(S("s_hc_in"), B("s_hc_in") + 32)
            for n in range(GROUPS // 4):
                if n >= 2:
                    pool.wait_ge(S("s_u_tp"), B("s_u_tp") + n - 1)
                pool.tensor_copy(HG[n % 2][0:NCH].rearrange("p (g t i) -> p g t i", g=4, t=L),
                                 HC[0:NCH, :, n * 64:n * 64 + 64].rearrange("p t (g i) -> p g t i", g=4)).then_inc(S("s_hg_ready"), 1)
            pool.wait_ge(S("s_tab_ready"), B("s_tab_ready") + 1)
            pool.wait_ge(S("s_v_ready"), B("s_v_ready") + Q // 4)
            turn = scan_turn(pool, G, 1)
            with pool.Fori(1, NCH) as i:
                G.enter(i - 1, 4)
                turn(NCH - i, 1)
                G.leave(NCH - 1)
            pool.sem_inc(S("s_bwd_done"), 1)

        @block.gpsimd
        def _(pool):
            moe_pool(pool, 0)
            s5_pool(pool)
            moe_pool(pool, 1)


def constants():
    k = np.arange(P)
    cst = np.zeros((P, 80), np.float32)
    cst[:, 0] = k
    cst[:, 2], cst[:, 3] = N_ALL + k, N_LAT + k
    cst[:, 4], cst[:, 5] = -(N_ALL + k), -(N_LAT + k)
    cst[:, 6], cst[:, 7] = k < ST, k >= ST
    cst[:, 8:72] = 8.0 ** (np.arange(N_EXP) % NSLOT)
    cst[:, 72] = 1.0
    cst[:, 73], cst[:, 74] = -cst[:, 6], -cst[:, 7]
    rot = np.zeros((ROPE, ROPE), np.float32)
    for i in range(ROPE // 2):
        rot[2 * i + 1, 2 * i], rot[2 * i, 2 * i + 1] = -1, 1
    t = np.arange(N_LAT)
    inv = (10000.0 ** (-np.arange(16, dtype=np.float32) / 16)).astype(np.float32)
    ang = np.concatenate([(t // 64).astype(np.float32)[:, None] * inv, (t % 64).astype(np.float32)[:, None] * inv], -1)
    cos = np.concatenate([np.ones((N_CTX, ROPE // 2), np.float32), np.cos(ang)])
    sin = np.concatenate([np.zeros((N_CTX, ROPE // 2), np.float32), np.sin(ang)])
    return dict(ident=np.eye(P, dtype=np.float32), tri=(k[:, None] < k[None, :]).astype(np.float32),
                iota=np.broadcast_to(k.astype(np.float32), (P, P)), cst=cst, rot=rot,
                cosT=np.repeat(cos, 2, 1).T, sinT=np.repeat(sin, 2, 1).T)


def laid_out(a):
    def by_state(x):
        return np.concatenate([x, x], 0)

    r = constants()
    r.update(x=a["x"][0], ctx=a["ctx"][0], cs=np.stack([a["c"][0], a["c_ctx"]], -1).reshape(P, DC, 2),
             ada_w=a["ada_w"], ada_b=a["ada_b"], norm_g=a["norm_g"].reshape(2, 4 * D),
             gcol=np.concatenate([a["mla_g_q"][0].reshape(P, QC), a["mla_g_kv"][0].reshape(P, KC)], 1),
             w_dqkv=a["mla_w_dqkv"][0], w_uq=a["mla_w_uq"][0], w_ukv=a["mla_w_ukv"][0], w_o=a["mla_w_o"][0],
             w_router=a["moe_w_router"], moe_bias=a["moe_bias"], w_gate=a["moe_w_gate"], w_up=a["moe_w_up"],
             w_down=a["moe_w_down"], sh_gate=a["sh_w_gate"], sh_up=a["sh_w_up"], sh_down=a["sh_w_down"],
             s5_d=a["s5_d"], w_glu=a["s5_w_glu"][0], b_glu=a["s5_b_glu"])
    lam_re, lam_im = (a[k][0].transpose(2, 0, 1).reshape(ST, Q) for k in ("s5_lam_re", "s5_lam_im"))
    log_step = np.broadcast_to(a["s5_log_step"][0].reshape(1, Q), (ST, Q))
    r["s5_par"] = by_state(np.concatenate([lam_re, lam_im, log_step], 1))
    r["s5_b"] = by_state(np.stack([a[k][0].transpose(2, 0, 1, 3).reshape(ST, Q, GI) for k in ("s5_b_re", "s5_b_im")], 1))
    r["s5_c"] = by_state(np.stack([a[k][0].transpose(3, 0, 1, 2).reshape(ST, Q, GI) for k in ("s5_c_re", "s5_c_im")], 1))
    return {k: np.ascontiguousarray(v) for k, v in r.items()}


def kernel(**inputs):
    import concourse.bacc as _bacc
    from concourse.bass_utils import run_bass_kernel_spmd as _run

    nc = _bacc.Bacc("TRN2", target_bir_lowering=False, num_devices=1)
    arrays = laid_out({k: np.asarray(v) for k, v in inputs.items()})
    I = {k: nc.dram_tensor(k, v.shape, F32, kind="ExternalInput").ap() for k, v in arrays.items()}
    O = {"out": nc.dram_tensor("out", (N_LAT, D), F32, kind="ExternalOutput").ap()}
    build(nc, I, O)
    r = _run(nc, [arrays], core_ids=[0])
    return np.asarray(r.results[0]["out"]).reshape(1, N_LAT, D)
```

```python
from contextlib import ExitStack

import numpy as np

import concourse.bass as bass
from concourse import mybir

F32 = mybir.dt.float32
BF16 = mybir.dt.bfloat16
U32 = mybir.dt.uint32
I32 = mybir.dt.int32
ALU = mybir.AluOpType
ACT = mybir.ActivationFunctionType
AX_X = mybir.AxisListType.X

P = 128
D = 1024
DC = D // P
N_LAT, N_CTX = 512, 256
N_ALL = N_LAT + N_CTX
CT, LT = N_CTX // P, N_LAT // P
AT = CT + LT
EPS = 1e-6
HEADS, NOPE, ROPE, VD = 8, 128, 64, 128
QL, KVL = 384, 256
QC, KC = QL // P, KVL // P
AW = QL + KVL + ROPE
QW, KVW = HEADS * (NOPE + ROPE), HEADS * (NOPE + VD)
SCALE = float(NOPE + ROPE) ** -0.5
N_EXP, FE = 64, 256
EPAD = N_EXP + 1
FC = FE // P
ROUTED = 2.5
TURNS = 8
TOP_K = 8
BIG = 1.0e30
SLOT = 2 * DC * FE + FC * D
NSLOT = 4
GROUPS, GI, ST = 64, 16, 64
L = 8
LC, CC_ = N_LAT // L, N_CTX // L
NCH = LC + CC_
BL = 8
Q = 2 * GROUPS
QB = 8
TWO_PI = float(2.0 * np.pi)
ROUND = 12582912.0
PI_A, PI_B = 6.28125, 0.0019350051879882812
PI_C = TWO_PI - PI_A - PI_B
ADA_T = 6 * D // 512


class Steps:

    def __init__(self, eng, sem):
        self.eng, self.sem, self.n, self.off = eng, sem, 0, None

    def __call__(self, ins):
        self.n += 1
        ins.then_inc(self.sem, 1)
        self.eng.wait_ge(self.sem, self.n if self.off is None else self.off + self.n)

    def enter(self, i, per):
        self.start, self.per, self.off = self.n, per, i * per

    def leave(self, turns):
        assert self.n - self.start == self.per, self.n - self.start
        self.n, self.off = self.start + self.per * turns, None


def build(nc, I, O):
    ctx = ExitStack()
    with ctx:
        def sb(name, shape, dt=F32):
            return ctx.enter_context(nc.sbuf_tensor("sb_" + name, shape, dt))

        def dram(name, shape):
            return nc.dram_tensor("scratch_" + name, shape, F32).ap()

        sems = {}

        def S(name):
            if name not in sems:
                sems[name] = ctx.enter_context(nc.semaphore(name))
            return sems[name]

        RING = sb("ring", [P, NSLOT * SLOT])
        X = sb("x", [P, AT, D])
        ROWS = sb("rows", [P, 4, D])
        WORK = sb("work", [P, 16384])
        ident = sb("ident", [P, P])
        rot = sb("rot", [ROPE, ROPE])
        cst = sb("cst", [P, 80])
        tri = sb("tri", [P, P], BF16)
        ones_b = sb("ones_b", [P, P], BF16)
        iota_b = sb("iota_b", [P, P], BF16)
        cs = sb("cs", [P, DC, 2])
        csl = sb("csl", [P, DC, 2])
        gcol = sb("gcol", [P, QC + KC])
        eps = sb("eps", [P, 1])
        junk = sb("junk", [P, D], BF16)
        ss = sb("ss", [P, 16])
        sd = sb("sd", [P, 16])
        rs = sb("rs", [P, 16])
        sm = sb("sm", [P, 8])
        mx = sb("mx", [P, 2])
        words = sb("words", [1, P // 2], I32)
        ends = sb("ends", [1, N_EXP], I32)
        idxg = sb("idxg", [P, 2], U32)
        gateg = sb("gateg", [P, 2])
        idxs = sb("idxs", [P, 2], U32)
        gates = sb("gates", [P, 2])
        it = sb("it", [P, 8])
        spare = sb("spare", [P, 2])
        PS = ctx.enter_context(nc.psum_tensor("ps", [P, 8, 512], F32))

        mod_d = dram("mod", (2, 2, 6 * D))
        f_d = [dram("f0", (N_ALL + P, D)), dram("f1", (N_LAT + P, D))]
        acc_d = [dram("acc0", (N_ALL + P, D)), dram("acc1", (N_LAT + P, D))]

        def work(a, n):
            return WORK[:, a:a + n]

        def bank2(b, n=1024):
            return PS[:, b:b + 2, :].rearrange("p b n -> p (b n)")[:, 0:n]

        ring = RING[:, :]
        w_dqkv = ring[:, 0:DC * AW].rearrange("p (j n) -> p j n", j=DC)
        OT = ring[:, 0:HEADS * N_ALL].rearrange("p (h n) -> p h n", h=HEADS)
        w_uq = ring[:, 7680:7680 + QC * QW].rearrange("p (j n) -> p j n", j=QC)
        w_ukv = ring[:, 12288:12288 + KC * KVW].rearrange("p (j n) -> p j n", j=KC)
        w_o = ring[:, 16384:24576].rearrange("p (h n) -> p h n", h=HEADS)
        HT = work(0, DC * N_ALL).rearrange("p (j n) -> p j n", j=DC)
        V = work(0, AT * D).rearrange("p (t n) -> p t n", t=AT)
        CQT = work(6144, QC * N_ALL).rearrange("p (j n) -> p j n", j=QC)
        CKT = work(8448, KC * N_ALL).rearrange("p (j n) -> p j n", j=KC)
        KPT = work(9984, N_ALL)[0:ROPE, :]
        KPR = work(10752, N_ALL)[0:ROPE, :]
        H = [work(11520, D), work(12544, D)]
        CA = work(13568, AW)
        qnT = work(11520, N_ALL)
        knT = work(12288, N_ALL)
        qpT = work(13056, N_ALL)[0:ROPE, :]
        qpR = work(13824, N_ALL)[0:ROPE, :]
        cosT = work(14592, N_ALL)[0:ROPE, :]
        sinT = work(15360, N_ALL)[0:ROPE, :]
        rows1 = ROWS[:, :, :].rearrange("p a b -> p (a b)")
        PR = [rows1[:, 0:N_ALL], work(9984, N_ALL)]
        PT = rows1[:, N_ALL:N_ALL + AT * N_LAT].rearrange("p (k q) -> p k q", k=AT)
        MOD = work(0, 6 * D)[0:2, :]
        MODB = work(6144, 6 * D)[0:2, :]
        NG = work(12288, 4 * D)[0:2, :]

        MOD1, MODB1, NG1 = (work(a, 2 * D)[0:2, :] for a in (8192, 6144, 13568))

        def ada1_slot(n):
            return ring[:, (n % 3) * 4096:(n % 3 + 1) * 4096].rearrange("p (j n) -> p j n", j=DC)

        def ada_slot(n):
            return ring[:, (n % 3 + 1) * SLOT:(n % 3 + 1) * SLOT + DC * 512].rearrange("p (j n) -> p j n", j=DC)

        def slot(u):
            return ring[:, u * SLOT:(u + 1) * SLOT]

        RING4 = ring.rearrange("p (s n) -> p s n", s=NSLOT)

        def gu_rhs(u, j):
            return slot(u)[:, 0:2 * DC * FE].rearrange("p (w j n) -> p w j n", w=2, j=DC)[:, :, j, :]

        def dn_rhs(u, j, h):
            return slot(u)[:, 2 * DC * FE + j * D + h * 512:2 * DC * FE + j * D + h * 512 + 512]

        XG = [work(0, D), work(1024, D)]
        XT = [work(2048, D).rearrange("p (j n) -> p j n", j=DC), work(3072, D).rearrange("p (j n) -> p j n", j=DC)]
        OS = [work(4096, D), work(5120, D)]
        SUM = [work(n * D, D) for n in range(AT)]
        SG = [work(7168, FE), work(7424, FE)]
        UP = [work(8704, FE), work(8960, FE)]
        RG = [work(8704, D), work(9728, D)]
        RT = work(13568, D)
        HH = [work(7680, FE), work(7936, FE)]
        HHT = [work(8192, FE).rearrange("p (j n) -> p j n", j=FC), work(8448, FE).rearrange("p (j n) -> p j n", j=FC)]
        OH = [work(8704 + 384 * k, 384).bitcast(BF16).rearrange("p (t n) -> p t n", t=AT) for k in range(2)]
        POSM = work(9472, AT * EPAD).rearrange("p (t e) -> p t e", t=AT)
        RH = work(9872, AT * EPAD * 3).bitcast(BF16).rearrange("p (t e c) -> p t e c", t=AT, c=6)
        MB16 = work(11064, 192).bitcast(BF16).rearrange("p (t e) -> p t e", t=AT)
        at = [13568]

        def temp(n):
            at[0] += n
            assert at[0] <= 16384
            return work(at[0] - n, n)

        def t_e(n):
            return temp(AT * n).rearrange("p (t e) -> p t e", t=AT)

        SC, BI, MR = t_e(64), t_e(64), t_e(64)
        GTE = t_e(64)
        M8 = work(6656, AT * 64).rearrange("p (t g k) -> p t g k", t=AT, g=8)
        GS, GR, G8, TR, GM, TB, E8 = t_e(16), t_e(16), t_e(8), t_e(8), t_e(8), t_e(8), t_e(8)
        WR = work(6144, DC * N_EXP).rearrange("p (j e) -> p j e", j=DC)
        BROW = temp(N_EXP)
        CNT, NB, END = temp(64), temp(64), temp(64)
        SHIFT = temp(P)
        TAB = temp(4)
        DG = temp(P).bitcast(BF16)


        x_rows = [I["ctx"][k * P:(k + 1) * P, :] for k in range(CT)] + [I["x"][k * P:(k + 1) * P, :] for k in range(LT)]
        stream = [1] * CT + [0] * LT
        TILES = [list(range(AT)), list(range(LT))]

        def row(k):
            return ROWS[:, k, :]

        def pe_transposes(src, dst, n, done):
            for j in range(n):
                ins = nc.tensor.transpose(dst[:, j * P:j * P + src.shape[0]], src[:, j::n], ident[0:src.shape[0], 0:src.shape[0]])
            ins.then_inc(done, 1)

        h1_d, x2_d = dram("h1", (N_ALL, D)), dram("x2", (N_LAT, D))
        left = {}

        def again(name, old, count):
            sems[name], left[name] = S(old), count

        for name, old, count in (
                ("s_rows", "rows_a", 64), ("s_h_out0", "ada_in0", 64), ("s_h_out1", "ada_in1", 64), ("s_x_out", "x_in", 16 * AT),
                ("s_hc_in", "w_dqkv_in", 16), ("s_par_in", "w_ukv_in", 16), ("s_b_in0", "w_uq_in", 16), ("s_b_in1", "w_o_in", 16),
                ("s_c_in0", "ada_in2", 64), ("s_t_in", "ada_in3", 0), ("s_d_in", "rope_in", 32), ("s_wg_in0", "rows_m", 64),
                ("s_wg_in1", "const_in", 80), ("s_bg_in", "modb_in", 32), ("s_rowg", "rows_g", 32), ("s_xr_in", "mod_out", 32),
                ("s_rown", "tri_in", 32),
                ("s_hg_ready", "a_mm", AT), ("s_pw_ready", "k_rot", 1), ("s_c_in1", "v_mm", 2 * AT), ("s_st_mm", "ct_tp", AT),
                ("s_chain_done", "pv_lat", HEADS), ("s_sd", "a_sd", 1), ("s_h_ready", "a_h_ready", AT), ("s_u_tp", "a_tp", AT), ("s_u_ready", "a_ht", 2 * AT),
                ("s_tab_v", "ca_ready", AT), ("s_tab_a", "c_sd", AT), ("s_tab_ready", "k_rope", 1), ("s_w_ready", "qn_ready", HEADS),
                ("s_w_tp", "qn_mm", HEADS), ("s_wt_ready", "qp_ready", HEADS), ("s_v_mm", "kn_mm", HEADS),
                ("s_v_ready", "ot_lat", HEADS), ("s_fwd_done", "kn_ready", HEADS), ("s_bwd_done", "mod_free", 0),
                ("s_cc_ready", "q_rope", HEADS), ("s_kk_mm", "qp_mm", HEADS), ("s_kk_ready", "ot_ctx", HEADS),
                ("s_y_mm", "q_rot", HEADS), ("s_y_ready", "p_ready", HEADS * AT), ("s_hd", "mod_ready", 2),
                ("s_gelu", "p_exp", HEADS * AT), ("s_yt_tp", "p_tp", HEADS * AT), ("s_yt", "nmax", HEADS * AT),
                ("s_glu_mm", "s_mm", HEADS * AT), ("s_z", "ct_ready", AT), ("s_sig", "pt_ready", HEADS * AT),
                ("s_oo", "o_used", AT), ("s_osd", "v_ready_a", AT), ("x3_ready", "v_ready_v", AT)):
            again(name, old, count)

        def B(name):
            return left[name]

        VST = ring[:, 0:(NCH + 1) * Q].rearrange("p (s q) -> p s q", q=Q)
        HC = ring[:, 12416:12416 + L * D].rearrange("p (t n) -> p t n", t=L)
        TEMP = ring[:, 20608:24576]
        U = work(0, GROUPS * NCH).rearrange("p (g c) -> p g c", g=GROUPS)
        TZ = work(6144, GROUPS * P).rearrange("p (g n) -> p g n", g=GROUPS)
        KKS = work(14336, 8 * 240)[0:GI, :].rearrange("p (g n) -> p g n", g=8)
        DROW = work(14336, D)
        tx = X[:, :, :].rearrange("p a b -> p (a b)")
        X1, X2 = (tx[:, a:a + 1152].rearrange("p (j q) -> p j q", q=Q) for a in (0, 1152))
        Y1, Y2 = (tx[:, a:a + 1024].rearrange("p (j q) -> p j q", q=Q) for a in (2304, 3328))
        LRE, LIM, LST = (tx[:, 4352 + k * Q:4352 + (k + 1) * Q] for k in range(3))
        tA, tTH, tEA, tK, tR, tR2, tFR, tFI, tM, tN = (tx[:, 4736 + k * Q:4736 + (k + 1) * Q] for k in range(10))
        F1, F2 = tA, tTH
        NR, NI = (rows1[:, a:a + 1152].rearrange("p (j q) -> p j q", q=Q) for a in (0, 1152))
        TMP = rows1[:, 2304:3456]
        GR_, GI_ = (TEMP[:, a:a + 1024].rearrange("p (j q) -> p j q", q=Q) for a in (0, 1024))
        WW = [TEMP[:, 0:1024], TEMP[:, 2560:3584]]
        WT = TEMP[:, 1024:2048].rearrange("p (k n) -> p k n", k=8)
        BB = [TEMP[:, 2048 + k * 256:2304 + k * 256].rearrange("p (c q i) -> p c q i", c=2, q=QB) for k in range(2)]
        HG = [TEMP[:, 2560 + k * 512:3072 + k * 512] for k in range(2)]
        CB, BD = ([m[:, a:a + 512].rearrange("p (d c q i) -> p d c q i", d=2, c=2, q=QB) for m in (TEMP, rows1[:, 1152:])] for a in (0, 512))
        BB2 = [m.rearrange("p (d q i) -> p d q i", d=2, q=QB) for m in (TEMP[:, 1024:1280], tx[:, 4992:5248])]
        CC = [m.rearrange("p (d q j i) -> p d q j i", d=2, q=QB, i=GI) for m in (TEMP[:, 1280:3584], tx[:, 2304:4608])]
        PWR, PWI = (tx[:, a:a + 1024].rearrange("p (k q) -> p k q", q=Q) for a in (2304, 3328))
        YT = work(0, DC * N_LAT).rearrange("p (j n) -> p j n", j=DC)
        OO = work(6144, LT * D).rearrange("p (t n) -> p t n", t=LT)
        BG = work(10240, 2 * D)
        ZT = [work(12288, D), work(13312, D)]
        WG = [ring[:, k * 8192:(k + 1) * 8192].rearrange("p (j w n) -> p j w n", j=DC, w=2) for k in range(2)]

        def scan(eng, W, d, t1, t2, along, into):
            q = slice(d * GROUPS, (d + 1) * GROUPS)
            beside = 1 if d else -1

            def combine(at, n, dist, k):
                cur = VST[:, at:at + (n - 1) * BL + 1:BL, q]
                last = VST[:, at + dist:at + dist + (n - 1) * BL + 1:BL, q]
                re, im = (x[:, k - 1, q].unsqueeze(1).to_broadcast((P, n, GROUPS)) for x in (PWR, PWI))
                a, b = (t[:, 0:n * GROUPS].rearrange("p (n q) -> p n q", q=GROUPS) for t in (t1, t2))
                W(eng.tensor_tensor(a, last, re, ALU.mult))
                eng.tensor_tensor(b[0:ST], last[ST:P], im[ST:P], ALU.mult)
                W(eng.tensor_tensor(b[ST:P], last[0:ST], im[0:ST], ALU.mult))
                W(eng.tensor_tensor(b, b, a, ALU.add))
                W(eng.tensor_tensor(cur, cur, b, ALU.add))

            def at(j):
                return BL - j if d else 1 + j

            lat, every = LC // BL, NCH // BL
            for j in range(1, BL if along else 1):
                combine(at(j), every, beside, 1)
            blocks = range(every - 2, -1, -1) if d else list(range(lat + 1, every)) + list(range(lat))
            for m in blocks if along else ():
                if d == 0 and m == 0:
                    W(eng.tensor_copy(VST[:, 0, q], VST[:, NCH, q]))
                combine(BL * m + at(BL - 1), 1, BL * beside, BL)
            for j in into:
                combine(at(j), lat, (j + 1) * beside, j + 1)

        def before_moe(l):
            n0 = AT
            left = dict(
                wr_in=32, sh_in=48, w_in0=768, w_in1=768, w_in2=768, w_in3=768, f_out0=n0 // 2 * 16, f_out1=n0 // 2 * 16,
                f_trash=16, acc_out0=n0 // 2 * 16, acc_out1=n0 // 2 * 16, acc_out2=16, rows_in=32,
                acc_in0=n0 // 2 * 16, acc_in1=n0 // 2 * 16, h_ready=n0, zero_ready=1, so_ready=n0,
                sh_down=n0, ht_tp=n0, ht_ready=2 * n0, logits=n0, sh_gu=n0, sh_h=n0, sh_tp=n0, sh_ht=n0, mask_ready=1,
                pos_mm=1, ends_ready=1, tab_mm=1, tab_ready=1, all_scattered=1, o_sd=n0, x_ready=n0, scores=1, sd=n0, sh_silu=n0)
            return lambda name: l * left[name]

        def pairs_of(eng, l):
            most = N_EXP + len(TILES[l]) * TOP_K
            total = eng.value_load(ends[0:1, N_EXP - 1:N_EXP], min_val=N_EXP, max_val=most)
            return eng.snap((total + 1) >> 1, min_val=N_EXP // 2, max_val=most // 2), most // 2

        def expert_of(eng, word, u):
            return nc.s_assert_within(eng.snap((word >> (7 * u)) & 127), 0, N_EXP,
                                      skip_runtime_bounds_check_because="the table holds experts' numbers")

        block = ctx.enter_context(nc.Block())

        def moe_sp(sp, l):
            tiles, NT = TILES[l], len(TILES[l])
            T = NT * P
            g, Z = "m_", before_moe(l)
            sp.dma_start(WR, I["w_router"][l].rearrange("(p j) e -> p j e", j=DC)).then_inc(S(g + "wr_in"), 16)
            sp.dma_start(BROW, I["moe_bias"][l:l + 1, :].to_broadcast((P, N_EXP))).then_inc(S(g + "wr_in"), 16)

            def load(u, gate_w, up_w, down_w, s):
                w = slot(u)
                sp.dma_start(w[:, 0:DC * FE], gate_w.rearrange("(p j) n -> p (j n)", j=DC)).then_inc(s, 16)
                sp.dma_start(w[:, DC * FE:2 * DC * FE], up_w.rearrange("(p j) n -> p (j n)", j=DC)).then_inc(s, 16)
                sp.dma_start(w[:, 2 * DC * FE:SLOT], down_w.rearrange("(p j) n -> p (j n)", j=FC)).then_inc(s, 16)

            if l:
                load(3, I["sh_gate"][l], I["sh_up"][l], I["sh_down"][l], S(g + "sh_in"))
            for n in range(NT):
                if l == 0 and n == NT - 2:
                    sp.wait_ge(S("o_mm"), AT)
                    load(3, I["sh_gate"][l], I["sh_up"][l], I["sh_down"][l], S(g + "sh_in"))
                sp.wait_ge(S(g + "h_ready"), Z("h_ready") + n + 1)
                sp.dma_start(f_d[l][n * P:(n + 1) * P, :], H[n % 2]).then_inc(S(g + f"f_out{n % 2}"), 16)
            sp.wait_ge(S(g + "zero_ready"), Z("zero_ready") + 1)
            sp.dma_start(f_d[l][T:T + P, :], ROWS[:, 0, :]).then_inc(S(g + "f_trash"), 16)
            sp.dma_start(acc_d[l][T:T + P, :], ROWS[:, 0, :]).then_inc(S(g + "acc_out2"), 16)
            for u in range(2):
                load(u, I["w_gate"][l, u], I["w_up"][l, u], I["w_down"][l, u], S(g + f"w_in{u}"))
            for n in range(NT):
                sp.wait_ge(S(g + "so_ready"), Z("so_ready") + n + 1)
                sp.dma_start(acc_d[l][n * P:(n + 1) * P, :], H[n % 2]).then_inc(S(g + f"acc_out{n % 2}"), 16)
                if n == 1:
                    load(2, I["w_gate"][l, 2], I["w_up"][l, 2], I["w_down"][l, 2], S(g + "w_in2"))
            sp.wait_ge(S(g + "sh_down"), Z("sh_down") + NT)
            sp.wait_ge(S(f"xg_in0_{l}"), 16)
            sp.wait_ge(S(f"xg_in1_{l}"), 16)
            load(3, I["w_gate"][l, 3], I["w_up"][l, 3], I["w_down"][l, 3], S(g + "w_in3"))
            wg = I["w_gate"][l].rearrange("e (p j) n -> p e (j n)", j=DC)
            wu = I["w_up"][l].rearrange("e (p j) n -> p e (j n)", j=DC)
            wd = I["w_down"][l].rearrange("e (p j) n -> p e (j n)", j=FC)
            sp.wait_ge(S(g + "ends_ready"), Z("ends_ready") + 1)
            for u in range(2):
                sp.wait_ge(S(g + f"w_in{u}"), Z(f"w_in{u}") + 48)
                sp.sem_inc(S(f"w_ready{l}"), 1)
            with sp.Fori(1, N_EXP // NSLOT) as eb:
                for u in range(NSLOT):
                    e = sp.snap(eb * NSLOT + u, min_val=0, max_val=N_EXP - 1)
                    k = (u + 2) % NSLOT
                    there = sp.snap(eb * 48 + (Z(f"w_in{k}") + 48 * (u >= 2)), min_val=1, max_val=4096)
                    sp.wait_ge(S(g + f"w_in{k}"), there)
                    sp.sem_inc(S(f"w_ready{l}"), 1)
                    blocks = sp.value_load(ends[0:1, bass.ds(eb * NSLOT + (u - NSLOT), 1)], min_val=1, max_val=N_EXP + NT * TOP_K)
                    sp.wait_ge(S(f"added{l}"), blocks)
                    sp.sem_inc(S("sp_starts"), 1)
                    w = slot(u)
                    sp.dma_start(w[:, 0:DC * FE], wg[:, bass.ds(e, 1), :].rearrange("p a n -> p (a n)")).then_inc(S(g + f"w_in{u}"), 16)
                    sp.dma_start(w[:, DC * FE:2 * DC * FE], wu[:, bass.ds(e, 1), :].rearrange("p a n -> p (a n)")).then_inc(S(g + f"w_in{u}"), 16)
                    sp.dma_start(w[:, 2 * DC * FE:SLOT], wd[:, bass.ds(e, 1), :].rearrange("p a n -> p (a n)")).then_inc(S(g + f"w_in{u}"), 16)
            for u in range(2, NSLOT):
                sp.wait_ge(S(g + f"w_in{u}"), Z(f"w_in{u}") + 48 * N_EXP // NSLOT)
                sp.sem_inc(S(f"w_ready{l}"), 1)
            sp.sem_inc(S(f"w_ready{l}"), 1)
            sp.wait_ge(S(g + "f_trash"), Z("f_trash") + 16)
            sp.wait_ge(S(g + "acc_out2"), Z("acc_out2") + 16)
            for k in range(2 if l == 0 else 1):
                sp.dma_start(row(k), mod_d[l, k:k + 1, 5 * D:6 * D].to_broadcast((P, D))).then_inc(S(g + "rows_in"), 16)
            sp.wait_ge(S(g + "all_scattered"), Z("all_scattered") + 1)
            for n in range(NT):
                sp.dma_start(SUM[n], acc_d[l][n * P:(n + 1) * P, :]).then_inc(S(g + f"acc_in{2 * n // NT}"), 16)


        def s5_sp(sp):
            sp.wait_ge(S("m_x_ready"), AT)
            for t in range(LT):
                sp.dma_start(x2_d[t * P:(t + 1) * P, :], X[:, CT + t, :]).then_inc(S("s_x_out"), 16)
            sp.wait_ge(S("a1_out"), 16)
            for k, (q, r) in enumerate([(1, 0), (0, 0), (1, 1), (0, 1)]):
                sp.dma_start(row(k), mod_d[1, r:r + 1, q * D:(q + 1) * D].to_broadcast((P, D))).then_inc(S("s_rows"), 16)
            for t in range(AT):
                sp.wait_ge(S("s_h_ready"), B("s_h_ready") + t + 1)
                sp.dma_start(h1_d[t * P:(t + 1) * P, :], H[t % 2]).then_inc(S(f"s_h_out{t % 2}"), 16)
            sp.wait_ge(S("s_x_out"), B("s_x_out") + 16 * LT)
            sp.dma_start(tx[:, 4352:4736], I["s5_par"]).then_inc(S("s_par_in"), 16)
            for k in range(2):
                sp.wait_ge(S(f"s_h_out{k}"), B(f"s_h_out{k}") + AT // 2 * 16)
            sp.dma_start(HC[0:LC, :, :], h1_d[N_CTX:N_ALL, :].rearrange("(c t) n -> c t n", t=L)).then_inc(S("s_hc_in"), 16)
            sp.dma_start(HC[LC:NCH, :, :], h1_d[0:N_CTX, :].rearrange("(c t) n -> c t n", t=L)).then_inc(S("s_hc_in"), 16)
            sp.wait_ge(S("s_tab_ready"), B("s_tab_ready") + 1)
            for n in range(Q // QB):
                if n >= 2:
                    sp.wait_ge(S("s_w_ready"), B("s_w_ready") + n - 1)
                sp.dma_start(BB[n % 2], I["s5_b"][:, :, n * QB:(n + 1) * QB, :]).then_inc(S(f"s_b_in{n % 2}"), 16)
            sp.dma_start(DROW, I["s5_d"].to_broadcast((P, D))).then_inc(S("s_d_in"), 16)
            sp.wait_ge(S("s_v_mm"), B("s_v_mm") + Q // 4)

            def load_c(n):
                for d in range(2):
                    c = slice(d * GROUPS + n * QB, d * GROUPS + (n + 1) * QB)
                    sp.dma_start(CB[n % 2][:, d], I["s5_c"][:, :, c, :]).then_inc(S(f"s_c_in{n % 2}"), 16)
                    sp.dma_start(BD[n % 2][:, d], I["s5_b"][:, :, c, :]).then_inc(S(f"s_c_in{n % 2}"), 16)

            sp.wait_ge(S("a1_out"), 3 * 16)
            load_c(0)
            sp.wait_ge(S("s_pw_ready"), B("s_pw_ready") + 1)
            load_c(1)
            for n in range(GROUPS // QB):
                sp.wait_ge(S("s_kk_ready"), B("s_kk_ready") + n + 1)
                for k in range(L):
                    sp.dma_start(TZ[k * GI:(k + 1) * GI, n * QB:(n + 1) * QB, :],
                                 KKS[:, :, (L - 1 - k) * GI:(L - 1 - k) * GI + P]).then_inc(S("s_t_in"), 16)
                if n + 2 < GROUPS // QB:
                    sp.wait_ge(S("s_cc_ready"), B("s_cc_ready") + n + 1)
                    load_c(n + 2)
            sp.wait_ge(S("s_y_mm"), B("s_y_mm") + GROUPS // QB)
            wg = I["w_glu"].rearrange("(p j) (w h n) -> p j w h n", j=DC, w=2, h=2)
            sp.dma_start(BG, I["b_glu"].to_broadcast((P, 2 * D))).then_inc(S("s_bg_in"), 16)
            for w in range(2):
                sp.dma_start(WG[0][:, :, w, :], wg[:, :, w, 0, :]).then_inc(S("s_wg_in0"), 16)
            sp.dma_start(row(0), mod_d[1, 0:1, 2 * D:3 * D].to_broadcast((P, D))).then_inc(S("s_rowg"), 16)
            xr = x2_d.rearrange("(c t) n -> t c n", t=L)
            for t in range(L):
                sp.dma_start(X[(t % 2) * LC:(t % 2 + 1) * LC, t // 2, :], xr[t]).then_inc(S("s_xr_in"), 16)
            sp.wait_ge(S("s_yt_tp"), B("s_yt_tp") + L)
            for w in range(2):
                sp.dma_start(WG[1][:, :, w, :], wg[:, :, w, 1, :]).then_inc(S("s_wg_in1"), 16)
            sp.wait_ge(S("x3_ready"), B("x3_ready") + LT)
            for k, q in enumerate((4, 3)):
                sp.dma_start(row(k), mod_d[1, 0:1, q * D:(q + 1) * D].to_broadcast((P, D))).then_inc(S("s_rown"), 16)

        @block.sync
        def _(sp):
            for name, dst in (("ident", ident[:, :]), ("rot", rot[:, :]), ("cst", cst[:, :]), ("cs", cs[:, :, :]),
                              ("gcol", gcol[:, :])):
                sp.dma_start(dst, I[name]).then_inc(S("const_in"), 16)
            sp.dma_start(work(0, P), I["tri"]).then_inc(S("tri_in"), 16)
            sp.dma_start(work(P, P), I["iota"]).then_inc(S("tri_in"), 16)
            w = I["ada_w"][0].rearrange("(p j) n -> p j n", j=DC)
            sp.dma_start(MODB, I["ada_b"][0:1, :].to_broadcast((2, 6 * D))).then_inc(S("modb_in"), 16)
            sp.dma_start(NG, I["norm_g"][0:1, :].to_broadcast((2, 4 * D))).then_inc(S("modb_in"), 16)
            for n in range(ADA_T):
                if n >= 3:
                    sp.wait_ge(S("ada_mm"), n - 2)
                sp.dma_start(ada_slot(n), w[:, :, n * 512:(n + 1) * 512]).then_inc(S(f"ada_in{n % 3}"), 16)
                if n == ADA_T // 2:
                    for t in range(AT):
                        sp.dma_start(X[:, t, :], x_rows[t]).then_inc(S("x_in"), 16)
                if n == ADA_T - 3:
                    sp.wait_ge(S("mod_ready"), 1)
                    sp.dma_start(mod_d[0][:, 0:2 * D], MOD[:, 0:2 * D]).then_inc(S("mod_out"), 16)
            sp.dma_start(w_dqkv, I["w_dqkv"].rearrange("(p j) n -> p j n", j=DC)).then_inc(S("w_dqkv_in"), 16)
            sp.wait_ge(S("mod_out"), 16)
            for k, (q, r) in enumerate([(1, 0), (0, 0), (1, 1), (0, 1)]):
                sp.dma_start(row(k), mod_d[0, r:r + 1, q * D:(q + 1) * D].to_broadcast((P, D))).then_inc(S("rows_a"), 16)
            sp.wait_ge(S("mod_ready"), 2)
            sp.dma_start(mod_d[0][:, 2 * D:6 * D], MOD[:, 2 * D:6 * D]).then_inc(S("mod_out"), 16)

            def load_rows(l, vectors, tag):
                for k, (v, r) in enumerate(vectors):
                    sp.dma_start(row(k), mod_d[l, r:r + 1, v * D:(v + 1) * D].to_broadcast((P, D))).then_inc(S(tag), 16)

            sp.wait_ge(S("ada_mm"), ADA_T)
            sp.dma_start(w_ukv, I["w_ukv"].rearrange("(p j) n -> p j n", j=KC)).then_inc(S("w_ukv_in"), 16)
            sp.dma_start(w_uq, I["w_uq"].rearrange("(p j) n -> p j n", j=QC)).then_inc(S("w_uq_in"), 16)
            sp.dma_start(w_o, I["w_o"].rearrange("(h p) n -> p h n", p=P)).then_inc(S("w_o_in"), 16)
            sp.dma_start(cosT, I["cosT"]).then_inc(S("rope_in"), 16)
            sp.dma_start(sinT, I["sinT"]).then_inc(S("rope_in"), 16)
            sp.wait_ge(S("pv_ctx"), HEADS)
            sp.wait_ge(S("pv_lat"), HEADS)
            for k in range(2):
                sp.dma_start(RG[k], mod_d[0, k:k + 1, 2 * D:3 * D].to_broadcast((P, D))).then_inc(S("rows_g"), 16)
            load_rows(0, [(4, 0), (3, 0), (4, 1), (3, 1)], "rows_m")
            moe_sp(sp, 0)
            s5_sp(sp)
            moe_sp(sp, 1)
            out = O["out"].rearrange("(c t) n -> t c n", t=L)
            for m in range(LT):
                sp.wait_ge(S("m_x_ready"), AT + m + 1)
                for k in range(2):
                    sp.dma_start(out[2 * m + k], X[k * LC:(k + 1) * LC, m, :]).then_inc(S("out_done"), 16)
            sp.wait_ge(S("out_done"), 16 * L)

        def front_pe(pe, l, n):
            g, Z = "m_", before_moe(l)
            if n < len(TILES[l]):
                pe.wait_ge(S(g + "h_ready"), Z("h_ready") + n + 1)
                if n:
                    pe.wait_ge(S(g + "ht_ready"), Z("ht_ready") + 2 * n)
                pe_transposes(H[n % 2], bank2(4), DC, S(g + "ht_tp"))
            if n:
                a = n - 1
                if a == 0:
                    pe.wait_ge(S(g + "wr_in"), Z("wr_in") + 32)
                pe.wait_ge(S(g + "ht_ready"), Z("ht_ready") + 2 * n)
                for j in range(DC):
                    mm = nc.tensor.matmul(PS[:, 7, a * 64:(a + 1) * 64], HT[:, j, a * P:(a + 1) * P], WR[:, j, :], start=j == 0, stop=j == DC - 1)
                mm.then_inc(S(g + "logits"), 1)

        def moe_pe(pe, l):
            tiles, NT = TILES[l], len(TILES[l])
            g, Z = "m_", before_moe(l)
            if l:
                for n in range(NT + 1):
                    front_pe(pe, l, n)
            pe.wait_ge(S(g + "sh_in"), Z("sh_in") + 48)
            for n in range(NT + 1):
                if n < NT:
                    if n >= 2:
                        pe.wait_ge(S(g + "sh_h"), Z("sh_h") + n - 1)
                    for j in range(DC):
                        mm = nc.tensor.matmul(PS[:, 4 + n % 2, :], HT[:, j, n * P:(n + 1) * P], gu_rhs(3, j), start=j == 0, stop=j == DC - 1)
                    mm.then_inc(S(g + "sh_gu"), 1)
                if n == NT:
                    pe.wait_ge(S(g + "mask_ready"), Z("mask_ready") + 1)
                    for m in range(NT):
                        for b in range(m):
                            nc.tensor.matmul(PS[:, 7, m * 64:(m + 1) * 64], ones_b[:, :], MB16[:, b, :], start=b == 0, stop=False)
                        nc.tensor.matmul(PS[:, 7, m * 64:(m + 1) * 64], tri[:, :], MB16[:, m, :], start=m == 0, stop=True)
                    for b in range(NT):
                        mm = nc.tensor.matmul(PS[:, 7, 384:448], ones_b[:, :], MB16[:, b, :], start=b == 0, stop=b == NT - 1)
                    mm.then_inc(S(g + "pos_mm"), 1)
                if n:
                    a = n - 1
                    pe.wait_ge(S(g + "sh_h"), Z("sh_h") + a + 1)
                    if a:
                        pe.wait_ge(S(g + "sh_ht"), Z("sh_ht") + a)
                    pe_transposes(HH[a % 2], PS[:, 6, :], FC, S(g + "sh_tp"))
                    pe.wait_ge(S(g + "sh_ht"), Z("sh_ht") + a + 1)
                    if a >= 2:
                        pe.wait_ge(S(g + "so_ready"), Z("so_ready") + a - 1)
                    for half in range(2):
                        for j in range(FC):
                            mm = nc.tensor.matmul(PS[:, 2 * (a % 2) + half, :], HHT[a % 2][:, j, :], dn_rhs(3, j, half), start=j == 0, stop=j == FC - 1)
                    mm.then_inc(S(g + "sh_down"), 1)
            pe.wait_ge(S(g + "so_ready"), Z("so_ready") + NT)

            pe.wait_ge(S(g + "ends_ready"), Z("ends_ready") + 1)
            nc.tensor.matmul(PS[:, 7, 0:2 * P], ones_b[:, :], DG, start=True, stop=True).then_inc(S(g + "tab_mm"), 1)

            def pick(k, e):
                for n in range(NT):
                    mm = nc.tensor.matmul(PS[:, 7, 0:6], OH[k][:, n, :], RH[:, n, bass.ds(e, 1), :].rearrange("p a c -> p (a c)"),
                                          start=n == 0, stop=n == NT - 1)
                return mm

            pe.wait_ge(S(g + "tab_ready"), Z("tab_ready") + 1)
            pairs, most = pairs_of(pe, l)
            word = pe.value_load(words[0:1, 0:1], min_val=0, max_val=2 ** 14 - 1)
            for b in range(2):
                pe.wait_ge(S(f"oh_ready{l}"), b + 1)
                if b:
                    pe.wait_ge(S(f"idx_ready{l}"), b)
                pick(b, expert_of(pe, word, b)).then_inc(S(f"idx_mm{l}"), 1)
            pe.wait_ge(S(f"xg_in0_{l}"), 16)
            pe_transposes(XG[0], bank2(0), DC, S(f"xt_tp{l}"))

            def down(s, u):
                dn = RING4[:, bass.ds(s, 1), 2 * DC * FE:SLOT].rearrange("p a (j n) -> p (a j) n", j=FC)
                for half in range(2):
                    for j in range(FC):
                        mm = nc.tensor.matmul(PS[:, 4 + half, :], HHT[u][:, j, :], dn[:, j, half * 512:(half + 1) * 512],
                                              start=j == 0, stop=j == FC - 1)
                mm.then_inc(S(f"dn_mm{l}"), 1)

            def slot_of(word, u):
                return pe.snap((word >> (7 * u)) & (NSLOT - 1), min_val=0, max_val=NSLOT - 1)

            def pair(i, first):
                word = pe.value_load(words[0:1, bass.ds(i, 1)], min_val=0, max_val=2 ** 14 - 1)
                ahead = pe.value_load(words[0:1, bass.ds(i + 1, 1)], min_val=0, max_val=2 ** 14 - 1)
                last = None if first else slot_of(pe.value_load(words[0:1, bass.ds(i - 1, 1)], min_val=0, max_val=2 ** 14 - 1), 1)
                for u in range(2):
                    b = i * 2 + u
                    e, e2, s = expert_of(pe, word, u), expert_of(pe, ahead, u), slot_of(word, u)
                    pe.wait_ge(S(f"w_ready{l}"), pe.snap(e + 1, min_val=1, max_val=EPAD))
                    pe.wait_ge(S(f"xt_ready{l}"), b + 1)
                    pe.wait_ge(S(f"h_ready{l}"), b + 1)
                    gu = RING4[:, bass.ds(s, 1), 0:2 * DC * FE].rearrange("p a (w j n) -> p (a w) j n", w=2, j=DC)
                    for j in range(DC):
                        mm = nc.tensor.matmul(PS[:, 2 + u, :], XT[u][:, j, :], gu[:, :, j, :], start=j == 0, stop=j == DC - 1)
                    mm.then_inc(S(f"gu_mm{l}"), 1)
                    pe.wait_ge(S(f"oh_ready{l}"), b + 3)
                    pe.wait_ge(S(f"idx_ready{l}"), b + 2)
                    pick(u, e2).then_inc(S(f"idx_mm{l}"), 1)
                    pe.wait_ge(S(f"xg_in{1 - u}_{l}"), i * 16 + 16 * (1 + u))
                    pe_transposes(XG[1 - u], bank2(0), DC, S(f"xt_tp{l}"))
                    pe.wait_ge(S(f"hht_ready{l}"), b + 1)
                    pe.wait_ge(S(f"h_ready{l}"), b + 3)
                    pe_transposes(HH[u], PS[:, 6, :], FC, S(f"h_tp{l}"))
                    if not (first and u == 0):
                        pe.wait_ge(S(f"out_a{l}"), b)
                        pe.wait_ge(S(f"out_v{l}"), b)
                        down(last, 1 - u)
                    last = s

            pair(0, True)
            with pe.Fori(0, -(-most // TURNS)) as q:
                with pe.If(pairs - q * TURNS > 1):
                    with pe.Fori(1, TURNS + 1) as r:
                        i = q * TURNS + r
                        with pe.If(pairs - i > 0):
                            pair(i, False)
            final = pe.value_load(words[0:1, bass.ds(pairs - 1, 1)], min_val=0, max_val=2 ** 14 - 1)
            pe.wait_ge(S(f"hht_ready{l}"), pe.snap(pairs * 2 + 1, min_val=1, max_val=2 * most + 1))
            pe.wait_ge(S(f"out_a{l}"), pe.snap(pairs * 2, min_val=1, max_val=2 * most))
            pe.wait_ge(S(f"out_v{l}"), pe.snap(pairs * 2, min_val=1, max_val=2 * most))
            down(slot_of(final, 1), 1)

        def s5_pe(pe):
            for n in range(ADA_T):
                pe.wait_ge(S(f"a1_in{n % 3}"), 16 * (n // 3 + 1))
                if n >= 4:
                    pe.wait_ge(S("a1_ev"), n - 3)
                for j in range(DC):
                    mm = nc.tensor.matmul(PS[0:2, 4 + n % 4, :], csl[:, j, :], ada1_slot(n)[:, j, :], start=j == 0, stop=j == DC - 1)
                mm.then_inc(S("a1_mm"), 1)
            pe.wait_ge(S("s_hc_in"), B("s_hc_in") + 32)
            for n in range(GROUPS // 4):
                if n >= 4:
                    pe.wait_ge(S("s_u_ready"), B("s_u_ready") + n - 3)
                pe.wait_ge(S("s_hg_ready"), B("s_hg_ready") + n + 1)
                for k in range(4):
                    mm = nc.tensor.transpose(PS[:, n % 4, k * NCH:(k + 1) * NCH], HG[n % 2][0:NCH, k * P:(k + 1) * P], ident[0:NCH, 0:NCH])
                mm.then_inc(S("s_u_tp"), 1)
            pe.wait_ge(S("s_u_ready"), B("s_u_ready") + GROUPS // 4)
            units = Q // 4
            for n in range(units + 1):
                if n < units:
                    pe.wait_ge(S("s_w_ready"), B("s_w_ready") + n // 2 + 1)
                    if n >= 2:
                        pe.wait_ge(S("s_wt_ready"), B("s_wt_ready") + n - 1)
                    for k in range(4):
                        mm = nc.tensor.transpose(PS[:, 4 + n % 2, k * P:(k + 1) * P], WW[n // 2 % 2][:, (4 * (n % 2) + k) * P:(4 * (n % 2) + k + 1) * P], ident[:, :])
                    mm.then_inc(S("s_w_tp"), 1)
                if n:
                    a = n - 1
                    pe.wait_ge(S("s_wt_ready"), B("s_wt_ready") + n)
                    if a >= 2:
                        pe.wait_ge(S("s_v_ready"), B("s_v_ready") + a - 1)
                    for k in range(4):
                        g = (4 * a + k) % GROUPS
                        mm = nc.tensor.matmul(PS[:, 6 + a % 2, k * NCH:(k + 1) * NCH], WT[:, 4 * (a % 2) + k, :], U[:, g, :], start=True, stop=True)
                    mm.then_inc(S("s_v_mm"), 1)
            pe.wait_ge(S("s_v_ready"), B("s_v_ready") + units)

            def taps(n):
                pe.wait_ge(S("s_cc_ready"), B("s_cc_ready") + n + 1)
                if n:
                    pe.wait_ge(S("s_kk_ready"), B("s_kk_ready") + n)
                bb, cc = BB2[n % 2], CC[n % 2]
                for k in range(QB):
                    ps = PS[0:GI, k // 2, (k % 2) * 240:(k % 2 + 1) * 240]
                    nc.tensor.matmul(ps[:, 0:112], bb[:, 1, k, :], cc[:, 1, k, 1:8, :].rearrange("p j i -> p (j i)"), start=True, stop=True)
                    nc.tensor.matmul(ps[:, 112:240], bb[:, 0, k, :], cc[:, 0, k, 0:8, :].rearrange("p j i -> p (j i)"), start=True, stop=False)
                    mm = nc.tensor.matmul(ps[:, 112:128], bb[:, 1, k, :], cc[:, 1, k, 8, :], start=False, stop=True)
                mm.then_inc(S("s_kk_mm"), 1)

            def outputs(n, k):
                return PS[0:LC, 4 + 2 * (n % 2) + k // 4, (k % 4) * P:(k % 4 + 1) * P]

            for n in range(GROUPS // QB + 1):
                if n < GROUPS // QB:
                    taps(n)
                    if n == 0:
                        pe.wait_ge(S("s_fwd_done"), B("s_fwd_done") + 1)
                        pe.wait_ge(S("s_bwd_done"), B("s_bwd_done") + 2)
                    if n >= 2:
                        pe.wait_ge(S("s_y_ready"), B("s_y_ready") + n - 1)
                    for k in range(QB):
                        g, cc = n * QB + k, CC[n % 2]
                        nc.tensor.matmul(outputs(n, k), VST[:, 0:LC, g], cc[:, 0, k, 1:9, :].rearrange("p j i -> p (j i)"), start=k % 4 == 0, stop=False, skip_group_check=True)
                        mm = nc.tensor.matmul(outputs(n, k), VST[:, 2:LC + 2, GROUPS + g], cc[:, 1, k, 0:8, :].rearrange("p j i -> p (j i)"), start=False, stop=False, skip_group_check=True)
                    mm.then_inc(S("s_st_mm"), 1)
                if n:
                    a = n - 1
                    pe.wait_ge(S("s_t_in"), B("s_t_in") + 16 * L * n)
                    for k in range(QB):
                        g = a * QB + k
                        mm = nc.tensor.matmul(outputs(a, k), U[:, g, 0:LC], TZ[:, g, :], start=False, stop=k % 4 == 3, skip_group_check=True)
                    mm.then_inc(S("s_y_mm"), 1)
            pe.wait_ge(S("s_gelu"), B("s_gelu") + GROUPS // QB)
            for t in range(L):
                if t >= 4:
                    pe.wait_ge(S("s_yt"), B("s_yt") + t - 3)
                for j in range(DC):
                    mm = nc.tensor.transpose(PS[:, t % 4, j * LC:(j + 1) * LC], HC[0:LC, t, j::DC], ident[0:LC, 0:LC])
                mm.then_inc(S("s_yt_tp"), 1)
            pe.wait_ge(S("s_yt"), B("s_yt") + L)
            pe.wait_ge(S("s_y_ready"), B("s_y_ready") + GROUPS // QB)
            for n in range(2 * LT):
                h, m = n // LT, n % LT
                pe.wait_ge(S(f"s_wg_in{h}"), B(f"s_wg_in{h}") + 32)
                if n >= 2:
                    pe.wait_ge(S("s_z"), B("s_z") + n - 1)
                for w in range(2):
                    for j in range(DC):
                        mm = nc.tensor.matmul(PS[:, 4 + 2 * (n % 2) + w, :], YT[:, j, m * P:(m + 1) * P], WG[h][:, j, w, :], start=j == 0, stop=j == DC - 1)
                mm.then_inc(S("s_glu_mm"), 1)
            pe.wait_ge(S("s_z"), B("s_z") + 2 * LT)

        @block.tensor
        def _(pe):
            pe.wait_ge(S("cs_ready"), 1)
            pe.wait_ge(S("const_in"), 5 * 16)
            for n in range(ADA_T):
                pe.wait_ge(S(f"ada_in{n % 3}"), 16 * (n // 3 + 1))
                if n >= 4:
                    pe.wait_ge(S("ada_ev"), n - 3)
                for j in range(DC):
                    mm = nc.tensor.matmul(PS[0:2, n % 4, :], csl[:, j, :], ada_slot(n)[:, j, :], start=j == 0, stop=j == DC - 1)
                mm.then_inc(S("ada_mm"), 1)
            pe.wait_ge(S("ada_ev"), ADA_T)
            pe.wait_ge(S("w_dqkv_in"), 16)
            for t in range(AT + 2):
                if t < AT:
                    pe.wait_ge(S("a_h_ready"), t + 1)
                    if t >= 1:
                        pe.wait_ge(S("a_ht"), 2 * t)
                    pe_transposes(H[t % 2], bank2(0), DC, S("a_tp"))
                if 1 <= t <= AT:
                    a = t - 1
                    pe.wait_ge(S("a_ht"), 2 * (a + 1))
                    if a >= 2:
                        pe.wait_ge(S("ca_ready"), a - 1)
                    for lo, hi in ((0, 512), (512, AW)):
                        for j in range(DC):
                            mm = nc.tensor.matmul(PS[:, 4 + 2 * (a % 2) + lo // 512, 0:hi - lo], HT[:, j, a * P:(a + 1) * P],
                                                  w_dqkv[:, j, lo:hi], start=j == 0, stop=j == DC - 1)
                    mm.then_inc(S("a_mm"), 1)
                if t >= 2:
                    a = t - 2
                    pe.wait_ge(S("ca_ready"), a + 1)
                    if a >= 1:
                        pe.wait_ge(S("ct_ready"), a)
                    ct = bank2(2)
                    for j in range(QC):
                        nc.tensor.transpose(ct[:, j * P:(j + 1) * P], CA[:, j:QL:QC], ident[:, :])
                    for j in range(KC):
                        nc.tensor.transpose(ct[:, (QC + j) * P:(QC + j + 1) * P], CA[:, QL + j:QL + KVL:KC], ident[:, :])
                    nc.tensor.transpose(ct[0:ROPE, (QC + KC) * P:(QC + KC + 1) * P], CA[:, QL + KVL:AW], ident[:, :])\
                        .then_inc(S("ct_tp"), 1)
            pe.wait_ge(S("ct_ready"), AT)
            pe.wait_ge(S("w_ukv_in"), 16)
            for n in range(2 * AT):
                t, half = n // 2, n % 2
                if n >= 4:
                    pe.wait_ge(S("v_ready_a"), (n - 3 + 1) // 2)
                    pe.wait_ge(S("v_ready_v"), (n - 3) // 2)
                for j in range(KC):
                    rhs = w_ukv[:, j, :].rearrange("p (h x) -> p h x", x=NOPE + VD)[:, 4 * half:4 * half + 4, NOPE:NOPE + VD]
                    mm = nc.tensor.matmul(PS[:, 4 + n % 4, :], CKT[:, j, t * P:(t + 1) * P], rhs, start=j == 0, stop=j == KC - 1)
                mm.then_inc(S("v_mm"), 1)

            def rotate(dst, src, done):
                nc.tensor.matmul(dst[:, 0:512], rot[:, :], src[:, 0:512], start=True, stop=True)
                nc.tensor.matmul(dst[:, 512:N_ALL], rot[:, :], src[:, 512:N_ALL], start=True, stop=True).then_inc(done, 1)

            pe.wait_ge(S("v_ready_a"), AT)
            pe.wait_ge(S("v_ready_v"), AT)
            rotate(bank2(6)[0:ROPE], KPT, S("k_rot"))
            pe.wait_ge(S("w_uq_in"), 16)

            def project(dst, w, col, m, src, n, done):
                for lo, hi in ((0, 512), (512, N_ALL)):
                    for j in range(n):
                        mm = nc.tensor.matmul(dst[0:m, lo:hi], w[:, j, col:col + m], src[:, j, lo:hi], start=j == 0, stop=j == n - 1)
                mm.then_inc(done, 1)

            for h in range(HEADS):
                if h:
                    pe.wait_ge(S("p_ready"), AT * h)
                    pe.wait_ge(S("pt_ready"), AT * h)
                    pe.wait_ge(S("q_rope"), h)
                project(bank2(4), w_uq, h * (NOPE + ROPE) + NOPE, ROPE, CQT, QC, S("qp_mm"))
                project(bank2(2), w_ukv, h * (NOPE + VD), NOPE, CKT, KC, S("kn_mm"))
                pe.wait_ge(S("qp_ready"), h + 1)
                if h == 0:
                    pe.wait_ge(S("k_rope"), 1)
                if h:
                    pe.wait_ge(S("ot_lat"), h)
                    pe.wait_ge(S("ot_ctx"), h)
                rotate(bank2(6)[0:ROPE], qpT, S("q_rot"))
                project(bank2(0), w_uq, h * (NOPE + ROPE), NOPE, CQT, QC, S("qn_mm"))
                pe.wait_ge(S("qn_ready"), h + 1)
                pe.wait_ge(S("kn_ready"), h + 1)
                pe.wait_ge(S("q_rope"), h + 1)
                for t in range(AT + 1):
                    if t < AT:
                        k = h * AT + t
                        if k >= 2:
                            pe.wait_ge(S("p_exp"), k - 1)
                        q0, nk = (N_CTX + t * P, N_ALL) if t < LT else ((t - LT) * P, N_CTX)
                        dst = bank2(2 * (t % 2))
                        for lo, hi in ((0, 512), (512, N_ALL)):
                            hi = min(hi, nk)
                            if lo < hi:
                                nc.tensor.matmul(dst[:, lo:hi], qnT[:, q0:q0 + P], knT[:, lo:hi], start=True, stop=False)
                                mm = nc.tensor.matmul(dst[:, lo:hi], qpR[:, q0:q0 + P], KPR[:, lo:hi], start=False, stop=True)
                        mm.then_inc(S("s_mm"), 1)
                    if t == LT + 1:
                        pe.wait_ge(S("pt_ready"), h * AT + LT)
                        for c in range(AT):
                            mm = nc.tensor.matmul(PS[:, 6, :], V[:, c, h * P:(h + 1) * P], PT[:, c, :], start=c == 0, stop=c == AT - 1)
                        mm.then_inc(S("pv_lat"), 1)
                    if t >= 1:
                        k = h * AT + t - 1
                        pe.wait_ge(S("p_ready"), k + 1)
                        if k:
                            pe.wait_ge(S("pt_ready"), k)
                        nk = AT if t - 1 < LT else CT
                        for c in range(nk):
                            mm = nc.tensor.transpose(bank2(4)[:, c * P:(c + 1) * P], PR[(t - 1) % 2][:, c * P:(c + 1) * P], ident[:, :])
                        mm.then_inc(S("p_tp"), 1)
                pe.wait_ge(S("pt_ready"), (h + 1) * AT)
                for c in range(CT):
                    mm = nc.tensor.matmul(PS[:, 7, 0:N_CTX], V[:, c, h * P:(h + 1) * P], PT[:, c, 0:N_CTX], start=c == 0, stop=c == CT - 1)
                mm.then_inc(S("pv_ctx"), 1)
            pe.wait_ge(S("w_o_in"), 16)
            pe.wait_ge(S("ot_lat"), HEADS)
            pe.wait_ge(S("ot_ctx"), HEADS)
            for t in range(AT + 3):
                if t < AT:
                    if t >= 2:
                        pe.wait_ge(S("o_used"), t - 1)
                    for half in range(2):
                        for h in range(HEADS):
                            mm = nc.tensor.matmul(PS[:, 2 * (t % 2) + half, :], OT[:, h, t * P:(t + 1) * P],
                                                  w_o[:, h, half * 512:(half + 1) * 512], start=h == 0, stop=h == HEADS - 1)
                    mm.then_inc(S("o_mm"), 1)
                if t >= 2:
                    front_pe(pe, 0, t - 2)
            pe.wait_ge(S("o_used"), AT)
            moe_pe(pe, 0)
            s5_pe(pe)
            moe_pe(pe, 1)

        def norm_act(act, A, l, n):
            if l == 0:
                act.wait_ge(S("x1_ready"), n + 1)
            else:
                act.wait_ge(S("x3_ready"), B("x3_ready") + n + 1)
            A(act.activation(junk[:, :], X[:, n, :], ACT.Square, accum_out=ss[:, n:n + 1]))
            act.activation(sd[:, n:n + 1], ss[:, n:n + 1], ACT.Sqrt, scale=1.0 / D, bias=eps[:, 0:1]).then_inc(S("m_sd"), 1)

        def turned_act(act, l, n):
            act.wait_ge(S("m_ht_tp"), before_moe(l)("ht_tp") + n + 1)
            for k in range(2):
                act.activation(HT[:, 4 * k:4 * k + 4, n * P:(n + 1) * P],
                               PS[:, 4 + k, :].rearrange("p (j n) -> p j n", j=4), ACT.Copy).then_inc(S("m_ht_ready"), 1)

        def moe_act(act, A, l):
            tiles, NT = TILES[l], len(TILES[l])
            g, Z = "m_", before_moe(l)
            if l:
                for n in range(NT):
                    norm_act(act, A, l, n)
                for n in range(NT):
                    turned_act(act, l, n)
            act.wait_ge(S(g + "logits"), Z("logits") + NT)
            act.activation(SC[:, 0:NT, :], PS[:, 7, 0:NT * 64].rearrange("p (t e) -> p t e", t=NT), ACT.Sigmoid).then_inc(S(g + "scores"), 1)
            for n in range(NT):
                act.wait_ge(S(g + "sh_gu"), Z("sh_gu") + n + 1)
                if n >= 2:
                    act.wait_ge(S(g + "sh_h"), Z("sh_h") + n - 1)
                act.activation(SG[n % 2], PS[:, 4 + n % 2, 0:FE], ACT.Silu)
                act.activation(UP[n % 2], PS[:, 4 + n % 2, FE:2 * FE], ACT.Copy).then_inc(S(g + "sh_silu"), 1)
                act.wait_ge(S(g + "sh_tp"), Z("sh_tp") + n + 1)
                if n >= 2:
                    act.wait_ge(S(g + "sh_down"), Z("sh_down") + n - 1)
                act.activation(HHT[n % 2], PS[:, 6, 0:FE].rearrange("p (j n) -> p j n", j=FC), ACT.Copy).then_inc(S(g + "sh_ht"), 1)
                act.wait_ge(S(g + "sh_down"), Z("sh_down") + n + 1)
                if n == 0:
                    for k in range(2):
                        act.wait_ge(S(g + f"f_out{k}"), Z(f"f_out{k}") + NT // 2 * 16)
                if n >= 2:
                    act.wait_ge(S(g + f"acc_out{n % 2}"), Z(f"acc_out{n % 2}") + n // 2 * 16)
                act.activation(H[n % 2], bank2(2 * (n % 2)), ACT.Copy).then_inc(S(g + "so_ready"), 1)

            act.sem_inc(S(f"out_a{l}"), 1)
            act.wait_ge(S(g + "sh_down"), Z("sh_down") + NT)
            act.wait_ge(S(f"xt_tp{l}"), 1)
            act.activation(XT[0], bank2(0).rearrange("p (j n) -> p j n", j=DC), ACT.Copy).then_inc(S(f"xt_ready{l}"), 1)
            pairs, most = pairs_of(act, l)

            def output(u, block):
                act.wait_ge(S(f"dn_mm{l}"), block)
                act.wait_ge(S(f"kept{l}"), block)
                act.activation(OS[u][:, 0:512], PS[:, 4, :], ACT.Copy, scale=gates[:, u:u + 1]).then_inc(S(f"out_a{l}"), 1)

            def pair(i, first):
                for u in range(2):
                    b = i * 2 + u
                    act.wait_ge(S(f"gu_mm{l}"), b + 1)
                    act.activation(SG[u], PS[:, 2 + u, 0:FE], ACT.Silu).then_inc(S(f"silu{l}"), 1)
                    act.wait_ge(S(f"xt_tp{l}"), b + 2)
                    act.activation(XT[1 - u], bank2(0).rearrange("p (j n) -> p j n", j=DC), ACT.Copy).then_inc(S(f"xt_ready{l}"), 1)
                    if not (first and u == 0):
                        output(1 - u, b)

            pair(0, True)
            with act.Fori(0, -(-most // TURNS)) as q:
                with act.If(pairs - q * TURNS > 1):
                    with act.Fori(1, TURNS + 1) as r:
                        i = q * TURNS + r
                        with act.If(pairs - i > 0):
                            pair(i, False)
            output(1, act.snap(pairs * 2, min_val=1, max_val=2 * most))
            for n in range(NT):
                act.wait_ge(S(g + f"acc_in{2 * n // NT}"), Z("acc_in0") + 16 * NT // 2)
                A(act.activation(junk[:, :], SUM[n], ACT.Square, accum_out=ss[:, n:n + 1]))
                act.activation(sd[:, n:n + 1], ss[:, n:n + 1], ACT.Sqrt, scale=1.0 / D, bias=eps[:, 0:1]).then_inc(S(g + "o_sd"), 1)


        def s5_act(act, A):
            for t in range(AT):
                act.wait_ge(S("m_x_ready"), t + 1)
                A(act.activation(junk[:, :], X[:, t, :], ACT.Square, accum_out=ss[:, t:t + 1]))
            act.activation(sd[:, 0:AT], ss[:, 0:AT], ACT.Sqrt, scale=1.0 / D, bias=eps[:, 0:1]).then_inc(S("s_sd"), 1)
            act.wait_ge(S("s_par_in"), B("s_par_in") + 16)
            act.activation(tEA, LST, ACT.Exp).then_inc(S("s_tab_a"), 1)
            act.wait_ge(S("s_tab_v"), B("s_tab_v") + 1)
            act.activation(tEA, tA, ACT.Exp).then_inc(S("s_tab_a"), 1)
            act.activation(tR, tR, ACT.Sin).then_inc(S("s_tab_a"), 1)
            act.activation(tR2, tR2, ACT.Sin).then_inc(S("s_tab_a"), 1)
            act.wait_ge(S("s_hc_in"), B("s_hc_in") + 32)
            for k in range(GROUPS // 4 + 1):
                if k < GROUPS // 4:
                    if k >= 2:
                        act.wait_ge(S("s_u_tp"), B("s_u_tp") + k - 1)
                    act.activation(HG[k % 2][0:NCH].rearrange("p (g t i) -> p g t i", g=4, t=L),
                                   HC[0:NCH, :, k * 64:k * 64 + 64].rearrange("p t (g i) -> p g t i", g=4), ACT.Copy).then_inc(S("s_hg_ready"), 1)
                if k == 0:
                    continue
                n = k - 1
                act.wait_ge(S("s_u_tp"), B("s_u_tp") + n + 1)
                act.activation(U[:, 4 * n:4 * n + 4, :], PS[:, n % 4, 0:4 * NCH].rearrange("p (g c) -> p g c", g=4), ACT.Copy)\
                    .then_inc(S("s_u_ready"), 1)
            units = Q // 4
            for n in range(units + 1):
                if n < units:
                    act.wait_ge(S("s_w_tp"), B("s_w_tp") + n + 1)
                    if n >= 2:
                        act.wait_ge(S("s_v_mm"), B("s_v_mm") + n - 1)
                    act.activation(WT[:, 4 * (n % 2):4 * (n % 2) + 4, :], PS[:, 4 + n % 2, :].rearrange("p (k n) -> p k n", k=4), ACT.Copy)\
                        .then_inc(S("s_wt_ready"), 1)
                if n:
                    a = n - 1
                    act.wait_ge(S("s_v_mm"), B("s_v_mm") + n)
                    act.activation(VST[:, 1:NCH + 1, 4 * a:4 * a + 4].rearrange("p s q -> p q s"),
                                   PS[:, 6 + a % 2, 0:4 * NCH].rearrange("p (q s) -> p q s", q=4), ACT.Copy).then_inc(S("s_v_ready"), 1)
            for n in range(GROUPS // QB + 2):
                if n < GROUPS // QB:
                    act.wait_ge(S("s_kk_mm"), B("s_kk_mm") + n + 1)
                    if n == 0:
                        act.wait_ge(S("s_hd"), B("s_hd") + 1)
                    else:
                        act.wait_ge(S("s_t_in"), B("s_t_in") + 16 * L * n)
                    act.activation(KKS.rearrange("p (b w) n -> p b (w n)", w=2), PS[0:GI, 0:4, 0:480], ACT.Copy).then_inc(S("s_kk_ready"), 1)
                if n >= 2:
                    a = n - 2
                    act.wait_ge(S("s_y_ready"), B("s_y_ready") + a + 1)
                    y = HC[0:LC, :, a * QB * GI:(a + 1) * QB * GI]
                    act.activation(y, y, ACT.Gelu_apprx_tanh).then_inc(S("s_gelu"), 1)
            for n in range(2 * LT):
                act.wait_ge(S("s_z"), B("s_z") + n + 1)
                act.activation(ZT[n % 2][:, 512:1024], ZT[n % 2][:, 512:1024], ACT.Sigmoid).then_inc(S("s_sig"), 1)
            for m in range(LT):
                act.wait_ge(S("s_oo"), B("s_oo") + LT + m + 1)
                A(act.activation(junk[:, :], OO[:, m, :], ACT.Square, accum_out=ss[:, 8 + m:9 + m]))
                act.activation(sd[:, 8 + m:9 + m], ss[:, 8 + m:9 + m], ACT.Sqrt, scale=1.0 / D, bias=eps[:, 0:1]).then_inc(S("s_osd"), 1)

        @block.scalar
        def _(act):
            A = Steps(act, S("act_step"))
            act.wait_ge(S("const_in"), 5 * 16)
            act.activation(csl[:, :, :], cs[:, :, :], ACT.Silu).then_inc(S("cs_ready"), 1)
            for t in range(AT):
                act.wait_ge(S("x_in"), 16 * AT)
                A(act.activation(junk[:, :], X[:, t, :], ACT.Square, accum_out=ss[:, t:t + 1]))
            act.wait_ge(S("eps_ready"), 1)
            act.activation(sd[:, 0:AT], ss[:, 0:AT], ACT.Sqrt, scale=1.0 / D, bias=eps[:, 0:1]).then_inc(S("a_sd"), 1)
            act.wait_ge(S("mod_out"), 32)
            for t in range(AT + 1):
                if t < AT:
                    act.wait_ge(S("a_tp"), t + 1)
                    for k in range(2):
                        act.activation(HT[:, 4 * k:4 * k + 4, t * P:(t + 1) * P],
                                       PS[:, k, :].rearrange("p (j n) -> p j n", j=4), ACT.Copy).then_inc(S("a_ht"), 1)
                if t:
                    a = t - 1
                    b = 4 + 2 * (a % 2)
                    act.wait_ge(S("a_mm"), a + 1)
                    if a:
                        act.wait_ge(S("c_sd"), a)
                    act.activation(junk[:, 0:QL], bank2(b)[:, 0:QL], ACT.Square, scale=QL ** -0.5, accum_out=ss[:, 0:1])
                    A(act.activation(junk[:, QL:QL + KVL], bank2(b)[:, QL:QL + KVL], ACT.Square, scale=KVL ** -0.5, accum_out=ss[:, 1:2]))
                    if a:
                        act.wait_ge(S("ca_ready"), a)
                    act.activation(sd[:, 6:8], ss[:, 0:2], ACT.Sqrt, bias=eps[:, 0:1]).then_inc(S("c_sd"), 1)
            for n in range(0, 2 * AT, 2):
                act.wait_ge(S("v_mm"), n + 1)
                act.activation(V[:, n // 2, 0:512], PS[:, 4 + n % 4, :], ACT.Copy).then_inc(S("v_ready_a"), 1)
            for h in range(HEADS):
                act.wait_ge(S("qp_mm"), h + 1)
                act.activation(qpT, bank2(4, N_ALL)[0:ROPE], ACT.Copy).then_inc(S("qp_ready"), 1)
                act.wait_ge(S("qn_mm"), h + 1)
                act.activation(qnT, bank2(0, N_ALL), ACT.Copy).then_inc(S("qn_ready"), 1)
                for t in range(AT + 1):
                    if t < AT:
                        k = h * AT + t
                        nk = N_ALL if t < LT else N_CTX
                        act.wait_ge(S("nmax"), k + 1)
                        if k >= 2:
                            act.wait_ge(S("p_tp"), k - 1)
                        act.activation(PR[t % 2][:, 0:nk], bank2(2 * (t % 2), nk), ACT.Exp, bias=mx[:, t % 2:t % 2 + 1],
                                       scale=SCALE, accum_out=sm[:, t % 2:t % 2 + 1]).then_inc(S("p_exp"), 1)
                    if t:
                        k = h * AT + t - 1
                        nk = AT if t - 1 < LT else CT
                        act.wait_ge(S("p_tp"), k + 1)
                        if t - 1 == 0 and h:
                            act.wait_ge(S("pv_ctx"), h)
                        if t - 1 == LT:
                            act.wait_ge(S("pv_lat"), h + 1)
                        q0 = (t - 1) * P if t - 1 < LT else (t - 1 - LT) * P
                        act.activation(PT[:, 0:nk, q0:q0 + P], bank2(4, nk * P).rearrange("p (c q) -> p c q", c=nk), ACT.Copy)\
                            .then_inc(S("pt_ready"), 1)
                act.wait_ge(S("pv_lat"), h + 1)
                act.activation(OT[:, h, N_CTX:N_ALL], PS[:, 6, :], ACT.Copy).then_inc(S("ot_lat"), 1)
                act.wait_ge(S("pv_ctx"), h + 1)
                act.activation(OT[:, h, 0:N_CTX], PS[:, 7, 0:N_CTX], ACT.Copy).then_inc(S("ot_ctx"), 1)
            for t in range(AT + 3):
                if t < AT:
                    act.wait_ge(S("o_mm"), t + 1)
                    A(act.activation(junk[:, :], bank2(2 * (t % 2)), ACT.Square, accum_out=ss[:, 8 + t:9 + t]))
                    act.activation(sd[:, 8 + t:9 + t], ss[:, 8 + t:9 + t], ACT.Sqrt, scale=1.0 / D, bias=eps[:, 0:1]).then_inc(S("o_sd"), 1)
                if 1 <= t <= AT:
                    norm_act(act, A, 0, t - 1)
                if 2 <= t < AT + 2:
                    turned_act(act, 0, t - 2)
            moe_act(act, A, 0)
            s5_act(act, A)
            moe_act(act, A, 1)

        def input_dve(v, W, modulated, l, n):
            Z = before_moe(l)

            def h_free(n):
                v.wait_ge(S("m_ht_tp"), Z("ht_tp") + n - 1)
                v.wait_ge(S(f"m_f_out{n % 2}"), Z(f"f_out{n % 2}") + n // 2 * 16)

            v.wait_ge(S("m_sd"), Z("sd") + n + 1)
            W(v.reciprocal(rs[:, n:n + 1], sd[:, n:n + 1]))
            modulated(n, TILES[l][n], 0 if l else stream[n], h_free, S("m_h_ready"))

        def moe_dve(v, W, modulated, l):
            tiles, NT = TILES[l], len(TILES[l])
            g, Z = "m_", before_moe(l)
            if l:
                v.wait_ge(S("s_rown"), B("s_rown") + 32)
                for n in range(NT):
                    input_dve(v, W, modulated, l, n)
            v.wait_ge(S(g + "h_ready"), Z("h_ready") + NT)
            W(v.memset(row(0), 0.0))
            v.sem_inc(S(g + "zero_ready"), 1)
            v.memset(GS[:, :, 8:16], BIG)
            v.memset(TR[:, :, 4:8], BIG)
            v.memset(POSM[:, :, N_EXP:EPAD], -1.0)
            v.memset(RH[:, :, N_EXP:EPAD, :], 0.0)
            v.memset(RH[:, :, 0:N_EXP, 0:1], 1.0)
            for n in range(NT):
                v.memset(RH[:, n, 0:N_EXP, 2:3], float(n))
            v.tensor_copy(RH[:, 0:NT, 0:N_EXP, 1:2], cst[:, 0:1].unsqueeze(2).unsqueeze(3).to_broadcast((P, NT, N_EXP, 1)))
            v.wait_ge(S(g + "scores"), Z("scores") + 1)
            N = slice(0, NT)
            W(v.tensor_tensor(BI[:, N], SC[:, N], BROW[:, :].unsqueeze(1).to_broadcast((P, NT, N_EXP)), ALU.add))
            for n in range(NT):
                for q in range(8):
                    ins = v.max(M8[:, n, q, :], BI[:, n, q * 8:(q + 1) * 8])
            W(ins)
            W(v.tensor_tensor(GS[:, N, 0:8], M8[:, N, :, 0], M8[:, N, :, 1], ALU.add))
            for n in range(NT):
                ins = v.max(G8[:, n, :], GS[:, n, 0:8])
            W(ins)
            W(v.tensor_copy(TR[:, N, 0:4], G8[:, N, 0:4]))
            for n in range(NT):
                ins = v.match_replace(GR[:, n, :], TR[:, n, :], GS[:, n, :], -BIG)
            W(ins)
            W(v.tensor_scalar(GM[:, N], GR[:, N, 0:8], -BIG, None, ALU.is_equal))
            W(v.tensor_scalar(TB[:, N], GM[:, N], BIG, -BIG, ALU.mult, ALU.add))
            for n in range(NT):
                b3 = BI[:, n, :].rearrange("p (q k) -> p q k", q=8)
                ins = v.tensor_tensor(b3, b3, GM[:, n, :].unsqueeze(2).to_broadcast((P, 8, 8)), ALU.mult)
            W(ins)
            for n in range(NT):
                b3 = BI[:, n, :].rearrange("p (q k) -> p q k", q=8)
                ins = v.tensor_tensor(b3, b3, TB[:, n, :].unsqueeze(2).to_broadcast((P, 8, 8)), ALU.add)
            W(ins)
            for n in range(NT):
                ins = v.max(E8[:, n, :], BI[:, n, :])
            W(ins)
            for n in range(NT):
                ins = v.match_replace(MR[:, n, :], E8[:, n, :], BI[:, n, :], -2 * BIG)
            W(ins)
            W(v.tensor_scalar(MR[:, N], MR[:, N], -2 * BIG, None, ALU.is_equal))
            W(v.tensor_copy(MB16[:, N], MR[:, N]))
            v.sem_inc(S(g + "mask_ready"), 1)
            W(v.tensor_tensor(GTE[:, N], SC[:, N], MR[:, N], ALU.mult))
            W(v.tensor_reduce(sm[:, 0:NT], GTE[:, N], AX_X, ALU.add))
            W(v.reciprocal(sm[:, 0:NT], sm[:, 0:NT]))
            W(v.tensor_tensor(GTE[:, N], GTE[:, N], sm[:, 0:NT].unsqueeze(2).to_broadcast((P, NT, N_EXP)), ALU.mult))
            W(v.tensor_scalar(GTE[:, N], GTE[:, N], ROUTED, None, ALU.mult))
            for c in (3, 4, 5):
                W(v.tensor_copy(RH[:, N, 0:N_EXP, c], GTE[:, N]))
                if c < 5:
                    W(v.tensor_tensor(GTE[:, N], GTE[:, N], RH[:, N, 0:N_EXP, c], ALU.subtract))
            v.wait_ge(S(g + "pos_mm"), Z("pos_mm") + 1)
            pos = PS[:, 7, 0:NT * 64].rearrange("p (t e) -> p t e", t=NT)
            W(v.scalar_tensor_tensor(POSM[:, N, 0:N_EXP], pos, 1.0, MR[:, N], ALU.add, ALU.mult))
            W(v.tensor_scalar(POSM[:, N, 0:N_EXP], POSM[:, N, 0:N_EXP], -1.0, None, ALU.add))
            W(v.tensor_copy(CNT, PS[:, 7, 384:448]))
            W(v.tensor_scalar(NB, CNT, float(P), 1.0, ALU.is_gt, ALU.add))
            for b in range(2, NT):
                W(v.scalar_tensor_tensor(NB, CNT, float(P * b), NB, ALU.is_gt, ALU.add))
            W(v.tensor_tensor_scan(END, cst[:, 72:73].to_broadcast((P, N_EXP)), NB, 0.0, ALU.mult, ALU.add))
            v.tensor_copy(ends[0:1, :], END[0:1, :])
            W(v.tensor_scalar(CNT, END, cst[:, 0:1], None, ALU.is_le))
            v.tensor_reduce(TAB[:, 0:1], CNT, AX_X, ALU.add)
            W(v.tensor_tensor(CNT, CNT, NB, ALU.mult))
            W(v.tensor_reduce(TAB[:, 1:2], CNT, AX_X, ALU.add))
            W(v.tensor_scalar(TAB[:, 1:2], TAB[:, 1:2], cst[:, 0:1], -float(P), ALU.subtract, ALU.mult))
            v.tensor_scalar(DG[:, 0:P], ident[:, :], TAB[:, 0:1], None, ALU.mult)
            W(v.tensor_scalar(DG[:, P:2 * P], ident[:, :], TAB[:, 1:2], None, ALU.mult))
            v.sem_inc(S(g + "ends_ready"), 1)
            v.wait_ge(S(g + "tab_mm"), Z("tab_mm") + 1)
            v.tensor_copy(SHIFT, PS[:, 7, P:2 * P])
            experts = PS[0:1, 7, 0:P].rearrange("p (a b) -> p a b", b=2)
            W(v.tensor_copy(CNT[0:1, :], experts[:, :, 0]))
            W(v.scalar_tensor_tensor(CNT[0:1, :], experts[:, :, 1], float(P), CNT[0:1, :], ALU.mult, ALU.add))
            W(v.tensor_copy(words[0:1, :], CNT[0:1, :]))
            v.sem_inc(S(g + "tab_ready"), 1)
            trash = 2 + l

            def slots(u, done, W):
                W(v.tensor_copy(it[:, 0:6], PS[:, 7, 0:6]))
                W(v.scalar_tensor_tensor(it[:, 6:7], it[:, 2:3], float(P), it[:, 1:2], ALU.mult, ALU.add))
                W(v.scalar_tensor_tensor(it[:, 6:7], it[:, 0:1], cst[:, trash + 2:trash + 3], it[:, 6:7], ALU.mult, ALU.add))
                v.tensor_tensor(it[:, 7:8], it[:, 4:5], it[:, 5:6], ALU.add)
                W(v.tensor_scalar(idxg[:, u:u + 1], it[:, 6:7], cst[:, trash:trash + 1], None, ALU.add))
                v.tensor_tensor(gateg[:, u:u + 1], it[:, 7:8], it[:, 3:4], ALU.add).then_inc(done, 1)

            def one_hot(k, e, b):
                for n in range(NT):
                    ins = v.tensor_scalar(OH[k][:, n, :], iota_b[:, :], SHIFT[:, bass.ds(b, 1)], POSM[:, n, bass.ds(e, 1)], ALU.add, ALU.is_equal)
                ins.then_inc(S(f"oh_ready{l}"), 1)

            v.sem_inc(S(f"h_ready{l}"), 2)
            v.sem_inc(S(f"hht_ready{l}"), 1)
            v.sem_inc(S(f"out_v{l}"), 1)
            pairs, most = pairs_of(v, l)
            word = v.value_load(words[0:1, 0:1], min_val=0, max_val=2 ** 14 - 1)
            for b in range(2):
                one_hot(b, expert_of(v, word, b), b)
                v.wait_ge(S(f"idx_mm{l}"), b + 1)
                slots(b, S(f"idx_ready{l}"), W)

            def output(u, block):
                v.wait_ge(S(f"dn_mm{l}"), block)
                v.tensor_scalar(OS[u][:, 512:1024], PS[:, 5, :], gates[:, u:u + 1], None, ALU.mult).then_inc(S(f"out_v{l}"), 1)

            def pair(i, first):
                ahead = v.value_load(words[0:1, bass.ds(i + 1, 1)], min_val=0, max_val=2 ** 14 - 1)
                LW = Steps(v, S(f"slot_step{l}"))
                LW.off = i * 10
                for u in range(2):
                    b = i * 2 + u
                    e2 = expert_of(v, ahead, u)
                    b2 = b + 2 if first else v.snap(b + 2, min_val=2, max_val=P - 1)
                    v.wait_ge(S(f"idx_mm{l}"), b + 1)
                    one_hot(u, e2, b2)
                    v.wait_ge(S(f"silu{l}"), b + 1)
                    v.tensor_tensor(HH[u], SG[u], PS[:, 2 + u, FE:2 * FE], ALU.mult).then_inc(S(f"h_ready{l}"), 1)
                    v.wait_ge(S(f"h_tp{l}"), b + 1)
                    v.tensor_copy(HHT[u], PS[:, 6, 0:FE].rearrange("p (j n) -> p j n", j=FC)).then_inc(S(f"hht_ready{l}"), 1)
                    v.wait_ge(S(f"os_free{l}"), b + 1)
                    v.wait_ge(S(f"idx_ready{l}"), b + 1)
                    v.tensor_copy(idxs[:, u:u + 1], idxg[:, u:u + 1])
                    LW(v.tensor_copy(gates[:, u:u + 1], gateg[:, u:u + 1]))
                    v.sem_inc(S(f"kept{l}"), 1)
                    v.wait_ge(S(f"idx_mm{l}"), b + 3)
                    v.wait_ge(S(f"xt_tp{l}"), b + 1)
                    slots(u, S(f"idx_ready{l}"), LW)
                    if not (first and u == 0):
                        output(1 - u, b)

            pair(0, True)
            with v.Fori(0, -(-most // TURNS)) as q:
                with v.If(pairs - q * TURNS > 1):
                    with v.Fori(1, TURNS + 1) as r:
                        i = q * TURNS + r
                        with v.If(pairs - i > 0):
                            pair(i, False)
            output(1, v.snap(pairs * 2, min_val=1, max_val=2 * most))
            v.wait_ge(S(g + "rows_in"), Z("rows_in") + 32 if l == 0 else 16)
            for n, t in enumerate(tiles):
                v.wait_ge(S(g + "o_sd"), Z("o_sd") + n + 1)
                W(v.reciprocal(rs[:, n:n + 1], sd[:, n:n + 1]))
                W(v.scalar_tensor_tensor(SUM[n], SUM[n], rs[:, n:n + 1], row(stream[t] if l == 0 else 0), ALU.mult, ALU.mult))
                v.tensor_tensor(X[:, t, :], X[:, t, :], SUM[n], ALU.add).then_inc(S(g + "x_ready"), 1)


        def ada1_dve(v, W, r):
            v.wait_ge(S("a1_bias"), 32 * (r + 1))
            if r:
                v.wait_ge(S("a1_out"), 16 * r)
            for m in range(4):
                v.wait_ge(S("a1_mm"), 4 * r + m + 1)
                c = slice(m * 512, (m + 1) * 512)
                v.tensor_tensor(MOD1[:, c], PS[0:2, 4 + m, :], MODB1[:, c], ALU.add).then_inc(S("a1_ev"), 1)
            v.wait_ge(S("a1_ev"), 4 * (r + 1))
            first, second = slice(0, D), slice(D, 2 * D)
            if r == 0:
                W(v.scalar_tensor_tensor(MOD1[:, second], MOD1[:, second], 1.0, NG1[:, first], ALU.add, ALU.mult))
            elif r == 1:
                W(v.tensor_tensor(MOD1[:, first], MOD1[:, first], NG1[:, first], ALU.mult))
            else:
                v.scalar_tensor_tensor(MOD1[:, first], MOD1[:, first], 1.0, NG1[:, first], ALU.add, ALU.mult)
                W(v.tensor_tensor(MOD1[:, second], MOD1[:, second], NG1[:, second], ALU.mult))
            v.sem_inc(S("a1_ready"), 1)

        def s5_dve(v, W, modulated):
            ada1_dve(v, W, 0)
            v.wait_ge(S("s_sd"), B("s_sd") + 1)
            W(v.reciprocal(rs[:, 0:AT], sd[:, 0:AT]))
            v.wait_ge(S("s_rows"), B("s_rows") + 64)
            for t in range(AT):
                modulated(t, t, stream[t], lambda n: v.wait_ge(S(f"s_h_out{n % 2}"), B(f"s_h_out{n % 2}") + n // 2 * 16), S("s_h_ready"))
            ada1_dve(v, W, 1)
            v.wait_ge(S("s_tab_a"), B("s_tab_a") + 1)
            v.tensor_tensor(tA, LRE, tEA, ALU.mult)
            W(v.tensor_tensor(tTH, LIM, tEA, ALU.mult))
            W(v.tensor_scalar(tK, tTH, 1.0 / TWO_PI, ROUND, ALU.mult, ALU.add))
            W(v.tensor_scalar(tK, tK, -ROUND, None, ALU.add))
            W(v.scalar_tensor_tensor(tR, tK, -PI_A, tTH, ALU.mult, ALU.add))
            W(v.scalar_tensor_tensor(tR, tK, -PI_B, tR, ALU.mult, ALU.add))
            W(v.scalar_tensor_tensor(tR, tK, -PI_C, tR, ALU.mult, ALU.add))
            W(v.tensor_scalar(tR2, tR, 0.5 * np.pi, None, ALU.add))
            W(v.tensor_scalar(tM, tR2, float(np.pi), -TWO_PI, ALU.is_gt, ALU.mult))
            W(v.tensor_tensor(tR2, tR2, tM, ALU.add))
            v.tensor_scalar(tR, tR, 3.1415925, -3.1415925, ALU.min, ALU.max)
            W(v.tensor_scalar(tR2, tR2, 3.1415925, -3.1415925, ALU.min, ALU.max))
            v.sem_inc(S("s_tab_v"), 1)
            v.memset(NR[:, 0, :], 1.0)
            v.memset(NI[:, 0, :], 0.0)
            v.wait_ge(S("s_tab_a"), B("s_tab_a") + 4)
            v.tensor_tensor(NR[:, 1, :], tEA, tR2, ALU.mult)
            W(v.tensor_tensor(NI[:, 1, :], tEA, tR, ALU.mult))

            def cmul(dr, di, ar, ai, br, bi, t1, t2):
                v.tensor_tensor(dr, ar, br, ALU.mult)
                v.tensor_tensor(t1, ai, bi, ALU.mult)
                v.tensor_tensor(di, ar, bi, ALU.mult)
                W(v.tensor_tensor(t2, ai, br, ALU.mult))
                v.tensor_tensor(dr, dr, t1, ALU.subtract)
                W(v.tensor_tensor(di, di, t2, ALU.add))

            for k in range(2, L + 1):
                cmul(NR[:, k, :], NI[:, k, :], NR[:, k - 1, :], NI[:, k - 1, :], NR[:, 1, :], NI[:, 1, :], tM, tN)
            v.tensor_scalar(tK, NR[:, 1, :], -1.0, None, ALU.add)
            v.tensor_tensor(tR, LRE, LRE, ALU.mult)
            W(v.tensor_tensor(tR2, LIM, LIM, ALU.mult))
            W(v.tensor_tensor(tR, tR, tR2, ALU.add))
            W(v.reciprocal(tR, tR))
            v.tensor_tensor(tFR, tK, LRE, ALU.mult)
            v.tensor_tensor(tM, NI[:, 1, :], LIM, ALU.mult)
            v.tensor_tensor(tFI, NI[:, 1, :], LRE, ALU.mult)
            W(v.tensor_tensor(tN, tK, LIM, ALU.mult))
            v.tensor_tensor(tFR, tFR, tM, ALU.add)
            W(v.tensor_tensor(tFI, tFI, tN, ALU.subtract))
            v.tensor_tensor(tFR, tFR, tR, ALU.mult)
            W(v.tensor_tensor(tFI, tFI, tR, ALU.mult))
            n8 = slice(0, L)
            tm = TMP[:, 0:1024].rearrange("p (j q) -> p j q", q=Q)

            def wide(t):
                return t.unsqueeze(1).to_broadcast((P, L, Q))

            v.tensor_tensor(GR_, NR[:, n8], wide(tFR), ALU.mult)
            v.tensor_tensor(GI_, NR[:, n8], wide(tFI), ALU.mult)
            W(v.tensor_tensor(tm, NI[:, n8], wide(tFI), ALU.mult))
            W(v.tensor_tensor(GR_, GR_, tm, ALU.subtract))
            W(v.tensor_tensor(tm, NI[:, n8], wide(tFR), ALU.mult))
            W(v.tensor_tensor(GI_, GI_, tm, ALU.add))
            mt, mb, nmt, nmb = (cst[:, k:k + 1] for k in (6, 7, 73, 74))

            def halves(dst, a, a_scale, b, b_scale):
                W(v.tensor_scalar(dst, a, a_scale, None, ALU.mult))
                W(v.scalar_tensor_tensor(dst, b, b_scale, dst, ALU.mult, ALU.add))

            f, b = slice(0, GROUPS), slice(GROUPS, Q)
            for d, q, step in ((X1, f, 1), (X1, b, -1)):
                halves(X1[:, :, q], NR[:, ::step, q], mt, NI[:, ::step, q], nmb)
                halves(X2[:, :, q], NI[:, ::step, q], nmt, NR[:, ::step, q], nmb)
                halves(Y1[:, :, q], GR_[:, ::-step, q], mt, GI_[:, ::-step, q], mb)
                halves(Y2[:, :, q], GI_[:, ::-step, q], nmt, GR_[:, ::-step, q], mb)
            halves(F1, tFR, mt, tFI, mb)
            halves(F2, tFI, nmt, tFR, mb)
            v.sem_inc(S("s_tab_ready"), 1)

            def scaled_sum(dst, tmp, a0, a1, b0, b1):
                v.tensor_tensor(dst, a0, a1, ALU.mult)
                W(v.tensor_tensor(tmp, b0, b1, ALU.mult))
                return v.tensor_tensor(dst, dst, tmp, ALU.add)

            ada1_dve(v, W, 2)
            for n in range(Q // QB):
                v.wait_ge(S(f"s_b_in{n % 2}"), B(f"s_b_in{n % 2}") + 16 * (n // 2 + 1))
                if n == 1:
                    v.wait_ge(S("s_u_tp"), B("s_u_tp") + GROUPS // 4)
                if n >= 2:
                    v.wait_ge(S("s_w_tp"), B("s_w_tp") + 2 * n - 2)
                q = slice(n * QB, (n + 1) * QB)
                shape = (P, QB, L, GI)
                w4 = WW[n % 2].rearrange("p (q s i) -> p q s i", q=QB, s=L)
                t4 = TMP[:, 0:1024].rearrange("p (q s i) -> p q s i", q=QB, s=L)
                y1, y2 = (y[:, :, q].rearrange("p s q -> p q s").unsqueeze(3).to_broadcast(shape) for y in (Y1, Y2))
                br, bi = (BB[n % 2][:, c].unsqueeze(2).to_broadcast(shape) for c in range(2))
                scaled_sum(w4, t4, br, y1, bi, y2).then_inc(S("s_w_ready"), 1)
                v.wait_ge(S("s_w_ready"), B("s_w_ready") + n + 1)
            v.tensor_copy(PWR[:, 0, :], NR[:, L, :])
            W(v.tensor_copy(PWI[:, 0, :], NI[:, L, :]))
            k = 1
            while k < BL:
                new, old = slice(k, 2 * k), slice(0, k)
                t1, t2 = (TMP[:, a:a + k * Q].rearrange("p (k q) -> p k q", q=Q) for a in (0, 512))
                top = [x[:, k - 1:k, :].to_broadcast((P, k, Q)) for x in (PWR, PWI)]
                cmul(PWR[:, new], PWI[:, new], PWR[:, old], PWI[:, old], top[0], top[1], t1, t2)
                k *= 2
            W(v.tensor_scalar(PWI, PWI, cst[:, 75:76], None, ALU.mult))
            v.sem_inc(S("s_pw_ready"), 1)
            v.wait_ge(S("s_v_ready"), B("s_v_ready") + Q // 4)
            scan(v, W, 0, TMP, TEMP[:, 1024:1792], True, range(BL - 1))
            v.sem_inc(S("s_fwd_done"), 1)
            v.wait_ge(S("s_d_in"), B("s_d_in") + 16)
            W(v.tensor_tensor(HC[0:LC], HC[0:LC], DROW[0:LC].unsqueeze(1).to_broadcast((LC, L, D)), ALU.mult))
            v.sem_inc(S("s_hd"), 1)
            v.wait_ge(S("s_chain_done"), B("s_chain_done") + 1)
            scan(v, W, 1, TMP, TEMP[:, 1024:1792], False, range(3, BL - 1))
            v.sem_inc(S("s_bwd_done"), 1)

            def y_add(n):
                v.wait_ge(S("s_y_mm"), B("s_y_mm") + n + 1)
                for k in range(2):
                    c = slice((n * QB + 4 * k) * GI, (n * QB + 4 * k + 4) * GI)
                    y = HC[0:LC, :, c].rearrange("p t (g i) -> p g t i", g=4)
                    ins = v.tensor_tensor(y, PS[0:LC, 4 + 2 * (n % 2) + k, :].rearrange("p (g t i) -> p g t i", g=4, t=L), y, ALU.add)
                ins.then_inc(S("s_y_ready"), 1)

            v.wait_ge(S("s_bwd_done"), B("s_bwd_done") + 2)
            for n in range(GROUPS // QB + 2):
                if n < GROUPS // QB:
                    k = n % 2
                    v.wait_ge(S(f"s_c_in{k}"), B(f"s_c_in{k}") + 64 * (n // 2 + 1))
                    if n >= 2:
                        v.wait_ge(S("s_st_mm"), B("s_st_mm") + n - 1)
                    for d in range(2):
                        q = slice(d * GROUPS + n * QB, d * GROUPS + (n + 1) * QB)
                        shape = (P, QB, L + 1, GI)
                        t4 = TMP.rearrange("p (q s i) -> p q s i", q=QB, s=L + 1)
                        x1, x2 = (x[:, :, q].rearrange("p s q -> p q s").unsqueeze(3).to_broadcast(shape) for x in (X1, X2))
                        cr, ci = (CB[k][:, d, c].unsqueeze(2).to_broadcast(shape) for c in range(2))
                        W(scaled_sum(CC[k][:, d], t4, cr, x1, ci, x2))
                        shape = (P, QB, GI)
                        f1, f2 = (x[:, q].unsqueeze(2).to_broadcast(shape) for x in (F1, F2))
                        W(scaled_sum(BB2[k][:, d], TMP[:, 0:QB * GI].rearrange("p (q i) -> p q i", q=QB), BD[k][:, d, 0], f1, BD[k][:, d, 1], f2))
                    v.sem_inc(S("s_cc_ready"), 1)
                if n >= 2:
                    y_add(n - 2)
            for t in range(L):
                v.wait_ge(S("s_yt_tp"), B("s_yt_tp") + t + 1)
                v.tensor_copy(YT[:, :, t * LC:(t + 1) * LC], PS[:, t % 4, :].rearrange("p (j c) -> p j c", j=DC)).then_inc(S("s_yt"), 1)
            v.wait_ge(S("s_bg_in"), B("s_bg_in") + 16)
            for n in range(2 * LT + 1):
                if n < 2 * LT:
                    h, b = n // LT, 4 + 2 * (n % 2)
                    v.wait_ge(S("s_glu_mm"), B("s_glu_mm") + n + 1)
                    if n >= 2:
                        v.wait_ge(S("s_oo"), B("s_oo") + n - 1)
                    v.tensor_tensor(ZT[n % 2][:, 0:512], PS[:, b, :], BG[:, h * 512:(h + 1) * 512], ALU.add)
                    v.tensor_tensor(ZT[n % 2][:, 512:1024], PS[:, b + 1, :], BG[:, D + h * 512:D + (h + 1) * 512], ALU.add).then_inc(S("s_z"), 1)
                if n:
                    a = n - 1
                    h, m = a // LT, a % LT
                    v.wait_ge(S("s_sig"), B("s_sig") + n)
                    v.tensor_tensor(OO[:, m, h * 512:(h + 1) * 512], ZT[a % 2][:, 0:512], ZT[a % 2][:, 512:1024], ALU.mult).then_inc(S("s_oo"), 1)
            v.wait_ge(S("s_rowg"), B("s_rowg") + 16)
            v.wait_ge(S("s_xr_in"), B("s_xr_in") + 16 * L)
            for m in range(LT):
                v.wait_ge(S("s_osd"), B("s_osd") + m + 1)
                W(v.reciprocal(rs[:, 8 + m:9 + m], sd[:, 8 + m:9 + m]))
                W(v.scalar_tensor_tensor(OO[:, m, :], OO[:, m, :], rs[:, 8 + m:9 + m], row(0), ALU.mult, ALU.mult))
                v.tensor_tensor(X[:, m, :], X[:, m, :], OO[:, m, :], ALU.add).then_inc(S("x3_ready"), 1)

        @block.vector
        def _(v):
            W = Steps(v, S("dve_step"))
            v.wait_ge(S("const_in"), 5 * 16)
            v.wait_ge(S("tri_in"), 32)
            v.tensor_copy(tri[:, :], work(0, P))
            v.tensor_copy(iota_b[:, :], work(P, P))
            v.memset(ones_b[:, :], 1.0)
            W(v.memset(eps[:, :], EPS))
            v.sem_inc(S("eps_ready"), 1)
            v.wait_ge(S("modb_in"), 32)
            for n in range(ADA_T):
                v.wait_ge(S("ada_mm"), n + 1)
                c = slice(n * 512, (n + 1) * 512)
                v.tensor_tensor(MOD[:, c], PS[0:2, n % 4, :], MODB[:, c], ALU.add).then_inc(S("ada_ev"), 1)
                if n % 2 == 0 or n == 1:
                    continue
                q = n // 2
                c = slice(q * D, (q + 1) * D)
                v.wait_ge(S("ada_ev"), n + 1)
                if q in (1, 4):
                    k = 0 if q == 1 else 2
                    W(v.scalar_tensor_tensor(MOD[:, c], MOD[:, c], 1.0, NG[:, k * D:(k + 1) * D], ALU.add, ALU.mult))
                if q in (2, 5):
                    k = 1 if q == 2 else 3
                    W(v.tensor_tensor(MOD[:, c], MOD[:, c], NG[:, k * D:(k + 1) * D], ALU.mult))
                if q in (1, 5):
                    v.sem_inc(S("mod_ready"), 1)
            v.wait_ge(S("a_sd"), 1)
            W(v.reciprocal(rs[:, 0:AT], sd[:, 0:AT]))
            v.wait_ge(S("rows_a"), 64)

            def modulated(n, t, lat_ctx, free, ready):
                k = 2 * lat_ctx
                if n >= 2:
                    free(n)
                W(v.scalar_tensor_tensor(H[n % 2], X[:, t, :], rs[:, n:n + 1], row(k), ALU.mult, ALU.mult))
                v.tensor_tensor(H[n % 2], H[n % 2], row(k + 1), ALU.add).then_inc(ready, 1)

            for t in range(AT + 2):
                if t < AT:
                    modulated(t, t, stream[t], lambda n: v.wait_ge(S("a_tp"), n - 1), S("a_h_ready"))
                if t >= 2:
                    a = t - 2
                    ps = bank2(4 + 2 * (a % 2))
                    v.wait_ge(S("c_sd"), a + 1)
                    W(v.reciprocal(rs[:, 6:8], sd[:, 6:8]))
                    if a:
                        v.wait_ge(S("ct_tp"), a)
                    v.tensor_scalar(CA[:, 0:QL], ps[:, 0:QL], rs[:, 6:7], None, ALU.mult)
                    v.tensor_scalar(CA[:, QL:QL + KVL], ps[:, QL:QL + KVL], rs[:, 7:8], None, ALU.mult)
                    v.tensor_copy(CA[:, QL + KVL:AW], ps[:, QL + KVL:AW]).then_inc(S("ca_ready"), 1)
                    v.wait_ge(S("ct_tp"), a + 1)
                    c = slice(a * P, (a + 1) * P)
                    ct = bank2(2)
                    for j in range(QC):
                        v.tensor_scalar(CQT[:, j, c], ct[:, j * P:(j + 1) * P], gcol[:, j:j + 1], None, ALU.mult)
                    for j in range(KC):
                        v.tensor_scalar(CKT[:, j, c], ct[:, (QC + j) * P:(QC + j + 1) * P], gcol[:, QC + j:QC + j + 1], None, ALU.mult)
                    v.tensor_copy(KPT[:, c], ct[0:ROPE, (QC + KC) * P:(QC + KC + 1) * P]).then_inc(S("ct_ready"), 1)
            for n in range(1, 2 * AT, 2):
                v.wait_ge(S("v_mm"), n + 1)
                v.tensor_copy(V[:, n // 2, 512:1024], PS[:, 4 + n % 4, :]).then_inc(S("v_ready_v"), 1)

            def rope(dst, src, ps, done):
                v.tensor_tensor(dst, src, cosT, ALU.mult)
                W(v.tensor_tensor(ps, ps, sinT, ALU.mult))
                v.tensor_tensor(dst, dst, ps, ALU.add).then_inc(done, 1)

            v.wait_ge(S("rope_in"), 32)
            v.wait_ge(S("k_rot"), 1)
            rope(KPR, KPT, bank2(6, N_ALL)[0:ROPE], S("k_rope"))
            for h in range(HEADS):
                v.wait_ge(S("kn_mm"), h + 1)
                v.tensor_copy(knT, bank2(2, N_ALL)).then_inc(S("kn_ready"), 1)
                v.wait_ge(S("q_rot"), h + 1)
                if h:
                    v.wait_ge(S("s_mm"), h * AT)
                rope(qpR, qpT, bank2(6, N_ALL)[0:ROPE], S("q_rope"))
                for t in range(AT + 1):
                    if t:
                        k = h * AT + t - 1
                        c = (t - 1) % 2
                        nk = N_ALL if t - 1 < LT else N_CTX
                        v.wait_ge(S("p_exp"), k + 1)
                        W(v.reciprocal(sm[:, 2 + c:3 + c], sm[:, c:c + 1]))
                        v.tensor_scalar(PR[c][:, 0:nk], PR[c][:, 0:nk], sm[:, 2 + c:3 + c], None, ALU.mult).then_inc(S("p_ready"), 1)
                    if t < AT:
                        k = h * AT + t
                        nk = N_ALL if t < LT else N_CTX
                        v.wait_ge(S("s_mm"), k + 1)
                        if k >= 2:
                            v.wait_ge(S("p_exp"), k - 1)
                        W(v.reduce_max(mx[:, t % 2:t % 2 + 1], bank2(2 * (t % 2), nk), AX_X))
                        v.tensor_scalar(mx[:, t % 2:t % 2 + 1], mx[:, t % 2:t % 2 + 1], -SCALE, None, ALU.mult).then_inc(S("nmax"), 1)
            v.wait_ge(S("rows_g"), 32)
            for t in range(AT + 1):
                if t < AT:
                    v.wait_ge(S("o_sd"), t + 1)
                    W(v.reciprocal(rs[:, 8 + t:9 + t], sd[:, 8 + t:9 + t]))
                    if t:
                        v.wait_ge(S("x1_ready"), t)
                    W(v.scalar_tensor_tensor(RT, bank2(2 * (t % 2)), rs[:, 8 + t:9 + t], RG[stream[t]], ALU.mult, ALU.mult))
                    v.sem_inc(S("o_used"), 1)
                    v.tensor_tensor(X[:, t, :], X[:, t, :], RT, ALU.add).then_inc(S("x1_ready"), 1)
                if t:
                    if t == 1:
                        v.wait_ge(S("rows_m"), 64)
                    input_dve(v, W, modulated, 0, t - 1)
            moe_dve(v, W, modulated, 0)
            s5_dve(v, W, modulated)
            moe_dve(v, W, modulated, 1)

        def moe_pool(pool, l):
            NT = len(TILES[l])
            g, Z = "m_", before_moe(l)

            def gather(dst, u, done):
                pool.sem_inc(S("pool_starts"), 1)
                pool.indirect_dma_start(out=dst, out_offset=None, in_=f_d[l][:, :],
                                        in_offset=bass.IndirectOffsetOnAxis(ap=idxg[:, u:u + 1], axis=0)).then_inc(done, 16)

            def scatter(src, u, done):
                pool.sem_inc(S("pool_starts"), 1)
                pool.indirect_dma_start(out=acc_d[l][:, :], out_offset=bass.IndirectOffsetOnAxis(ap=idxs[:, u:u + 1], axis=0),
                                        in_=src, in_offset=None, compute_op=ALU.add).then_inc(done, 16)

            for n in range(NT):
                pool.wait_ge(S(g + "sh_silu"), Z("sh_silu") + n + 1)
                if n >= 2:
                    pool.wait_ge(S(g + "sh_tp"), Z("sh_tp") + n - 1)
                pool.tensor_tensor(HH[n % 2], SG[n % 2], UP[n % 2], ALU.mult).then_inc(S(g + "sh_h"), 1)
            for k in range(2):
                pool.wait_ge(S(g + f"f_out{k}"), Z(f"f_out{k}") + NT // 2 * 16)
            pool.wait_ge(S(g + "f_trash"), Z("f_trash") + 16)
            pool.wait_ge(S(g + "sh_down"), Z("sh_down") + NT)
            for b in range(2):
                pool.dma_start(spare[:, b:b + 1], cst[:, 0:1]).then_inc(S(f"scat{b}_{l}"), 16)
            for b in range(2):
                pool.wait_ge(S(f"idx_ready{l}"), b + 1)
                gather(XG[b], b, S(f"xg_in{b}_{l}"))
            for k in range(2):
                pool.wait_ge(S(g + f"acc_out{k}"), Z(f"acc_out{k}") + NT // 2 * 16)
            pool.wait_ge(S(g + "acc_out2"), Z("acc_out2") + 16)
            pairs, most = pairs_of(pool, l)

            def add(u, outputs):
                pool.wait_ge(S(f"out_a{l}"), outputs)
                pool.wait_ge(S(f"out_v{l}"), outputs)
                scatter(OS[u], u, S(f"scat{u}_{l}"))
                pool.sem_inc(S(f"added{l}"), 1)

            def pair(i, first):
                for u in range(2):
                    b = i * 2 + u
                    pool.wait_ge(S(f"scat{u}_{l}"), i * 16 + 16)
                    pool.sem_inc(S(f"os_free{l}"), 1)
                    pool.wait_ge(S(f"idx_ready{l}"), b + 3)
                    pool.wait_ge(S(f"xt_tp{l}"), b + 1)
                    gather(XG[u], u, S(f"xg_in{u}_{l}"))
                    if not (first and u == 0):
                        add(1 - u, b + 1)

            pair(0, True)
            with pool.Fori(0, -(-most // TURNS)) as q:
                with pool.If(pairs - q * TURNS > 1):
                    with pool.Fori(1, TURNS + 1) as r:
                        i = q * TURNS + r
                        with pool.If(pairs - i > 0):
                            pair(i, False)
            pool.wait_ge(S(f"scat0_{l}"), pool.snap(pairs * 16 + 16, min_val=16, max_val=most * 16 + 16))
            add(1, pool.snap(pairs * 2 + 1, min_val=1, max_val=2 * most + 1))
            done = pool.snap(pairs * 16 + 16, min_val=16, max_val=most * 16 + 16)
            for k in range(2):
                pool.wait_ge(S(f"scat{k}_{l}"), done)
                pool.wait_ge(S(f"xg_in{k}_{l}"), done)
                pool.sem_inc(S("pool_starts"), 1)
            pool.sem_inc(S(g + "all_scattered"), 1)


        def ada1_pool(pool):
            w = I["ada_w"][1].rearrange("(p j) n -> p j n", j=DC)

            def bias_and_gains(r):
                gains = slice(r * D, (r + 1) * D) if r < 2 else slice(2 * D, 4 * D)
                pool.dma_start(MODB1, I["ada_b"][1:2, 2 * r * D:2 * (r + 1) * D].to_broadcast((2, 2 * D))).then_inc(S("a1_bias"), 16)
                pool.dma_start(NG1[:, 0:gains.stop - gains.start], I["norm_g"][1:2, gains].to_broadcast((2, gains.stop - gains.start)))\
                    .then_inc(S("a1_bias"), 16)

            def store(r):
                pool.wait_ge(S("a1_ready"), r + 1)
                pool.dma_start(mod_d[1][:, 2 * r * D:2 * (r + 1) * D], MOD1).then_inc(S("a1_out"), 16)

            for n in range(ADA_T):
                if n >= 3:
                    pool.wait_ge(S("a1_mm"), n - 2)
                pool.dma_start(ada1_slot(n), w[:, :, n * 512:(n + 1) * 512]).then_inc(S(f"a1_in{n % 3}"), 16)
                if n == 1:
                    bias_and_gains(0)
                if n in (6, 10):
                    store(n // 4 - 1)
                    bias_and_gains(n // 4)
            store(2)

        def s5_pool(pool):
            G = Steps(pool, S("pool_step"))
            pool.wait_ge(S("s_pw_ready"), B("s_pw_ready") + 1)
            pool.wait_ge(S("s_v_ready"), B("s_v_ready") + Q // 4)
            scan(pool, G, 1, TEMP[:, 1792:2560], TEMP[:, 2560:3328], True, ())
            pool.sem_inc(S("s_chain_done"), 1)
            scan(pool, G, 1, TEMP[:, 1792:2560], TEMP[:, 2560:3328], False, range(3))
            pool.sem_inc(S("s_bwd_done"), 1)

        @block.gpsimd
        def _(pool):
            moe_pool(pool, 0)
            ada1_pool(pool)
            s5_pool(pool)
            moe_pool(pool, 1)


def constants():
    k = np.arange(P)
    cst = np.zeros((P, 80), np.float32)
    cst[:, 0] = k
    cst[:, 2], cst[:, 3] = N_ALL + k, N_LAT + k
    cst[:, 4], cst[:, 5] = -(N_ALL + k), -(N_LAT + k)
    cst[:, 6], cst[:, 7] = k < ST, k >= ST
    cst[:, 8:72] = 8.0 ** (np.arange(N_EXP) % NSLOT)
    cst[:, 72] = 1.0
    cst[:, 73], cst[:, 74] = -cst[:, 6], -cst[:, 7]
    cst[:, 75] = cst[:, 6] - cst[:, 7]
    rot = np.zeros((ROPE, ROPE), np.float32)
    for i in range(ROPE // 2):
        rot[2 * i + 1, 2 * i], rot[2 * i, 2 * i + 1] = -1, 1
    t = np.arange(N_LAT)
    inv = (10000.0 ** (-np.arange(16, dtype=np.float32) / 16)).astype(np.float32)
    ang = np.concatenate([(t // 64).astype(np.float32)[:, None] * inv, (t % 64).astype(np.float32)[:, None] * inv], -1)
    cos = np.concatenate([np.ones((N_CTX, ROPE // 2), np.float32), np.cos(ang)])
    sin = np.concatenate([np.zeros((N_CTX, ROPE // 2), np.float32), np.sin(ang)])
    return dict(ident=np.eye(P, dtype=np.float32), tri=(k[:, None] < k[None, :]).astype(np.float32),
                iota=np.broadcast_to(k.astype(np.float32), (P, P)), cst=cst, rot=rot,
                cosT=np.repeat(cos, 2, 1).T, sinT=np.repeat(sin, 2, 1).T)


def laid_out(a):
    def by_state(x):
        return np.concatenate([x, x], 0)

    r = constants()
    r.update(x=a["x"][0], ctx=a["ctx"][0], cs=np.stack([a["c"][0], a["c_ctx"]], -1).reshape(P, DC, 2),
             ada_w=a["ada_w"], ada_b=a["ada_b"], norm_g=a["norm_g"].reshape(2, 4 * D),
             gcol=np.concatenate([a["mla_g_q"][0].reshape(P, QC), a["mla_g_kv"][0].reshape(P, KC)], 1),
             w_dqkv=a["mla_w_dqkv"][0], w_uq=a["mla_w_uq"][0], w_ukv=a["mla_w_ukv"][0], w_o=a["mla_w_o"][0],
             w_router=a["moe_w_router"], moe_bias=a["moe_bias"], w_gate=a["moe_w_gate"], w_up=a["moe_w_up"],
             w_down=a["moe_w_down"], sh_gate=a["sh_w_gate"], sh_up=a["sh_w_up"], sh_down=a["sh_w_down"],
             s5_d=a["s5_d"], w_glu=a["s5_w_glu"][0], b_glu=a["s5_b_glu"])
    lam_re, lam_im = (a[k][0].transpose(2, 0, 1).reshape(ST, Q) for k in ("s5_lam_re", "s5_lam_im"))
    log_step = np.broadcast_to(a["s5_log_step"][0].reshape(1, Q), (ST, Q))
    r["s5_par"] = by_state(np.concatenate([lam_re, lam_im, log_step], 1))
    r["s5_b"] = by_state(np.stack([a[k][0].transpose(2, 0, 1, 3).reshape(ST, Q, GI) for k in ("s5_b_re", "s5_b_im")], 1))
    r["s5_c"] = by_state(np.stack([a[k][0].transpose(3, 0, 1, 2).reshape(ST, Q, GI) for k in ("s5_c_re", "s5_c_im")], 1))
    return {k: np.ascontiguousarray(v) for k, v in r.items()}


def kernel(**inputs):
    import concourse.bacc as _bacc
    from concourse.bass_utils import run_bass_kernel_spmd as _run

    nc = _bacc.Bacc("TRN2", target_bir_lowering=False, num_devices=1)
    arrays = laid_out({k: np.asarray(v) for k, v in inputs.items()})
    I = {k: nc.dram_tensor(k, v.shape, F32, kind="ExternalInput").ap() for k, v in arrays.items()}
    O = {"out": nc.dram_tensor("out", (N_LAT, D), F32, kind="ExternalOutput").ap()}
    build(nc, I, O)
    r = _run(nc, [arrays], core_ids=[0])
    return np.asarray(r.results[0]["out"]).reshape(1, N_LAT, D)
```
